# Optimizing a Trainium2 kernel written in Bass

```python
import math
import jax
import jax.numpy as jnp
from jax import lax

D_MODEL = 1024
BATCH = 1
SEQ = 256
DEPTH = 2
DEC_BATCH = 1
DEC_SEQ = 1024
PAST_LEN = 512

GRID_W = 64
DN_DK = 128
DN_DV = 128
DN_HEADS = (D_MODEL // 2) // DN_DV
DN_WIDTH = DN_HEADS * DN_DV
DN_CHUNK = 64
CONV_W = 3
SC_GROUPS = 4
SC_WIDTH = D_MODEL // 4
FO_GROUPS = 4
FO_GROUP_W = (D_MODEL // 4) // FO_GROUPS
FO_WIDTH = FO_GROUPS * FO_GROUP_W
D_MIX = DN_WIDTH + SC_WIDTH + FO_WIDTH
IN_SPLITS = (3 * DN_WIDTH, DN_WIDTH, DN_HEADS, DN_HEADS, DN_HEADS, DN_HEADS,
             SC_WIDTH, SC_WIDTH, SC_WIDTH, FO_WIDTH)
D_IN = sum(IN_SPLITS)
N_EXPERTS = 16
EC_CAPACITY = 2
D_EXPERT = 1024
N_MOD = 6
RMS_EPS = 1e-6
POS_BASE = 10000.0

kernel_name = 'hybrid_deltanet_conv_fourier_ec_diffusion_step'

def rms_norm(x, w):
    xf = x.astype(jnp.float32)
    y = xf * lax.rsqrt(jnp.mean(xf * xf, axis=-1, keepdims=True) + RMS_EPS)
    return (y * w.astype(jnp.float32)).astype(x.dtype)

def centred_conv(x, w):
    half = CONV_W // 2
    n = x.shape[1]
    xp = jnp.pad(x, ((0, 0), (half, half), (0, 0)))
    return sum(xp[:, j:j + n] * w[j] for j in range(CONV_W))

def l2_normalize(x):
    return x * lax.rsqrt(jnp.sum(x * x, axis=-1, keepdims=True) + 1e-6)

def chunk_gated_delta(q, k, v, g, beta, s0):
    b, h, n, dk = k.shape
    dv = v.shape[-1]
    nc = n // DN_CHUNK
    q = q * (dk ** -0.5)
    rs = lambda t: t.reshape((b, h, nc, DN_CHUNK) + t.shape[3:])
    q, k, v, g, beta = rs(q), rs(k), rs(v), rs(g), rs(beta)
    gc = jnp.cumsum(g, axis=-1)
    idx = jnp.arange(DN_CHUNK)
    causal = idx[:, None] >= idx[None, :]
    strict = idx[:, None] > idx[None, :]
    diff = gc[..., :, None] - gc[..., None, :]
    decay = jnp.where(causal, jnp.exp(jnp.where(causal, diff, 0.0)), 0.0)
    kb = k * beta[..., None]
    lmat = jnp.where(strict, jnp.einsum('bhcik,bhcjk->bhcij', kb, k) * decay, 0.0)
    amat = lmat + jnp.eye(DN_CHUNK, dtype=lmat.dtype)
    rhs = jnp.concatenate([v * beta[..., None], kb * jnp.exp(gc)[..., None]], axis=-1)
    sol = lax.linalg.triangular_solve(amat, rhs, left_side=True, lower=True, unit_diagonal=True)
    u, w = sol[..., :dv], sol[..., dv:]
    qk = jnp.einsum('bhcik,bhcjk->bhcij', q, k) * decay
    q_dec = q * jnp.exp(gc)[..., None]
    k_dec = k * jnp.exp(gc[..., -1:] - gc)[..., None]
    g_last = jnp.exp(gc[..., -1])

    def step(s, xs):
        u_c, w_c, qd_c, qk_c, kd_c, gl_c = xs
        v_new = u_c - jnp.einsum('bhik,bhkv->bhiv', w_c, s)
        o = jnp.einsum('bhik,bhkv->bhiv', qd_c, s) + jnp.einsum('bhij,bhjv->bhiv', qk_c, v_new)
        s = s * gl_c[..., None, None] + jnp.einsum('bhik,bhiv->bhkv', kd_c, v_new)
        return s, o

    xs = tuple(jnp.moveaxis(t, 2, 0) for t in (u, w, q_dec, qk, k_dec, g_last))
    s_fin, o = lax.scan(step, s0, xs)
    o = jnp.moveaxis(o, 0, 2).reshape(b, h, n, dv)
    return o, s_fin

def bidir_gated_deltanet(qkv, z, beta_raw, a_raw, conv_w, a_log, dt_bias, norm_w, s0):
    bsz, n, _ = qkv.shape
    f32 = jnp.float32
    qkv = jax.nn.silu(centred_conv(qkv, conv_w)).astype(f32)
    heads = lambda t: t.reshape(bsz, n, DN_HEADS, -1).transpose(0, 2, 1, 3)
    q, k, v = (heads(t) for t in jnp.split(qkv, 3, axis=-1))
    q, k = l2_normalize(q), l2_normalize(k)
    outs, finals = [], []
    for d in range(2):
        beta = jax.nn.sigmoid(beta_raw[d].astype(f32)).transpose(0, 2, 1)
        g = (-jnp.exp(a_log[d].astype(f32))
             * jax.nn.softplus(a_raw[d].astype(f32) + dt_bias[d].astype(f32))).transpose(0, 2, 1)
        seq = (q, k, v, g, beta)
        if d == 1:
            seq = tuple(jnp.flip(t, axis=2) for t in seq)
        o, s_fin = chunk_gated_delta(*seq, s0[:, d])
        if d == 1:
            o = jnp.flip(o, axis=2)
        outs.append(o)
        finals.append(s_fin)
    o = (outs[0] + outs[1]).transpose(0, 2, 1, 3)
    zf = z.astype(f32).reshape(bsz, n, DN_HEADS, DN_DV)
    o = (o * lax.rsqrt(jnp.mean(o * o, axis=-1, keepdims=True) + RMS_EPS)
         * norm_w.astype(f32) * jax.nn.silu(zf))
    return o.reshape(bsz, n, DN_WIDTH).astype(z.dtype), jnp.stack(finals, axis=1)

def short_gated_conv(b_gate, c_gate, u, conv_w):
    return b_gate * centred_conv(c_gate * u, conv_w)

def fourier_mix(u):
    bsz, n, _ = u.shape
    uf = u.astype(jnp.float32).reshape(bsz, n, FO_GROUPS, FO_GROUP_W)
    f = jnp.fft.fft2(uf, axes=(1, 3), norm='ortho').real
    return f.reshape(bsz, n, FO_WIDTH).astype(u.dtype)

def parallel_mixers(h, s0, w_in, dn_conv_w, dn_a_log, dn_dt_bias, dn_norm_w, sc_conv_w, w_out):
    offsets = []
    acc = 0
    for size in IN_SPLITS[:-1]:
        acc += size
        offsets.append(acc)
    qkv, z, bf, bb, af, ab, sb, sc, su, fu = jnp.split(h @ w_in, offsets, axis=-1)
    dn, s_fin = bidir_gated_deltanet(qkv, z, (bf, bb), (af, ab), dn_conv_w, dn_a_log,
                                     dn_dt_bias, dn_norm_w, s0)
    y = jnp.concatenate([dn, short_gated_conv(sb, sc, su, sc_conv_w), fourier_mix(fu)], axis=-1)
    return y @ w_out, s_fin

def expert_choice_ffn(h, w_router, w_gate, w_up, w_down):
    bsz, n, d = h.shape
    t = h.reshape(bsz * n, d)
    cap = max(1, EC_CAPACITY * t.shape[0] // N_EXPERTS)
    aff = jax.nn.softmax((t @ w_router).astype(jnp.float32), axis=-1)
    top_w, top_i = lax.top_k(aff.T, cap)
    xe = t[top_i]
    hid = jax.nn.silu(jnp.einsum('ecd,edf->ecf', xe, w_gate)) * jnp.einsum('ecd,edf->ecf', xe, w_up)
    ye = jnp.einsum('ecf,efd->ecd', hid, w_down) * top_w[..., None].astype(t.dtype)
    out = jnp.zeros_like(t).at[top_i.reshape(-1)].add(ye.reshape(-1, d))
    return out.reshape(bsz, n, d)

def trunk_layer(x, cond, s0, w_ada, b_ada, norm1_w, norm2_w, w_in, dn_conv_w, dn_a_log, dn_dt_bias,
                dn_norm_w, sc_conv_w, w_out, w_router, w_gate, w_up, w_down):
    mod = (jax.nn.silu(cond) @ w_ada + b_ada)[:, None, :]
    sh1, sc1, g1, sh2, sc2, g2 = jnp.split(mod, N_MOD, axis=-1)
    h = rms_norm(x, norm1_w) * (1 + sc1) + sh1
    mix, s_fin = parallel_mixers(h, s0, w_in, dn_conv_w, dn_a_log, dn_dt_bias, dn_norm_w, sc_conv_w, w_out)
    x = x + g1 * mix
    h = rms_norm(x, norm2_w) * (1 + sc2) + sh2
    x = x + g2 * expert_choice_ffn(h, w_router, w_gate, w_up, w_down)
    return x, s_fin

def grid_pos_embed(n, d, dtype):
    rows = n // GRID_W
    f32 = jnp.float32
    r = jnp.repeat(jnp.arange(rows, dtype=f32), GRID_W)
    col = jnp.tile(jnp.arange(GRID_W, dtype=f32), rows)
    quarter = d // 4
    omega = jnp.power(POS_BASE, -jnp.arange(quarter, dtype=f32) / quarter)
    ra = r[:, None] * omega
    ca = col[:, None] * omega
    return jnp.concatenate([jnp.sin(ra), jnp.cos(ra), jnp.sin(ca), jnp.cos(ca)], axis=-1).astype(dtype)

def setup_inputs(seed: int = 0) -> dict:
    key = jax.random.key(seed)
    ks = jax.random.split(key, 24)
    f32 = jnp.float32
    nrm = lambda k, shape, s: jax.random.normal(k, shape, f32) * s
    dt = jnp.exp(jax.random.uniform(ks[11], (DEPTH, 2, DN_HEADS), f32,
                                    minval=math.log(1e-3), maxval=math.log(1e-1)))
    return {
        'x_prompt': nrm(ks[0], (BATCH, SEQ, D_MODEL), 1.0),
        'x_sample': nrm(ks[1], (DEC_BATCH, DEC_SEQ, D_MODEL), 1.0),
        'state_delta': nrm(ks[2], (DEC_BATCH, DEPTH, 2, DN_HEADS, DN_DK, DN_DV), DN_DK ** -0.5),
        'c': nrm(ks[3], (DEC_BATCH, D_MODEL), 1.0),
        'c_ctx': nrm(ks[4], (D_MODEL,), 1.0),
        'w_ada': nrm(ks[5], (DEPTH, D_MODEL, N_MOD * D_MODEL), 0.5 * D_MODEL ** -0.5),
        'b_ada': nrm(ks[6], (DEPTH, N_MOD * D_MODEL), 0.02),
        'norm1_w': 1.0 + nrm(ks[7], (DEPTH, D_MODEL), 0.02),
        'norm2_w': 1.0 + nrm(ks[8], (DEPTH, D_MODEL), 0.02),
        'w_in': nrm(ks[9], (DEPTH, D_MODEL, D_IN), D_MODEL ** -0.5),
        'dn_conv_w': nrm(ks[10], (DEPTH, CONV_W, 3 * DN_WIDTH), CONV_W ** -0.5),
        'dn_a_log': jnp.log(jax.random.uniform(ks[12], (DEPTH, 2, DN_HEADS), f32, minval=1.0, maxval=16.0)),
        'dn_dt_bias': jnp.log(jnp.expm1(dt)),
        'dn_norm_w': 1.0 + nrm(ks[13], (DEPTH, DN_DV), 0.02),
        'sc_conv_w': nrm(ks[14], (DEPTH, CONV_W, SC_WIDTH), CONV_W ** -0.5),
        'w_out': nrm(ks[15], (DEPTH, D_MIX, D_MODEL), D_MIX ** -0.5),
        'w_router': nrm(ks[16], (DEPTH, D_MODEL, N_EXPERTS), D_MODEL ** -0.5),
        'w_gate': nrm(ks[17], (DEPTH, N_EXPERTS, D_MODEL, D_EXPERT), D_MODEL ** -0.5),
        'w_up': nrm(ks[18], (DEPTH, N_EXPERTS, D_MODEL, D_EXPERT), D_MODEL ** -0.5),
        'w_down': nrm(ks[19], (DEPTH, N_EXPERTS, D_EXPERT, D_MODEL), D_EXPERT ** -0.5),
        'final_norm_w': 1.0 + nrm(ks[20], (D_MODEL,), 0.02),
    }

def reference(x_prompt, x_sample, state_delta, c, c_ctx, w_ada, b_ada, norm1_w, norm2_w, w_in,
              dn_conv_w, dn_a_log, dn_dt_bias, dn_norm_w, sc_conv_w, w_out, w_router, w_gate, w_up,
              w_down, final_norm_w):
    def layer_weights(l):
        return (w_ada[l], b_ada[l], norm1_w[l], norm2_w[l], w_in[l], dn_conv_w[l], dn_a_log[l],
                dn_dt_bias[l], dn_norm_w[l], sc_conv_w[l], w_out[l], w_router[l], w_gate[l], w_up[l],
                w_down[l])

    s_zero = jnp.zeros((x_prompt.shape[0], 2, DN_HEADS, DN_DK, DN_DV), jnp.float32)
    xp = x_prompt
    ctx_states = []
    for l in range(DEPTH):
        xp, s_fin = trunk_layer(xp, c_ctx[None, :], s_zero, *layer_weights(l))
        ctx_states.append(s_fin.astype(x_prompt.dtype))
    y_prompt = rms_norm(xp, final_norm_w)
    new_state_delta = jnp.stack(ctx_states, axis=1)

    xs = x_sample + grid_pos_embed(x_sample.shape[1], x_sample.shape[2], x_sample.dtype)[None]
    for l in range(DEPTH):
        xs, _ = trunk_layer(xs, c, state_delta[:, l].astype(jnp.float32), *layer_weights(l))
    y_sample = rms_norm(xs, final_norm_w)
    return (y_prompt, y_sample, new_state_delta)


_drawn_inputs = setup_inputs


def setup_inputs(seed=0):
    import zlib

    import numpy as np

    out = dict(_drawn_inputs(seed))
    spreads = {}
    factors = {'state_delta': 5.7, 'norm2_w': 6.567, 'dn_norm_w': 8.0, 'final_norm_w': 2.945}
    for name, (base, spread) in spreads.items():
        noise = np.random.default_rng([zlib.crc32(name.encode()), seed]).standard_normal(out[name].shape)
        drawn = base * np.exp(spread * noise) if base else spread * noise
        out[name] = jnp.asarray(drawn.astype(out[name].dtype))
    for name, factor in factors.items():
        out[name] = (out[name] * factor).astype(out[name].dtype)
    return out
```

```python
from contextlib import ExitStack

import concourse.bass as bass
from concourse import mybir

F32 = mybir.dt.float32
BF16 = mybir.dt.bfloat16
U32 = mybir.dt.uint32
I32 = mybir.dt.int32
ALU = mybir.AluOpType
ACT = mybir.ActivationFunctionType
AX = mybir.AxisListType
ds = bass.ds

P = 128
D = 1024
KT = D // P
DEPTH = 2
LAT, CTX = 1024, 256
LT, CT = LAT // P, CTX // P
T = LT + CT
N = T * P
HEADS = 4
DNW = HEADS * P
SCW = FOW = 256
SC0 = 3 * DNW + DNW + 4 * HEADS
EXPERTS = 16
CAPL, CAPC = 2 * LAT // EXPERTS, 2 * CTX // EXPERTS
CAP = CAPL + CAPC
LEVELS = [1, 2, 4, 8, 16, 32, 64]
EPS = 1e-6
BANK = 512
R_ADA, R_N1, R_N2, R_DNC, R_SCC, R_DNN = 0, 48, 56, 64, 100, 106
ROWS = 107
SH1, SC1, G1, SH2, SC2, G2 = 0, 8, 16, 24, 32, 40
Q_G, Q_NB, Q_B, Q_GC, Q_EG, Q_NEG, Q_END, Q_GL = range(8)
SPANS = [(0, 512), (512, 1024), (1024, 1280)]
GROUPS = [(0, 4), (4, 8), (8, 10)]
SEGS = [(0, LAT), (LAT, N)]
NCONST = 128 * (4 + 2 * len(LEVELS) + 2 + 2) + 2


def trunk(nc, x_prompt, x_sample, state_delta, c, c_ctx, w_ada, b_ada, norm1_w, norm2_w, w_in, dn_conv_w,
          dn_a_log, dn_dt_bias, dn_norm_w, sc_conv_w, w_out, w_router, w_gate, w_up, w_down, final_norm_w,
          consts, dft_lat, dft_ctx, pos_row, pos_col, y_prompt, y_sample, new_state):
    xres = nc.dram_tensor("xres", (N, D), F32, kind="Internal").ap()
    xnorm = nc.dram_tensor("xnorm", (N, D), F32, kind="Internal").ap()

    with ExitStack() as ctx:
        def sb(name, shape, dt=F32):
            return ctx.enter_context(nc.sbuf_tensor(name, shape, dt))

        def sem(name):
            return ctx.enter_context(nc.semaphore(name))

        ring = sb("ring", [P, 6 * 4096])
        hT = ring[:, 0:KT * N].rearrange("p (k n) -> p k n", k=KT)
        yT = ring[:, KT * N:2 * KT * N]
        hw = ring[:, 2 * KT * N:].rearrange("p (j k c) -> p j k c", j=4, k=KT)
        area = sb("area", [P, 19200])
        kq = area[:, 0:2560].rearrange("p (c j n) -> p c j n", j=2, n=P)
        ktok = area[:, 2560:3840].rearrange("p (c n) -> p c n", n=P)
        vtok = area[:, 3840:5120].rearrange("p (c n) -> p c n", n=P)
        zT = area[:, 5120:6400]

        def pair(at):
            return area[:, at:at + 2560].rearrange("p (d c n) -> p d c n", d=2, n=P)

        U, DD, LL, PP, QK = (pair(at) for at in range(6400, 19200, 2560))
        spare = [area[:, at:at + N] for at in range(6400, 19200, N)]
        oo = area[:, 8960:10240].rearrange("p (c n) -> p c n", n=P)
        chain = sb("chain", [P, 4, 4, P])
        cst = sb("cst", [P, NCONST])
        ident, ones, triF, triB = (cst[:, P * i:P * i + P] for i in range(4))
        lower = [cst[:, P * (4 + i):P * (5 + i)].bitcast(I32) for i in range(7)]
        upper = [cst[:, P * (11 + i):P * (12 + i)].bitcast(I32) for i in range(7)]
        big = cst[:, P * 18:P * 20]
        chdft = cst[:, P * 20:P * 22]
        eps_col = cst[:, P * 22:P * 22 + 1]
        qscale_col = cst[:, P * 22 + 1:P * 22 + 2]
        identb = sb("identb", [P, P], BF16)
        bigb = sb("bigb", [P, 2, P], BF16)
        condT = sb("condT", [P, 2, KT])
        rows = sb("rows", [P, P])
        cols = sb("cols", [P, P])
        mod = sb("mod", [P, 48, 2])
        A1 = sb("A1", [P, KT, 2])
        A2 = sb("A2", [P, KT, 2])
        g1b = sb("g1b", [P, 2, D])
        w16 = sb("w16", [P, KT, 16])
        wr = sb("wr", [P, KT, EXPERTS])
        alog = sb("alog", [P, 2, 8])
        gs = sb("gs", [P, 8, 8, T])
        hs = sb("hs", [P, 8, 2, T])
        hcw = sb("hcw", [P, 16])
        small = sb("small", [P, 64])
        tw = sb("tw", [P, 2, 17])
        ix = sb("ix", [P, 2, 17], U32)
        cur = sb("cur", [P, 2, 2])
        curi = sb("curi", [P, 2, 2], U32)
        xt = [area[:, 1024 * i:1024 * i + 1024] for i in range(2)]
        xn = [area[:, 1024 * i:1024 * i + 1024] for i in (2, 3)]
        h2T = [area[:, 1024 * i:1024 * i + 1024].rearrange("p (k n) -> p k n", k=KT) for i in (4, 5)]
        ada = [area[:, at:at + 4096].rearrange("p (k c) -> p k c", k=KT) for at in (6400, 10496, 14592)]
        wo = ada
        affT = area[0:EXPERTS, 14592:14592 + N]
        work = area[0:EXPERTS, 14592 + N:14592 + 2 * N]
        tv = area[0:EXPERTS, 17152:17152 + CAP]
        ti = area[0:EXPERTS, 17312:17312 + CAP].bitcast(U32)
        tf = area[0:EXPERTS, 17472:17472 + CAP]
        xeL = [area[:, 1024 * i:1024 * i + 1024] for i in range(2)]
        xeC = [area[0:CAPC, 1024 * i:1024 * i + 1024] for i in (2, 3)]
        xeT = [area[:, 4096 + 1280 * i:5376 + 1280 * i].rearrange("p (k n) -> p k n", k=KT) for i in range(2)]
        hid = area[:, 6656:7936].rearrange("p (k n) -> p k n", k=KT)
        yeT = area[:, 7936:9216].rearrange("p (k n) -> p k n", k=KT)
        yeL = [area[:, 9216 + 1024 * i:10240 + 1024 * i] for i in range(2)]
        yeC = [area[0:CAPC, 11264 + 1024 * i:12288 + 1024 * i] for i in range(2)]
        sg = area[:, 13312:13632].rearrange("p (b n) -> p b n", b=2)

        ps = ctx.enter_context(nc.psum_tensor("ps", [P, 8 * BANK], F32))
        PAB = [ps[:, 0:N], ps[:, 3 * BANK:3 * BANK + N]]

        def chunks(ap):
            return ap.rearrange("p (c n) -> p c n", n=P)

        def spread(col, n):
            return col.unsqueeze(len(col.shape)).to_broadcast(list(col.shape) + [n])

        def over(mat, n):
            return mat.unsqueeze(1).to_broadcast([P, n, P])

        local = []

        def lsem(name):
            s = sem(name)
            local.append(s)
            return s

        loaded = [lsem(f"loaded{i}") for i in range(8)]
        stored = lsem("stored")
        act_step, dve_step, pool_step = lsem("act_step"), lsem("dve_step"), lsem("pool_step")
        mm_a, mm_b, mm_c, mm_d, mm_e = (lsem(f"mm_{x}") for x in "abcde")
        dv_a, dv_b, dv_c, dv_d, dv_e, dv_f = (lsem(f"dv_{x}") for x in "abcdef")
        ac_a, ac_b, ac_c, ac_d, ac_e = (lsem(f"ac_{x}") for x in "abcde")
        po_a, po_b = lsem("po_a"), lsem("po_b")
        hs_ready, hcw_ready, conv0, rn, dec, lsig, dv_g = (lsem(x) for x in (
            "hs_ready", "hcw_ready", "conv0", "rn", "dec", "lsig", "dv_g"))
        ks_ps, vprime, vnew_ps, vnew_sb, upd_ps, o_half, o_done = (lsem(x) for x in (
            "ks_ps", "vprime", "vnew_ps", "vnew_sb", "upd_ps", "o_half", "o_done"))
        st = [lsem(f"st{i}") for i in range(4)]
        arrive = sem("arrive")
        go = {x: sem(f"go_{x}") for x in ("pe", "act", "dve", "sp")}
        hw_landed, hw_free = sem("hw_landed"), sem("hw_free")
        ring_landed = [sem(f"ring_landed{i}") for i in range(6)]
        ring_free = [sem(f"ring_free{i}") for i in range(6)]
        epoch = []
        for b in range(2):
            e = {n: sem(f"{n}{b}") for n in ("gathered_lat", "gathered_ctx", "xe_ps", "xe_sb", "gu_ps", "gate_sb", "hid_sb", "dn_ps",
                                             "ye_ch", "ye_ps", "ye_sb", "moe_dve")}
            epoch.append(e)
        ep_arrive = [sem(f"ep_arrive{b}") for b in range(2)]
        ep_go = [{x: sem(f"ep_go_{x}{b}") for x in ("pe", "act", "dve")} for b in range(2)]
        scattered = [sem("scattered_lat"), sem("scattered_ctx")]

        SCAN, PREV, SEEN, last_of, visited, n = [], {}, {}, {}, {}, 0
        for stp in range(LT):
            live = []
            for x in range(4 if stp < CT else 2):
                cc = (stp, LT - 1 - stp, LT + stp, T - 1 - stp)[x]
                PREV[n], SEEN[n] = last_of.get(x), visited.get(cc)
                last_of[x] = visited[cc] = n
                live.append((n, x, cc))
                n += 1
            SCAN.append((stp, live))
        NSCAN = n

        def XA(x):
            return ps[:, 2 * x * BANK:2 * x * BANK + 2 * P]

        def XB(x):
            return ps[:, (2 * x + 1) * BANK:(2 * x + 1) * BANK + 3 * P]

        def YF(t):
            return area[:, 14080 + 2560 * t:16640 + 2560 * t].rearrange("p (c n) -> p c n", n=256)

        def table(i, half):
            base = [ring[:, 0:4096], ring[:, 4096:8192], area[:, 0:4096], ring[:, 20480:24576]][2 * i + half]
            return base.rearrange("p (k c) -> p k c", k=LT)

        def table_ctx(i):
            return ring[:, 8192 + 512 * i:8704 + 512 * i].rearrange("p (k c) -> p k c", k=CT)

        def nums(sems):
            n = sorted(s.num for s in sems)
            assert n == list(range(n[0], n[-1] + 1))
            return range(n[0], n[-1] + 1)

        def meet(eng, who):
            eng.drain().then_inc(arrive, 1)
            eng.wait_ge(go[who], 1)
            eng.sem_clear(go[who])

        def meet_pool(pool):
            pool.drain()
            pool.wait_ge(arrive, 4)
            pool.sem_clear(arrive)
            pool.sem_clear(nums(local))
            for g in go.values():
                pool.sem_inc(g, 1)

        class Steps:

            def __init__(self, eng, s):
                self.eng, self.s, self.n = eng, s, 0

            def reset(self):
                self.n = 0

            def __call__(self, ins):
                self.n += 1
                ins.then_inc(self.s, 1)
                self.eng.wait_ge(self.s, self.n)

        xres_t = xres.rearrange("(t p) d -> t p d", p=P)
        xnorm_t = xnorm.rearrange("(t p) d -> t p d", p=P)
        xs_t = x_sample[0].rearrange("(t p) d -> t p d", p=P)
        sd = state_delta[0].rearrange("l s h k v -> (l s h) k v")
        ns = new_state[0].rearrange("l s h k v -> (l s h) k v")
        wg = w_gate.rearrange("l e d f -> (l e) d f")
        wu = w_up.rearrange("l e d f -> (l e) d f")
        wd = w_down.rearrange("l e d f -> (l e) d f")
        yp_t = y_prompt[0].rearrange("(t p) d -> t p d", p=P)
        ys_t = y_sample[0].rearrange("(t p) d -> t p d", p=P)

        block = ctx.enter_context(nc.Block())

        @block.sync
        def _(sp):
            def load_ring(slot, e):
                w = (wg, wu, wg, wu, wd, wd)[slot]
                half = (0, 0, 1, 1, 0, 1)[slot]
                src = w[ds(e, 1), :, 512 * half:512 * half + 512].rearrange("a (k p) f -> p (a k) f", p=P)
                sp.dma_start(ring[:, 4096 * slot:4096 * slot + 4096].rearrange("p (k f) -> p k f", k=KT),
                             src).then_inc(ring_landed[slot], 16)

            def take(s):
                sp.wait_ge(s, 1)
                sp.sem_clear(s)

            sp.dma_start(cst[:], consts).then_inc(loaded[0], 16)
            sp.dma_start(rows[0:8, :], c[0].rearrange("(r p) -> r p", p=P)).then_inc(loaded[0], 16)
            sp.dma_start(rows[8:16, :], c_ctx.rearrange("(r p) -> r p", p=P)).then_inc(loaded[0], 16)
            sp.dma_start(xres[LAT:N, :], x_prompt[0]).then_inc(stored, 16)
            for half in range(2):
                sp.dma_start(area[64 * half:64 * half + 64, 7168:7680], pos_col).then_inc(loaded[1], 16)
            for t in range(LT):
                b = t % 2
                if t >= 2:
                    sp.wait_ge(st[b], 16 * (t // 2))
                sp.dma_start(xt[b], xs_t[t]).then_inc(loaded[2 + b], 16)
                for half in range(2):
                    r = 2 * t + half
                    sp.dma_start(area[64 * half:64 * half + 64, 6656 - 512 * b:7168 - 512 * b],
                                 pos_row[r:r + 1, :].to_broadcast([64, 512])).then_inc(loaded[2 + b], 16)
                sp.wait_ge(dv_a, 2 * (t + 1))
                sp.dma_start(xres_t[t], xt[b]).then_inc(st[b], 16)
            sp.wait_ge(stored, 16)
            for b in range(2):
                sp.wait_ge(st[b], 16 * LT // 2)
            meet(sp, "sp")

            with sp.Fori(0, DEPTH) as l:
                for r0, src in ((R_ADA, b_ada), (R_N1, norm1_w), (R_N2, norm2_w), (R_DNN, dn_norm_w)):
                    n = src.shape[1] // P
                    sp.dma_start(rows[r0:r0 + n, :], src[ds(l, 1), :].rearrange("a (r p) -> (a r) p", p=P)
                                 ).then_inc(loaded[0], 16)
                for r0, src in ((R_DNC, dn_conv_w), (R_SCC, sc_conv_w)):
                    n = src.shape[1] * src.shape[2] // P
                    sp.dma_start(rows[r0:r0 + n, :], src[ds(l, 1), :, :].rearrange("a j (r p) -> (a j r) p", p=P)
                                 ).then_inc(loaded[0], 16)
                for i, src in enumerate((dn_a_log, dn_dt_bias)):
                    sp.dma_start(alog[:, i, :], src[ds(l, 1), :, :].rearrange("a s h -> a (s h)")
                                 .to_broadcast([P, 8])).then_inc(loaded[0], 16)
                sp.dma_start(w16[:], w_in[ds(l, 1), :, 4 * DNW:4 * DNW + 16].rearrange("a (k p) c -> p (a k) c", p=P)
                             ).then_inc(loaded[1], 16)
                sp.dma_start(wr[:], w_router[ds(l, 1), :, :].rearrange("a (k p) c -> p (a k) c", p=P)
                             ).then_inc(loaded[1], 16)

                def load_ada(j):
                    if j >= 3:
                        sp.wait_ge(mm_a, j - 2)
                    sp.dma_start(ada[j % 3], w_ada[ds(l, 1), :, 512 * j:512 * j + 512].rearrange(
                        "a (k p) c -> p (a k) c", p=P)).then_inc(loaded[2 + j % 3], 16)

                for j in range(12):
                    load_ada(j)
                for t in range(T):
                    if t >= 2:
                        sp.wait_ge(dv_b, t - 1)
                        sp.wait_ge(ac_a, t - 1)
                    sp.dma_start(xt[t % 2], xres_t[t]).then_inc(loaded[5 + t % 2], 16)
                sp.wait_ge(loaded[1], 32)
                meet(sp, "sp")

                def load_heads(col):
                    for j in range(4):
                        sp.dma_start(hw[:, j], w_in[ds(l, 1), :, ds(col(j), P)].rearrange(
                            "a (k p) c -> p (a k) c", p=P)).then_inc(hw_landed, 16)

                load_heads(lambda j: j * DNW)
                meet(sp, "sp")

                def head(h, following):
                    for s in range(2):
                        sp.dma_start(chain[:, s, 0], sd[ds(l * 8 + h + 4 * s, 1)].rearrange("a k v -> (a k) v")
                                     ).then_inc(loaded[0], 16)
                    take(hw_free)
                    load_heads(following)
                    sp.wait_ge(dv_f, 4 * CT)
                    for s in range(2):
                        sp.dma_start(ns[ds(l * 8 + h + 4 * s, 1)].rearrange("a k v -> (a k) v"), chain[:, 2 + s, 0]
                                     ).then_inc(stored, 16)
                    sp.wait_ge(stored, 32)
                    meet(sp, "sp")

                def branch(t):
                    return lambda j: SC0 + (1, 2, 0, 3)[j] * SCW + t * P

                with sp.Fori(0, HEADS - 1) as h:
                    head(h, lambda j: h * P + (j * DNW + P))
                head(HEADS - 1, branch(0))

                take(hw_free)
                load_heads(branch(1))
                take(hw_free)
                for i in range(2):
                    for half in range(2):
                        if (i, half) == (0, 0):
                            sp.wait_ge(mm_a, 8)
                        sp.dma_start(table(i, half), dft_lat[i, :, 512 * half:512 * half + 512].rearrange(
                            "(k p) c -> p k c", p=P)).then_inc(loaded[0], 16)
                    sp.dma_start(table_ctx(i), dft_ctx[i].rearrange("(k p) c -> p k c", p=P)).then_inc(loaded[0], 16)
                sp.wait_ge(loaded[0], 16 * 6)
                meet(sp, "sp")

                for half in range(2):
                    sp.dma_start(wo[half], w_out[ds(l, 1), :, 512 * half:512 * half + 512].rearrange(
                        "a (k p) c -> p (a k) c", p=P)).then_inc(loaded[0], 16)

                for t in range(T + 1):
                    if t < T:
                        if t >= 2:
                            sp.wait_ge(st[t % 2], 16 * (t // 2))
                            sp.wait_ge(dv_b, t - 1)
                        sp.dma_start(xt[t % 2], xres_t[t]).then_inc(loaded[1 + t % 2], 16)
                    if t == 0:
                        for s in (0, 1, 5):
                            load_ring(s, l * EXPERTS)
                    if t >= 1:
                        sp.wait_ge(po_a, t)
                        sp.dma_start(xres_t[t - 1], xt[(t - 1) % 2]).then_inc(st[(t - 1) % 2], 16)
                        sp.wait_ge(dv_b, t)
                        sp.dma_start(xnorm_t[t - 1], xn[(t - 1) % 2]).then_inc(st[2 + (t - 1) % 2], 16)
                sp.wait_ge(mm_a, T)
                for s in (2, 3, 4):
                    load_ring(s, l * EXPERTS)
                for i in range(4):
                    sp.wait_ge(st[i], 16 * T // 2)
                meet(sp, "sp")

                with sp.Fori(1, EXPERTS) as e:
                    for s in range(6):
                        take(ring_free[s])
                        load_ring(s, l * EXPERTS + e)
                for s in range(6):
                    take(ring_free[s])
                meet(sp, "sp")

            sp.dma_start(g1b[:, 0, :], final_norm_w.rearrange("(a d) -> a d", a=1).to_broadcast([P, D])
                         ).then_inc(loaded[0], 16)
            for t in range(T + 1):
                if t < T:
                    if t >= 2:
                        sp.wait_ge(dv_b, t - 1)
                        sp.wait_ge(ac_a, t - 1)
                    sp.dma_start(xt[t % 2], xres_t[t]).then_inc(loaded[1 + t % 2], 16)
                if t >= 1:
                    sp.wait_ge(dv_b, t)
                    dst = ys_t[t - 1] if t - 1 < LT else yp_t[t - 1 - LT]
                    sp.dma_start(dst, xn[(t - 1) % 2]).then_inc(st[(t - 1) % 2], 16)
            for b in range(2):
                sp.wait_ge(st[b], 16 * T // 2)

        @block.tensor
        def _(pe):
            mm = nc.tensor.matmul

            def transposes(dst, src, n=P):
                return nc.tensor.transpose(dst, src, ident[0:src.shape[0], 0:src.shape[0]])

            pe.wait_ge(loaded[0], 48)
            transposes(ps[:, 0:16], rows[0:16, :]).then_inc(mm_a, 1)
            meet(pe, "pe")

            with pe.Fori(0, DEPTH) as l:
                pe.wait_ge(loaded[0], 16 * 8)
                transposes(ps[:, BANK:BANK + ROWS], rows[0:ROWS, :]).then_inc(mm_b, 1)
                for j in range(12):
                    pe.wait_ge(loaded[2 + j % 3], 16 * (j // 3 + 1))
                    for m in range(4):
                        col = 2 * (4 * j + m)
                        for k in range(KT):
                            last = mm(ps[:, col:col + 2], ada[j % 3][:, k, P * m:P * m + P], condT[:, :, k],
                                      start=(k == 0), stop=(k == KT - 1))
                    last.then_inc(mm_a, 1)
                for i in range(2):
                    pe.wait_ge(dv_c, i + 1)
                    for k in range(KT):
                        last = mm(ps[:, (2 + 2 * i) * BANK + P * k:(2 + 2 * i) * BANK + P * k + P], ones,
                                  spare[2 * i + 0][:, 0:1024].rearrange("p (k n) -> p k n", k=KT)[:, k],
                                  start=True, stop=True)
                    last.then_inc(mm_c, 1)
                for t in range(T):
                    pe.wait_ge(dv_b, t + 1)
                    if t == 0:
                        pe.wait_ge(ac_c, 2)
                    if t >= 2:
                        pe.wait_ge(dv_d, 4 * (t - 1))
                        pe.wait_ge(ac_b, 4 * (t - 1))
                    for k in range(KT):
                        at = (2 + 2 * (t % 2)) * BANK + P * k
                        last = transposes(ps[:, at:at + P], xn[t % 2][:, P * k:P * k + P])
                    last.then_inc(mm_d, 1)
                meet(pe, "pe")

                for t in range(T):
                    for k in range(KT):
                        last = mm(ps[:, 16 * t:16 * t + 16], hT[:, k, P * t:P * t + P], w16[:, k, :],
                                  start=(k == 0), stop=(k == KT - 1))
                last.then_inc(mm_a, 1)
                pe.wait_ge(dv_a, 1)
                mm(ps[:, BANK:BANK + 4 * T], triF, gs[:, Q_G, 0:4, :], start=True, stop=True)
                mm(ps[:, BANK + 4 * T:BANK + 8 * T], triB, gs[:, Q_G, 4:8, :], start=True, stop=True)
                mm(ps[:, 2 * BANK:2 * BANK + 8 * T], ones, gs[:, Q_G, :, :], start=True, stop=True).then_inc(mm_b, 1)
                meet(pe, "pe")

                def project(j, dst):
                    for k in range(KT):
                        for a, b in SPANS:
                            last = mm(dst[:, a:b], hw[:, j, k, :], hT[:, k, a:b], start=(k == 0), stop=(k == KT - 1))
                    return last

                with pe.Fori(0, HEADS) as h:
                    pe.wait_ge(hw_landed, 64)
                    pe.sem_clear(hw_landed)
                    for j in range(4):
                        if j >= 2:
                            pe.wait_ge(dv_a, j - 1)
                        last = project(j, PAB[j % 2])
                        last.then_inc(mm_a, 1)
                    for j in range(2):
                        if j == 0:
                            pe.wait_ge(mm_a, 4)
                            pe.sem_inc(hw_free, 1)
                        pe.wait_ge(ac_b, j + 1)
                        if j == 0:
                            pe.wait_ge(dv_a, 3)
                        else:
                            pe.wait_ge(ac_c, 1)
                        for a, b in SPANS:
                            last = mm(PAB[j][:, a:b], ones, spare[4 + j][:, a:b], start=True, stop=True)
                        last.then_inc(mm_b, 1)
                    pe.wait_ge(dv_b, 2)
                    pe.wait_ge(ac_d, 2)
                    for cc in range(T):
                        last = transposes(chunks(PAB[0])[:, cc], kq[:, cc, 0])
                    last.then_inc(mm_c, 1)
                    pe.wait_ge(ac_a, 3)
                    for cc in range(T):
                        last = transposes(chunks(PAB[1])[:, cc], chunks(spare[3])[:, cc])
                    last.then_inc(mm_c, 1)
                    for d in range(2):
                        if d == 0:
                            pe.wait_ge(ac_e, 1)
                        else:
                            pe.wait_ge(dv_c, 1)
                        pe.wait_ge(hs_ready, 1)
                        for cc in range(T):
                            mm(chunks(PAB[d])[:, cc], hs[:, Q_G, d, cc:cc + 1].to_broadcast([P, P]), (triF, triB)[d],
                               start=True, stop=False)
                            last = mm(chunks(PAB[d])[:, cc], identb[:], bigb[:, d], start=False, stop=True)
                        last.then_inc(mm_d, 1)
                    for g, (a, b) in enumerate(GROUPS):
                        pe.wait_ge(dv_d, (1, 2, 6)[g])
                        dst = (ps[:, 0:1024], ps[:, 3 * BANK:5 * BANK], ps[:, 0:1024])[g]
                        for cc in range(a, b):
                            last = mm(dst[:, 256 * (cc - a):256 * (cc - a) + 256], kq[:, cc, 0], kq[:, cc],
                                      start=True, stop=True)
                        last.then_inc(mm_e, 1)
                    pe.wait_ge(dv_d, 14)
                    for d in range(2):
                        for cc in range(T):
                            last = transposes(chunks(PAB[d])[:, cc], DD[:, d, cc])
                        last.then_inc(mm_e, 1)
                    for d in range(2):
                        pe.wait_ge(dv_e, d + 1)
                        for cc in range(T):
                            last = transposes(chunks(PAB[d])[:, cc], DD[:, d, cc])
                        last.then_inc(mm_e, 1)
                    for i, s in enumerate(LEVELS[1:]):
                        for d in range(2):
                            pe.wait_ge(ac_e, 2 + 4 * i + d)
                            for cc in range(T):
                                last = mm(chunks(PAB[d])[:, cc], LL[:, d, cc], U[:, d, cc], start=True, stop=True)
                            last.then_inc(mm_e, 1)
                        for d in range(2):
                            pe.wait_ge(ac_e, 4 + 4 * i + d)
                            for cc in range(T):
                                last = mm(chunks(PAB[d])[:, cc], DD[:, d, cc], PP[:, d, cc], start=True, stop=True)
                            last.then_inc(mm_e, 1)
                        if i < 5:
                            for d in range(2):
                                pe.wait_ge(dv_e, 2 + 2 * i + d + 1)
                                for cc in range(T):
                                    last = transposes(chunks(PAB[d])[:, cc], U[:, d, cc])
                                last.then_inc(mm_e, 1)
                    pe.wait_ge(po_b, 2)
                    pe.wait_ge(loaded[0], 32)
                    pe.wait_ge(dv_e, 14 + 1)
                    for step, live in SCAN:
                        for n, x, cc in live:
                            if step:
                                pe.wait_ge(dv_f, PREV[n] + 1)
                            mm(XA(x)[:, 0:P], kq[:, cc, 0], chain[:, x, 0], start=True, stop=True)
                            mm(XA(x)[:, P:2 * P], kq[:, cc, 1], chain[:, x, 0], start=True, stop=True
                               ).then_inc(ks_ps, 1)
                        for n, x, cc in live:
                            pe.wait_ge(vprime, n + 1)
                            if step:
                                pe.wait_ge(o_done, PREV[n] + 1)
                            mm(XB(x)[:, 2 * P:3 * P], U[:, x % 2, cc], chain[:, x, 1], start=True, stop=True
                               ).then_inc(vnew_ps, 1)
                        for n, x, cc in live:
                            pe.wait_ge(vnew_sb, 2 * n + 2)
                            mm(XB(x)[:, P:2 * P], ktok[:, cc], chain[:, x, 3], start=True, stop=True)
                            mm(XB(x)[:, 0:P], QK[:, x % 2, cc], chain[:, x, 2], start=True, stop=True
                               ).then_inc(upd_ps, 1)
                    pe.wait_ge(dv_c, 2)
                    for cc in range(T):
                        last = transposes(chunks(PAB[0])[:, cc], oo[:, cc])
                    last.then_inc(mm_c, 1)
                    meet(pe, "pe")

                for t in range(2):
                    pe.wait_ge(hw_landed, 64)
                    pe.sem_clear(hw_landed)
                    for j in range(4):
                        n = 4 * t + j
                        if n == 2:
                            pe.wait_ge(ac_a, 1)
                        if n == 3:
                            pe.wait_ge(dv_a, 1)
                        if n == 4:
                            pe.wait_ge(dv_a, 2)
                        if n == 5:
                            pe.wait_ge(ac_a, 2)
                        if n == 6:
                            pe.wait_ge(ac_a, 3)
                        if n == 7:
                            pe.wait_ge(dv_a, 3)
                        last = project(j, PAB[j % 2])
                        last.then_inc(mm_a, 1)
                    pe.wait_ge(mm_a, 4 * t + 4)
                    pe.sem_inc(hw_free, 1)
                pe.wait_ge(ac_a, 4)
                pe.wait_ge(dv_a, 4)
                for t in range(2):
                    for g, (a, b) in enumerate(GROUPS):
                        n = 3 * t + g
                        if n >= 2:
                            pe.wait_ge(ac_b, n - 1)
                        dst = ps[:, 2 * BANK * (n % 2):2 * BANK * (n % 2) + 2 * BANK]
                        for cc in range(a, b):
                            last = mm(dst[:, 256 * (cc - a):256 * (cc - a) + 256],
                                      spare[4 + t][:, P * cc:P * cc + P], chdft, start=True, stop=True)
                        last.then_inc(mm_b, 1)
                pe.wait_ge(loaded[0], 16 * 6)
                pe.wait_ge(ac_b, 6)
                n = 0
                for t in range(2):
                    Y = YF(t)
                    for half in range(3):
                        lo, hi = SPANS[half]
                        dst = ps[:, (4 + n % 2) * BANK:(4 + n % 2) * BANK + hi - lo]
                        if n >= 2:
                            pe.wait_ge(dv_b, n - 1)
                        tiles = range(LT) if half < 2 else range(LT, T)
                        for i in range(2):
                            tab = table(i, half) if half < 2 else table_ctx(i)
                            for m in tiles:
                                last = mm(dst, Y[:, m, P * i:P * i + P], tab[:, m - tiles[0], :],
                                          start=(i == 0 and m == tiles[0]), stop=(i == 1 and m == tiles[-1]))
                        last.then_inc(mm_c, 1)
                        n += 1
                meet(pe, "pe")

                yT3 = yT.rearrange("p (k n) -> p k n", k=KT)
                pe.wait_ge(loaded[0], 32)
                for t in range(T + 1):
                    if t < T:
                        if t >= 2:
                            pe.wait_ge(dv_a, t - 1)
                        for half in range(2):
                            for k in range(KT):
                                at = (2 * (t % 2) + half) * BANK
                                last = mm(ps[:, at:at + 512], yT3[:, k, P * t:P * t + P], wo[half][:, k, :],
                                          start=(k == 0), stop=(k == KT - 1))
                        last.then_inc(mm_a, 1)
                    if t >= 1:
                        u = t - 1
                        pe.wait_ge(dv_b, u + 1)
                        if u >= 1:
                            pe.wait_ge(dv_d, 4 * u)
                            pe.wait_ge(ac_b, 4 * u)
                        for k in range(KT):
                            last = transposes(ps[:, 4 * BANK + P * k:4 * BANK + P * k + P],
                                              xn[u % 2][:, P * k:P * k + P])
                        last.then_inc(mm_b, 1)
                        pe.wait_ge(dv_d, 4 * u + 4)
                        pe.wait_ge(ac_b, 4 * u + 4)
                        if u >= 1:
                            pe.wait_ge(dv_c, u)
                        for k in range(KT):
                            last = mm(ps[:, 6 * BANK:6 * BANK + EXPERTS], h2T[u % 2][:, k, :], wr[:, k, :],
                                      start=(k == 0), stop=(k == KT - 1))
                        last.then_inc(mm_c, 1)
                        pe.wait_ge(dv_c, u + 1)
                        if u >= 1:
                            pe.wait_ge(ac_d, u)
                        transposes(ps[0:EXPERTS, 7 * BANK:7 * BANK + P], small[:, 32:48]).then_inc(mm_d, 1)
                pe.wait_ge(dv_e, 1)
                for i, (src, lo, n) in enumerate(((tv, 0, CAPL), (tf, 0, CAPL), (tv, CAPL, CAPC), (tf, CAPL, CAPC))):
                    last = transposes(ps[0:n, 16 * i:16 * i + 16], src[:, lo:lo + n])
                last.then_inc(mm_e, 1)
                meet(pe, "pe")

                def gather_T(b):
                    E = epoch[b]
                    pe.wait_ge(E["gathered_lat"], 16)
                    pe.wait_ge(E["gathered_ctx"], 16)
                    for k in range(KT):
                        transposes(ps[:, P * k:P * k + P], xeL[b][:, P * k:P * k + P])
                    for k in range(KT):
                        last = transposes(ps[:, 2 * BANK + CAPC * k:2 * BANK + CAPC * k + CAPC],
                                          xeC[b][:, P * k:P * k + P])
                    last.then_inc(E["xe_ps"], 1)

                def slot(i):
                    return ring[:, 4096 * i:4096 * i + 4096].rearrange("p (k f) -> p k f", k=KT)

                def arrived(i):
                    pe.wait_ge(ring_landed[i], 16)
                    pe.sem_clear(ring_landed[i])

                gather_T(0)
                with pe.Fori(0, EXPERTS // 2):
                    for b in range(2):
                        E = epoch[b]
                        pe.wait_ge(E["xe_sb"], 10)
                        for m in range(KT):
                            half = m // 4
                            if m % 4 == 0:
                                arrived(2 * half)
                                arrived(2 * half + 1)
                            if m >= 2:
                                pe.wait_ge(E["hid_sb"], m - 1)
                            for i in range(2):
                                at = (4 + m % 2) * BANK + CAP * i
                                for k in range(KT):
                                    last = mm(ps[:, at:at + CAP], slot(2 * half + i)[:, k, P * (m % 4):P * (m % 4) + P],
                                              xeT[b][:, k, :], start=(k == 0), stop=(k == KT - 1))
                            last.then_inc(E["gu_ps"], 1)
                            if m % 4 == 3:
                                pe.wait_ge(E["gu_ps"], m + 1)
                                pe.sem_inc(ring_free[2 * half], 1)
                                pe.sem_inc(ring_free[2 * half + 1], 1)
                        pe.wait_ge(ep_go[1 - b]["pe"], 1)
                        pe.sem_clear(ep_go[1 - b]["pe"])
                        gather_T(1 - b)
                        pe.wait_ge(E["hid_sb"], KT)

                        def back(m):
                            pe.wait_ge(E["ye_ch"], 2 * m + 2)
                            if m == 0:
                                pe.wait_ge(epoch[1 - b]["xe_sb"], 10)
                            transposes(ps[:, P * m:P * m + P], yeT[:, m, 0:CAPL])
                            return transposes(ps[0:CAPC, 2 * BANK + P * m:2 * BANK + P * m + P], yeT[:, m, CAPL:CAP])

                        for m in range(KT):
                            half = m // 4
                            if m % 4 == 0:
                                arrived(4 + half)
                            if m >= 2:
                                pe.wait_ge(E["ye_ch"], 2 * (m - 1))
                            at = (6 + m % 2) * BANK
                            for k in range(KT):
                                last = mm(ps[:, at:at + CAP], slot(4 + half)[:, k, P * (m % 4):P * (m % 4) + P],
                                          hid[:, k, :], start=(k == 0), stop=(k == KT - 1))
                            last.then_inc(E["dn_ps"], 1)
                            if m % 4 == 3:
                                pe.wait_ge(E["dn_ps"], m + 1)
                                pe.sem_inc(ring_free[4 + half], 1)
                            if m >= 1:
                                back(m - 1)
                        back(KT - 1).then_inc(E["ye_ps"], 1)
                        pe.wait_ge(E["ye_sb"], 2)
                        pe.drain().then_inc(ep_arrive[b], 1)
                pe.wait_ge(ep_go[1]["pe"], 1)
                pe.sem_clear(ep_go[1]["pe"])
                meet(pe, "pe")

        @block.scalar
        def _(act):
            f = nc.scalar.activation
            step = Steps(act, act_step)

            act.wait_ge(mm_a, 1)
            f(condT[:], ps[:, 0:16].rearrange("p (s k) -> p s k", s=2), ACT.Silu)
            meet(act, "act")

            with act.Fori(0, DEPTH) as l:
                for i in range(2):
                    act.wait_ge(mm_c, i + 1)
                    f(g1b[:, i, :], ps[:, (2 + 2 * i) * BANK:(4 + 2 * i) * BANK], ACT.Copy).then_inc(ac_c, 1)
                for t in range(T + 1):
                    if t < T:
                        act.wait_ge(loaded[5 + t % 2], 16 * (t // 2 + 1))
                        if t >= 1:
                            act.wait_ge(ac_a, t)
                        f(h2T[0].rearrange("p k n -> p (k n)"), xt[t % 2], ACT.Square,
                          accum_out=small[:, t:t + 1]).then_inc(ac_a, 1)
                        act.wait_ge(dv_a, t + 1)
                        f(small[:, 10 + t:11 + t], small[:, 10 + t:11 + t], ACT.Sqrt).then_inc(ac_d, 1)
                    if t >= 1:
                        u, s = t - 1, int(t - 1 >= LT)
                        act.wait_ge(mm_d, u + 1)
                        for k in range(4):
                            at = (2 + 2 * (u % 2)) * BANK + P * k
                            f(hT[:, k, P * u:P * u + P], ps[:, at:at + P], ACT.Identity, scale=A1[:, k, s:s + 1],
                              bias=mod[:, SH1 + k, s:s + 1]).then_inc(ac_b, 1)
                meet(act, "act")

                gate = ps[:, 0:16 * T].rearrange("p (t j) -> p j t", j=16)
                act.wait_ge(mm_a, 1)
                f(gs[:, Q_B], gate[:, 0:8], ACT.Exp, scale=-1.0).then_inc(ac_a, 1)
                f(alog[:, 0, :], alog[:, 0, :], ACT.Exp).then_inc(ac_a, 1)
                act.wait_ge(dv_b, 1)
                f(gs[:, Q_GC], gs[:, Q_GC], ACT.Exp, scale=-1.0).then_inc(ac_b, 1)
                act.wait_ge(dv_b, 2)
                f(gs[:, Q_GL], gs[:, Q_EG], ACT.Ln).then_inc(ac_b, 1)
                act.wait_ge(dv_c, 2)
                act.wait_ge(mm_b, 1)
                f(gs[:, Q_EG], gs[:, Q_GC], ACT.Exp).then_inc(ac_c, 1)
                f(gs[:, Q_END], gs[:, Q_END], ACT.Exp).then_inc(ac_c, 1)
                f(gs[:, Q_GL], ps[:, 2 * BANK:2 * BANK + 8 * T].rearrange("p (j t) -> p j t", t=T), ACT.Exp
                  ).then_inc(ac_c, 1)
                meet(act, "act")

                with act.Fori(0, HEADS) as h:
                    for j in range(4):
                        act.wait_ge(mm_a, j + 1)
                        if j < 3:
                            if j == 0:
                                act.wait_ge(hcw_ready, 1)
                            f(spare[j], PAB[j % 2], ACT.Copy, scale=hcw[:, 3 + j:4 + j]).then_inc(conv0, 1)
                        else:
                            f(zT, PAB[1], ACT.Silu).then_inc(ac_c, 1)
                        if j >= 1:
                            i = j - 1
                            act.wait_ge(dv_a, i + 1)
                            dst = (kq[:, :, 1], kq[:, :, 0], chunks(spare[3]))[i]
                            f(dst, chunks(spare[i]), ACT.Silu).then_inc(ac_a, 1)
                    act.wait_ge(ac_a, 2)
                    for i in range(2):
                        f(chunks(spare[4 + i]), kq[:, :, 1 - i], ACT.Square).then_inc(ac_b, 1)
                    for i in range(2):
                        act.wait_ge(mm_b, i + 1)
                        f(spare[6 + i], PAB[i], ACT.Ln, bias=eps_col).then_inc(ac_d, 1)
                    for i in range(2):
                        act.wait_ge(ac_d, i + 1)
                        f(spare[6 + i], spare[6 + i], ACT.Exp, scale=-0.5, bias=(qscale_col if i == 0 else 0.0)
                          ).then_inc(rn, 1)
                    act.wait_ge(mm_c, 1)
                    f(ktok, chunks(PAB[0]), ACT.Copy).then_inc(ac_e, 1)
                    for d in range(2):
                        act.wait_ge(dv_d, d + 1)
                        f(PP[:, d], PP[:, d], ACT.Exp).then_inc(dec, 1)
                    for d in range(2):
                        act.wait_ge(mm_e, 6 + d)
                        f(U[:, d], chunks(PAB[d]), ACT.Copy).then_inc(ac_e, 1)
                    for i in range(6):
                        for d in range(2):
                            act.wait_ge(mm_e, 7 + 6 * i + d + 1)
                            f(PP[:, d], chunks(PAB[d]), ACT.Copy).then_inc(ac_e, 1)
                        if i < 5:
                            for d in range(2):
                                act.wait_ge(mm_e, 7 + 6 * i + 4 + d + 1)
                                f(DD[:, d], chunks(PAB[d]), ACT.Copy).then_inc(ac_e, 1)
                    for stp, live in SCAN:
                        for n, x, cc in live:
                            act.wait_ge(vnew_ps, n + 1)
                            if stp:
                                act.wait_ge(upd_ps, PREV[n] + 1)
                            f(chain[:, x, 3], XB(x)[:, 2 * P:3 * P], ACT.Copy, scale=hs[:, Q_END, x % 2, cc:cc + 1]
                              ).then_inc(vnew_sb, 1)
                            f(chain[:, x, 2], XB(x)[:, 2 * P:3 * P], ACT.Copy).then_inc(vnew_sb, 1)
                    act.wait_ge(dv_b, 3)
                    f(small[:, 20:20 + T], small[:, 10:10 + T], ACT.Sqrt).then_inc(ac_b, 1)
                    meet(act, "act")

                for t in range(2):
                    act.wait_ge(mm_a, 4 * t + 1)
                    if t:
                        act.wait_ge(dv_a, 2)
                    f(spare[0], PAB[0], ACT.Copy).then_inc(ac_a, 1)
                    act.wait_ge(dv_a, 2 * t + 1)
                    f(spare[2], spare[1], ACT.Copy, scale=cols[:, R_SCC + 2 + t:R_SCC + 3 + t]).then_inc(ac_c, 1)
                    act.wait_ge(mm_a, 4 * t + 4)
                    f(spare[4 + t], PAB[1], ACT.Copy).then_inc(ac_a, 1)
                for n in range(6):
                    t, (a, b) = n // 3, GROUPS[n % 3]
                    act.wait_ge(mm_b, n + 1)
                    f(YF(t)[:, a:b], ps[:, 2 * BANK * (n % 2):2 * BANK * (n % 2) + 256 * (b - a)].rearrange(
                        "p (c n) -> p c n", n=256), ACT.Copy).then_inc(ac_b, 1)
                meet(act, "act")

                for t in range(T):
                    s = int(t >= LT)
                    act.wait_ge(po_a, t + 1)
                    if t >= 1:
                        act.wait_ge(ac_a, t)
                    f(area[:, 17664:18688], xt[t % 2], ACT.Square, accum_out=small[:, t:t + 1]).then_inc(ac_a, 1)
                    act.wait_ge(dv_f, t + 1)
                    f(small[:, 10 + t:11 + t], small[:, 10 + t:11 + t], ACT.Sqrt).then_inc(ac_c, 1)
                    act.wait_ge(mm_b, t + 1)
                    if t >= 2:
                        act.wait_ge(mm_c, t - 1)
                    for k in range(4):
                        f(h2T[t % 2][:, k, :], ps[:, 4 * BANK + P * k:4 * BANK + P * k + P], ACT.Identity,
                          scale=A2[:, k, s:s + 1], bias=mod[:, SH2 + k, s:s + 1]).then_inc(ac_b, 1)
                    act.wait_ge(dv_g, t + 1)
                    f(small[:, 32:48], ps[:, 6 * BANK:6 * BANK + EXPERTS], ACT.Exp, bias=small[:, 50:51],
                      accum_out=small[:, 51:52]).then_inc(ac_e, 1)
                    act.wait_ge(mm_d, t + 1)
                    f(affT[:, P * t:P * t + P], ps[0:EXPERTS, 7 * BANK:7 * BANK + P], ACT.Copy).then_inc(ac_d, 1)
                meet(act, "act")

                def modulate(b):
                    E = epoch[b]
                    act.wait_ge(E["xe_ps"], 1)
                    for k in range(4):
                        f(xeT[b][:, k, 0:CAPL], ps[:, P * k:P * k + P], ACT.Identity, scale=A2[:, k, 0:1],
                          bias=mod[:, SH2 + k, 0:1]).then_inc(E["xe_sb"], 1)

                modulate(0)
                with act.Fori(0, EXPERTS // 2):
                    for b in range(2):
                        E = epoch[b]
                        for m in range(KT):
                            act.wait_ge(E["gu_ps"], m + 1)
                            if m >= 2:
                                act.wait_ge(E["hid_sb"], m - 1)
                            f(sg[:, m % 2], ps[:, (4 + m % 2) * BANK:(4 + m % 2) * BANK + CAP], ACT.Silu
                              ).then_inc(E["gate_sb"], 1)
                        act.wait_ge(ep_go[1 - b]["act"], 1)
                        act.sem_clear(ep_go[1 - b]["act"])
                        modulate(1 - b)
                        for m in range(KT):
                            act.wait_ge(E["dn_ps"], m + 1)
                            at = (6 + m % 2) * BANK
                            f(yeT[:, m, 0:CAPL], ps[:, at:at + CAPL], ACT.Copy, scale=mod[:, G2 + m, 0:1]
                              ).then_inc(E["ye_ch"], 1)
                            f(yeT[:, m, CAPL:CAP], ps[:, at + CAPL:at + CAP], ACT.Copy, scale=mod[:, G2 + m, 1:2]
                              ).then_inc(E["ye_ch"], 1)
                        act.wait_ge(E["ye_ps"], 1)
                        f(yeC[b], ps[0:CAPC, 2 * BANK:4 * BANK], ACT.Copy, scale=cur[0:CAPC, b, 1:2]
                          ).then_inc(E["ye_sb"], 1)
                        act.drain().then_inc(ep_arrive[b], 1)
                act.wait_ge(ep_go[1]["act"], 1)
                act.sem_clear(ep_go[1]["act"])
                meet(act, "act")

            for t in range(T):
                act.wait_ge(loaded[1 + t % 2], 16 * (t // 2 + 1))
                if t >= 1:
                    act.wait_ge(ac_a, t)
                f(h2T[0].rearrange("p k n -> p (k n)"), xt[t % 2], ACT.Square, accum_out=small[:, t:t + 1]
                  ).then_inc(ac_a, 1)
                act.wait_ge(dv_a, t + 1)
                f(small[:, 10 + t:11 + t], small[:, 10 + t:11 + t], ACT.Sqrt).then_inc(ac_d, 1)

        @block.vector
        def _(dve):
            v = nc.vector
            step = Steps(dve, dve_step)

            dve.wait_ge(loaded[0], 48)
            v.tensor_copy(identb[:], ident)
            v.tensor_copy(bigb[:].rearrange("p d n -> p (d n)"), big)
            v.memset(tw[:], 0.0)
            v.memset(ix[:], 0)
            dve.wait_ge(loaded[1], 32)
            for t in range(LT):
                b = t % 2
                dve.wait_ge(loaded[2 + b], 48 * (t // 2 + 1))
                v.tensor_tensor(xt[b][:, 0:512], xt[b][:, 0:512], area[:, 6656 - 512 * b:7168 - 512 * b], ALU.add
                                ).then_inc(dv_a, 1)
                v.tensor_tensor(xt[b][:, 512:1024], xt[b][:, 512:1024], area[:, 7168:7680], ALU.add
                                ).then_inc(dv_a, 1)
            meet(dve, "dve")

            with dve.Fori(0, DEPTH) as l:
                step.reset()
                dve.wait_ge(mm_b, 1)
                step(v.tensor_copy(cols[:, 0:ROWS], ps[:, BANK:BANK + ROWS]))
                dve.wait_ge(mm_a, 12)
                step(v.tensor_tensor(mod[:], ps[:, 0:96].rearrange("p (m s) -> p m s", s=2),
                                     spread(cols[:, 0:48], 2), ALU.add))
                for A, sc, r in ((A1, SC1, R_N1), (A2, SC2, R_N2)):
                    step(v.scalar_tensor_tensor(out=A[:], in0=mod[:, sc:sc + KT, :], scalar=1.0,
                                                in1=spread(cols[:, r:r + KT], 2), op0=ALU.add, op1=ALU.mult))
                for i in range(2):
                    v.tensor_tensor(spare[2 * i][:, 0:1024].rearrange("p (k n) -> p k n", k=KT), over(ident, KT),
                                    spread(mod[:, G1:G1 + KT, i], P), ALU.mult).then_inc(dv_c, 1)
                for t in range(T + 1):
                    if t < T:
                        dve.wait_ge(ac_a, t + 1)
                        step(v.tensor_scalar(small[:, 10 + t:11 + t], small[:, t:t + 1], 1.0 / D, EPS, ALU.mult, ALU.add))
                        v.reciprocal(small[:, 10 + t:11 + t], small[:, 10 + t:11 + t]).then_inc(dv_a, 1)
                        dve.wait_ge(ac_d, t + 1)
                        if t >= 2:
                            dve.wait_ge(mm_d, t - 1)
                        v.tensor_scalar(xn[t % 2], xt[t % 2], small[:, 10 + t:11 + t], None, ALU.mult).then_inc(dv_b, 1)
                    if t >= 1:
                        u, s = t - 1, int(t - 1 >= LT)
                        dve.wait_ge(mm_d, u + 1)
                        for k in range(4, KT):
                            at = (2 + 2 * (u % 2)) * BANK + P * k
                            v.tensor_scalar(hT[:, k, P * u:P * u + P], ps[:, at:at + P], A1[:, k, s:s + 1],
                                            mod[:, SH1 + k, s:s + 1], ALU.mult, ALU.add).then_inc(dv_d, 1)
                meet(dve, "dve")

                step.reset()
                gate = ps[:, 0:16 * T].rearrange("p (t j) -> p j t", j=16)
                dve.wait_ge(mm_a, 1)
                dve.wait_ge(ac_a, 1)
                X = gs[:, Q_G]
                step(v.tensor_tensor(X, gate[:, 8:16], spread(alog[:, 1, :], T), ALU.add))
                v.scalar_tensor_tensor(out=gs[:, Q_GC], in0=X, scalar=-1.0, in1=X, op0=ALU.mult, op1=ALU.max
                                       ).then_inc(dv_b, 1)
                dve.wait_ge(ac_b, 1)
                v.tensor_scalar(gs[:, Q_EG], gs[:, Q_GC], 1.0, None, ALU.add).then_inc(dv_b, 1)
                dve.wait_ge(dv_b, 2)
                step(v.tensor_scalar(gs[:, Q_NEG], gs[:, Q_EG], -1.0, None, ALU.add))
                step(v.tensor_tensor(gs[:, Q_NEG], gs[:, Q_GC], gs[:, Q_NEG], ALU.subtract))
                dve.wait_ge(ac_b, 2)
                step(v.tensor_tensor(gs[:, Q_GL], gs[:, Q_GL], gs[:, Q_NEG], ALU.add))
                step(v.scalar_tensor_tensor(out=X, in0=X, scalar=0.0, in1=gs[:, Q_GL], op0=ALU.max, op1=ALU.add))
                dve.wait_ge(ac_a, 2)
                v.scalar_tensor_tensor(out=X, in0=X, scalar=-1.0, in1=spread(alog[:, 0, :], T), op0=ALU.mult,
                                       op1=ALU.mult).then_inc(dv_a, 1)
                step(v.tensor_scalar(gs[:, Q_B], gs[:, Q_B], 1.0, None, ALU.add))
                step(v.reciprocal(gs[:, Q_B], gs[:, Q_B]))
                v.tensor_scalar(gs[:, Q_NB], gs[:, Q_B], -1.0, None, ALU.mult)
                dve.wait_ge(mm_b, 1)
                v.tensor_copy(gs[:, Q_GC], ps[:, BANK:BANK + 8 * T].rearrange("p (j t) -> p j t", t=T)
                              ).then_inc(dv_c, 1)
                dve.wait_ge(dv_c, 1)
                v.tensor_tensor(gs[:, Q_END], ps[:, 2 * BANK:2 * BANK + 8 * T].rearrange("p (j t) -> p j t", t=T),
                                gs[:, Q_GC], ALU.subtract).then_inc(dv_c, 1)
                dve.wait_ge(ac_c, 3)
                v.tensor_scalar(gs[:, Q_NEG], gs[:, Q_EG], -1.0, None, ALU.mult)
                meet(dve, "dve")

                with dve.Fori(0, HEADS) as h:
                    step.reset()
                    v.tensor_copy(hs[:].rearrange("p q d t -> p (q d) t"), gs[:].rearrange(
                        "p q (d h) t -> p (q d) (h t)", d=2)[:, :, ds(h * T, T)]).then_inc(hs_ready, 1)
                    v.tensor_copy(hcw[:, 0:9], cols[:, ds(h + R_DNC, 33)][:, 0:33:4]).then_inc(hcw_ready, 1)
                    dve.wait_ge(hcw_ready, 1)
                    for j in range(3):
                        dve.wait_ge(conv0, j + 1)
                        src, dst = PAB[j % 2], spare[j]
                        for lo, hi in SEGS:
                            ins = v.scalar_tensor_tensor(out=dst[:, lo + 1:hi], in0=src[:, lo:hi - 1],
                                                         scalar=hcw[:, j:j + 1], in1=dst[:, lo + 1:hi],
                                                         op0=ALU.mult, op1=ALU.add)
                        step(ins)
                        for lo, hi in SEGS:
                            ins = v.scalar_tensor_tensor(out=dst[:, lo:hi - 1], in0=src[:, lo + 1:hi],
                                                         scalar=hcw[:, 6 + j:7 + j], in1=dst[:, lo:hi - 1],
                                                         op0=ALU.mult, op1=ALU.add)
                        ins.then_inc(dv_a, 1)
                    for i in range(2):
                        dve.wait_ge(rn, i + 1)
                        v.tensor_tensor(kq[:, :, 1 - i], kq[:, :, 1 - i], chunks(spare[6 + i]), ALU.mult
                                        ).then_inc(dv_b, 1)
                    dve.wait_ge(mm_c, 2)
                    v.tensor_copy(vtok, chunks(PAB[1])).then_inc(dv_c, 1)
                    dve.wait_ge(dv_b, 2)
                    for d in range(2):
                        dve.wait_ge(mm_d, d + 1)
                        v.tensor_tensor(PP[:, d], chunks(PAB[d]), spread(hs[:, Q_GC, d], P), ALU.subtract
                                        ).then_inc(dv_d, 1)
                    for g, (a, b) in enumerate(GROUPS):
                        dve.wait_ge(mm_e, g + 1)
                        src = (ps[:, 0:1024], ps[:, 3 * BANK:5 * BANK], ps[:, 0:1024])[g]
                        src = src[:, 0:256 * (b - a)].rearrange("p (c j n) -> p c j n", j=2, n=P)
                        for d in range(2):
                            dve.wait_ge(dec, d + 1)
                            for i, dst in enumerate((DD, QK)):
                                v.tensor_tensor(dst[:, d, a:b], src[:, :, i], PP[:, d, a:b], ALU.mult
                                                ).then_inc(dv_d, 1)
                    for d in range(2):
                        dve.wait_ge(mm_e, 4 + d)
                        v.tensor_tensor(LL[:, d], chunks(PAB[d]), spread(hs[:, Q_NB, d], P), ALU.mult
                                        ).then_inc(lsig, 1)
                        step(v.tensor_copy(DD[:, d], over(ident, T)))
                        dve.wait_ge(lsig, d + 1)
                        v.copy_predicated(DD[:, d], over((lower, upper)[d][0], T), LL[:, d]).then_inc(dv_e, 1)
                    for i in range(6):
                        for d in range(2):
                            dve.wait_ge(mm_e, 7 + 6 * i + 2 + d + 1)
                            v.copy_predicated(U[:, d], over((upper, lower)[d][i + 1], T), chunks(PAB[d])
                                              ).then_inc(dv_e, 1)
                    dve.wait_ge(mm_e, 7 + 6 * 5 + 4)
                    v.memset(oo, 0.0)
                    v.memset(chain[:, 2:4, 0], 0.0).then_inc(dv_e, 1)
                    dve.wait_ge(dv_e, 15)
                    for stp, live in SCAN:
                        for n, x, cc in live:
                            dve.wait_ge(ks_ps, n + 1)
                            v.scalar_tensor_tensor(out=chain[:, x, 1], in0=XA(x)[:, 0:P],
                                                   scalar=hs[:, Q_NEG, x % 2, cc:cc + 1], in1=vtok[:, cc],
                                                   op0=ALU.mult, op1=ALU.add).then_inc(vprime, 1)
                        for n, x, cc in live:
                            if SEEN[n] is not None:
                                dve.wait_ge(o_done, SEEN[n] + 1)
                            v.scalar_tensor_tensor(out=oo[:, cc], in0=XA(x)[:, P:2 * P],
                                                   scalar=hs[:, Q_EG, x % 2, cc:cc + 1], in1=oo[:, cc],
                                                   op0=ALU.mult, op1=ALU.add).then_inc(o_half, 1)
                        for n, x, cc in live:
                            dve.wait_ge(upd_ps, n + 1)
                            v.scalar_tensor_tensor(out=chain[:, x, 0], in0=chain[:, x, 0],
                                                   scalar=hs[:, Q_GL, x % 2, cc:cc + 1], in1=XB(x)[:, P:2 * P],
                                                   op0=ALU.mult, op1=ALU.add).then_inc(dv_f, 1)
                            dve.wait_ge(o_half, n + 1)
                            v.tensor_tensor(oo[:, cc], XB(x)[:, 0:P], oo[:, cc], ALU.add).then_inc(o_done, 1)
                    dve.wait_ge(o_done, NSCAN)
                    step(v.tensor_tensor(PP[:, 0], oo, oo, ALU.mult))
                    step(v.tensor_reduce(small[:, 0:T], PP[:, 0], AX.X, ALU.add))
                    step(v.tensor_scalar(small[:, 10:10 + T], small[:, 0:T], 1.0 / P, EPS, ALU.mult, ALU.add))
                    v.reciprocal(small[:, 10:10 + T], small[:, 10:10 + T]).then_inc(dv_b, 1)
                    dve.wait_ge(ac_b, 3)
                    v.tensor_tensor(oo, oo, spread(small[:, 20:20 + T], P), ALU.mult).then_inc(dv_c, 1)
                    dve.wait_ge(mm_c, 3)
                    v.scalar_tensor_tensor(out=yT[:, ds(h * N, N)], in0=PAB[0], scalar=cols[:, R_DNN:R_DNN + 1],
                                           in1=zT, op0=ALU.mult, op1=ALU.mult)
                    meet(dve, "dve")

                step.reset()
                for t in range(2):
                    dve.wait_ge(mm_a, 4 * t + 2)
                    dve.wait_ge(ac_a, 2 * t + 1)
                    v.tensor_tensor(spare[1], PAB[1], spare[0], ALU.mult).then_inc(dv_a, 1)
                    dve.wait_ge(dv_a, 2 * t + 1)
                    dve.wait_ge(ac_c, t + 1)
                    for tap, (di, si) in ((0, (1, 0)), (4, (0, 1))):
                        for lo, hi in SEGS:
                            ins = v.scalar_tensor_tensor(out=spare[2][:, lo + di:hi - si], in0=spare[1][:, lo + si:hi - di],
                                                         scalar=cols[:, R_SCC + tap + t:R_SCC + tap + t + 1],
                                                         in1=spare[2][:, lo + di:hi - si], op0=ALU.mult, op1=ALU.add)
                        step(ins)
                    dve.wait_ge(mm_a, 4 * t + 3)
                    v.tensor_tensor(yT[:, (4 + t) * N:(5 + t) * N], PAB[0], spare[2], ALU.mult).then_inc(dv_a, 1)
                    dve.wait_ge(dv_a, 2 * t + 2)
                n = 0
                for t in range(2):
                    for half in range(3):
                        lo, hi = SPANS[half]
                        dve.wait_ge(mm_c, n + 1)
                        v.tensor_copy(yT[:, (6 + t) * N + lo:(6 + t) * N + hi],
                                      ps[:, (4 + n % 2) * BANK:(4 + n % 2) * BANK + hi - lo]).then_inc(dv_b, 1)
                        n += 1
                meet(dve, "dve")

                step.reset()
                for t in range(T):
                    s = int(t >= LT)
                    b = t % 2
                    dve.wait_ge(mm_a, t + 1)
                    if t >= 2:
                        dve.wait_ge(st[2 + b], 16 * (t // 2))
                        dve.wait_ge(mm_b, t - 1)
                    v.tensor_tensor(xn[b], ps[:, 2 * b * BANK:2 * b * BANK + D], g1b[:, s, :], ALU.mult).then_inc(dv_a, 1)
                    dve.wait_ge(ac_a, t + 1)
                    step(v.tensor_scalar(small[:, 10 + t:11 + t], small[:, t:t + 1], 1.0 / D, EPS, ALU.mult, ALU.add))
                    v.reciprocal(small[:, 10 + t:11 + t], small[:, 10 + t:11 + t]).then_inc(dv_f, 1)
                    dve.wait_ge(ac_c, t + 1)
                    v.tensor_scalar(xn[b], xt[b], small[:, 10 + t:11 + t], None, ALU.mult).then_inc(dv_b, 1)
                    dve.wait_ge(mm_b, t + 1)
                    if t >= 2:
                        dve.wait_ge(mm_c, t - 1)
                    for k in range(4, KT):
                        v.tensor_scalar(h2T[b][:, k, :], ps[:, 4 * BANK + P * k:4 * BANK + P * k + P],
                                        A2[:, k, s:s + 1], mod[:, SH2 + k, s:s + 1], ALU.mult, ALU.add
                                        ).then_inc(dv_d, 1)
                    dve.wait_ge(mm_c, t + 1)
                    v.tensor_reduce(small[:, 50:51], ps[:, 6 * BANK:6 * BANK + EXPERTS], AX.X, ALU.max, negate=True
                                    ).then_inc(dv_g, 1)
                    dve.wait_ge(ac_e, t + 1)
                    step(v.reciprocal(small[:, 52:53], small[:, 51:52]))
                    if t >= 1:
                        dve.wait_ge(mm_d, t)
                    v.tensor_scalar(small[:, 32:48], small[:, 32:48], small[:, 52:53], None, ALU.mult).then_inc(dv_c, 1)
                dve.wait_ge(ac_d, T)
                step(v.tensor_copy(work, affT))
                for lo, hi, o, cap in ((0, LAT, 0, CAPL), (LAT, N, CAPL, CAPC)):
                    for r in range(cap // 8):
                        q = slice(o + 8 * r, o + 8 * r + 8)
                        step(v.max(out=tv[:, q], in_=work[:, lo:hi]))
                        step(v.max_index(out=ti[:, q], in_max=tv[:, q], in_values=work[:, lo:hi]))
                        step(v.match_replace(out=work[:, lo:hi], in_to_replace=tv[:, q], in_values=work[:, lo:hi],
                                             imm_value=-1.0))
                step(v.tensor_copy(tf, ti))
                v.tensor_scalar(tf[:, CAPL:CAP], tf[:, CAPL:CAP], float(LAT), None, ALU.add).then_inc(dv_e, 1)
                dve.wait_ge(mm_e, 1)
                for s, n in ((0, CAPL), (1, CAPC)):
                    for j in (0, 16):
                        v.tensor_copy(tw[0:n, s, j:j + (16 if j == 0 else 1)],
                                      ps[0:n, 32 * s:32 * s + (16 if j == 0 else 1)])
                        v.tensor_copy(ix[0:n, s, j:j + (16 if j == 0 else 1)],
                                      ps[0:n, 32 * s + 16:32 * s + 16 + (16 if j == 0 else 1)])
                meet(dve, "dve")

                def modulate(b):
                    E = epoch[b]
                    dve.wait_ge(E["xe_ps"], 1)
                    for k in range(4, 8):
                        v.tensor_scalar(xeT[b][:, k, 0:CAPL], ps[:, P * k:P * k + P], A2[:, k, 0:1],
                                        mod[:, SH2 + k, 0:1], ALU.mult, ALU.add).then_inc(E["xe_sb"], 1)
                    v.tensor_tensor(xeT[b][:, :, CAPL:CAP], ps[:, 2 * BANK:2 * BANK + CAPC * KT].rearrange(
                        "p (k n) -> p k n", k=KT), spread(A2[:, :, 1], CAPC), ALU.mult).then_inc(E["moe_dve"], 1)
                    dve.wait_ge(E["moe_dve"], 1)
                    v.tensor_tensor(xeT[b][:, :, CAPL:CAP], xeT[b][:, :, CAPL:CAP],
                                    spread(mod[:, SH2:SH2 + KT, 1], CAPC), ALU.add).then_inc(E["xe_sb"], 2)

                modulate(0)
                with dve.Fori(0, EXPERTS // 2):
                    for b in range(2):
                        E = epoch[b]
                        for m in range(KT):
                            dve.wait_ge(E["gate_sb"], m + 1)
                            at = (4 + m % 2) * BANK + CAP
                            v.tensor_tensor(hid[:, m, :], ps[:, at:at + CAP], sg[:, m % 2], ALU.mult
                                            ).then_inc(E["hid_sb"], 1)
                        dve.wait_ge(ep_go[1 - b]["dve"], 1)
                        dve.sem_clear(ep_go[1 - b]["dve"])
                        modulate(1 - b)
                        dve.wait_ge(E["ye_ps"], 1)
                        v.tensor_scalar(yeL[b], ps[:, 0:D], cur[:, b, 0:1], None, ALU.mult).then_inc(E["ye_sb"], 1)
                        dve.drain().then_inc(ep_arrive[b], 1)
                dve.wait_ge(ep_go[1]["dve"], 1)
                dve.sem_clear(ep_go[1]["dve"])
                meet(dve, "dve")

            step.reset()
            dve.wait_ge(loaded[0], 16)
            for t in range(T):
                dve.wait_ge(ac_a, t + 1)
                step(v.tensor_scalar(small[:, 10 + t:11 + t], small[:, t:t + 1], 1.0 / D, EPS, ALU.mult, ALU.add))
                v.reciprocal(small[:, 10 + t:11 + t], small[:, 10 + t:11 + t]).then_inc(dv_a, 1)
                dve.wait_ge(ac_d, t + 1)
                if t >= 2:
                    dve.wait_ge(st[t % 2], 16 * (t // 2))
                v.scalar_tensor_tensor(out=xn[t % 2], in0=xt[t % 2], scalar=small[:, 10 + t:11 + t], in1=g1b[:, 0, :],
                                       op0=ALU.mult, op1=ALU.mult).then_inc(dv_b, 1)

        @block.gpsimd
        def _(pool):
            g = nc.gpsimd
            meet_pool(pool)
            with pool.Fori(0, DEPTH) as l:
                meet_pool(pool)
                meet_pool(pool)
                with pool.Fori(0, HEADS):
                    for d in range(2):
                        pool.wait_ge(dv_e, 13 + d)
                        pool.wait_ge(hs_ready, 1)
                        g.tensor_tensor(U[:, d], U[:, d], spread(hs[:, Q_B, d], P), ALU.mult).then_inc(po_b, 1)
                    meet_pool(pool)
                meet_pool(pool)
                for t in range(T):
                    pool.wait_ge(dv_a, t + 1)
                    pool.wait_ge(loaded[1 + t % 2], 16 * (t // 2 + 1))
                    g.tensor_tensor(xt[t % 2], xt[t % 2], xn[t % 2], ALU.add).then_inc(po_a, 1)
                meet_pool(pool)

                def gather(b, e):
                    E = epoch[b]
                    g.tensor_copy(curi[:, b, :], ix[:, :, ds(e, 1)].rearrange("p s a -> p (s a)")).then_inc(pool_step, 1)
                    g.tensor_copy(cur[:, b, :], tw[:, :, ds(e, 1)].rearrange("p s a -> p (s a)")).then_inc(pool_step, 1)
                    pool.wait_ge(pool_step, 2)
                    pool.sem_clear(pool_step)
                    for s, (dst, n) in enumerate(((xeL[b], CAPL), (xeC[b], CAPC))):
                        g.indirect_dma_start(out=dst, out_offset=None, in_=xnorm,
                                             in_offset=bass.IndirectOffsetOnAxis(ap=curi[0:n, b, s:s + 1], axis=0)
                                             ).then_inc(E[("gathered_lat", "gathered_ctx")[s]], 16)

                gather(0, 0)
                for x in ("pe", "act", "dve"):
                    pool.sem_inc(ep_go[1][x], 1)
                with pool.Fori(0, EXPERTS // 2) as i:
                    for b in range(2):
                        E = epoch[b]
                        gather(1 - b, i * 2 + (b + 1))
                        pool.wait_ge(E["ye_sb"], 2)
                        for s, (src, n) in enumerate(((yeL[b], CAPL), (yeC[b], CAPC))):
                            g.indirect_dma_start(out=xres, out_offset=bass.IndirectOffsetOnAxis(
                                ap=curi[0:n, b, s:s + 1], axis=0), in_=src, in_offset=None,
                                compute_op=ALU.add).then_inc(scattered[s], 16)
                        for s in scattered + [epoch[1 - b]["gathered_lat"], epoch[1 - b]["gathered_ctx"]]:
                            pool.wait_ge(s, 16)
                        pool.dma_reset(nums(scattered))
                        pool.sem_clear(nums(scattered))
                        pool.wait_ge(ep_arrive[b], 3)
                        pool.sem_clear(ep_arrive[b])
                        pool.dma_reset(nums([E["gathered_lat"], E["gathered_ctx"]]))
                        pool.sem_clear(nums(E.values()))
                        for x in ("pe", "act", "dve"):
                            pool.sem_inc(ep_go[b][x], 1)
                pool.drain()
                pool.wait_ge(arrive, 4)
                pool.sem_clear(arrive)
                pool.sem_clear(nums(local))
                pool.dma_reset(nums([epoch[0]["gathered_lat"], epoch[0]["gathered_ctx"]]))
                pool.sem_clear(nums(epoch[0].values()))
                for x in go.values():
                    pool.sem_inc(x, 1)


_INS = ["x_prompt", "x_sample", "state_delta", "c", "c_ctx", "w_ada", "b_ada", "norm1_w", "norm2_w", "w_in",
        "dn_conv_w", "dn_a_log", "dn_dt_bias", "dn_norm_w", "sc_conv_w", "w_out", "w_router", "w_gate", "w_up",
        "w_down", "final_norm_w"]
_OUTS = [(1, CTX, D), (1, LAT, D), (1, DEPTH, 2, HEADS, P, P)]


def _constants():
    import numpy as np

    i = np.arange(P)
    row, col = i[:, None], i[None, :]
    parts = [row == col, np.ones((P, P)), row <= col, row >= col]
    low = [(row // (2 * s) == col // (2 * s)) & (row // s % 2 == 1) & (col // s % 2 == 0) for s in LEVELS]
    parts += low + [m.T for m in low]
    parts += [-1e30 * (row > col), -1e30 * (row < col)]
    ang = 2 * np.pi * np.outer(i % 64, i % 64) / 64
    same = row // 64 == col // 64
    parts += [np.cos(ang) * same, np.sin(ang) * same]
    parts += [np.full((P, 1), EPS), np.full((P, 1), -0.5 * np.log(P))]
    consts = np.concatenate([p.astype(np.float32) for p in parts], axis=1)

    def dft(n):
        ang = 2 * np.pi * (np.outer(np.arange(n), np.arange(n)) % n) / n
        return (np.stack([np.cos(ang), -np.sin(ang)]) / np.sqrt(n * 64)).astype(np.float32)

    quarter = D // 4
    omega = 10000.0 ** (-np.arange(quarter, dtype=np.float64) / quarter)

    def pos(n):
        a = np.arange(n)[:, None] * omega
        return np.concatenate([np.sin(a), np.cos(a)], axis=1).astype(np.float32)

    return {"consts": consts, "dft_lat": dft(LAT), "dft_ctx": dft(CTX), "pos_row": pos(LAT // 64), "pos_col": pos(64)}


def kernel(**inputs):
    import numpy as _np
    import concourse.bacc as _bacc
    from concourse.bass_utils import run_bass_kernel_spmd as _run

    nc = _bacc.Bacc("TRN2", target_bir_lowering=False, num_devices=1)
    arrays, args = {}, []
    given = {name: _np.ascontiguousarray(inputs[name]) for name in _INS}
    given.update(_constants())
    for name, a in given.items():
        arrays[f"in_{name}_dram"] = a
        args.append(nc.dram_tensor(f"in_{name}_dram", a.shape, mybir.dt.from_np(a.dtype), kind="ExternalInput").ap())
    for i, shape in enumerate(_OUTS):
        args.append(nc.dram_tensor(f"out_{i}_dram", shape, F32, kind="ExternalOutput").ap())
    trunk(nc, *args)
    r = _run(nc, [arrays], core_ids=[0])
    return tuple(r.results[0][f"out_{i}_dram"] for i in range(len(_OUTS)))
```

```python
from contextlib import ExitStack

import concourse.bass as bass
from concourse import mybir

F32 = mybir.dt.float32
BF16 = mybir.dt.bfloat16
U32 = mybir.dt.uint32
I32 = mybir.dt.int32
ALU = mybir.AluOpType
ACT = mybir.ActivationFunctionType
AX = mybir.AxisListType
ds = bass.ds

P = 128
D = 1024
KT = D // P
DEPTH = 2
LAT, CTX = 1024, 256
LT, CT = LAT // P, CTX // P
T = LT + CT
N = T * P
HEADS = 4
DNW = HEADS * P
SCW = FOW = 256
SC0 = 3 * DNW + DNW + 4 * HEADS
EXPERTS = 16
CAPL, CAPC = 2 * LAT // EXPERTS, 2 * CTX // EXPERTS
CAP = CAPL + CAPC
LEVELS = [1, 2, 4, 8, 16, 32, 64]
EPS = 1e-6
BANK = 512
R_ADA, R_N1, R_N2, R_DNC, R_SCC, R_DNN = 0, 48, 56, 64, 100, 106
ROWS = 107
SH1, SC1, G1, SH2, SC2, G2 = 0, 8, 16, 24, 32, 40
Q_G, Q_NB, Q_B, Q_GC, Q_EG, Q_NEG, Q_END, Q_GL = range(8)
SPANS = [(0, 512), (512, 1024), (1024, 1280)]
GROUPS = [(0, 4), (4, 8), (8, 10)]
SEGS = [(0, LAT), (LAT, N)]
NCONST = 128 * (4 + 2 * len(LEVELS) + 2 + 2) + 3


def trunk(nc, x_prompt, x_sample, state_delta, c, c_ctx, w_ada, b_ada, norm1_w, norm2_w, w_in, dn_conv_w,
          dn_a_log, dn_dt_bias, dn_norm_w, sc_conv_w, w_out, w_router, w_gate, w_up, w_down, final_norm_w,
          consts, dft_lat, dft_ctx, pos_row, pos_col, y_prompt, y_sample, new_state):
    xres = nc.dram_tensor("xres", (N, D), F32, kind="Internal").ap()
    xnorm = nc.dram_tensor("xnorm", (N, D), F32, kind="Internal").ap()

    with ExitStack() as ctx:
        def sb(name, shape, dt=F32):
            return ctx.enter_context(nc.sbuf_tensor(name, shape, dt))

        def sem(name):
            return ctx.enter_context(nc.semaphore(name))

        ring = sb("ring", [P, 6 * 4096])
        hT = ring[:, 0:KT * N].rearrange("p (k n) -> p k n", k=KT)
        yT = ring[:, KT * N:2 * KT * N]
        hw = ring[:, 2 * KT * N:].rearrange("p (j k c) -> p j k c", j=4, k=KT)
        area = sb("area", [P, 19200])
        kq = area[:, 0:2560].rearrange("p (c j n) -> p c j n", j=2, n=P)
        ktok = area[:, 2560:3840].rearrange("p (c n) -> p c n", n=P)
        vtok = area[:, 3840:5120].rearrange("p (c n) -> p c n", n=P)
        zT = area[:, 5120:6400]

        def pair(at):
            return area[:, at:at + 2560].rearrange("p (d c n) -> p d c n", d=2, n=P)

        U, DD, LL, PP, QK = (pair(at) for at in range(6400, 19200, 2560))
        spare = [area[:, at:at + N] for at in range(6400, 19200, N)]
        oo = area[:, 8960:10240].rearrange("p (c n) -> p c n", n=P)
        chain = sb("chain", [P, 4, 4, P])
        cst = sb("cst", [P, NCONST])
        ident, ones, triF, triB = (cst[:, P * i:P * i + P] for i in range(4))
        lower = [cst[:, P * (4 + i):P * (5 + i)].bitcast(I32) for i in range(7)]
        upper = [cst[:, P * (11 + i):P * (12 + i)].bitcast(I32) for i in range(7)]
        big = cst[:, P * 18:P * 20]
        chdft = cst[:, P * 20:P * 22]
        eps_col = cst[:, P * 22:P * 22 + 1]
        qscale_col = cst[:, P * 22 + 1:P * 22 + 2]
        middle_col = cst[:, P * 22 + 2:P * 22 + 3]
        identb = sb("identb", [P, P], BF16)
        bigb = sb("bigb", [P, 2, P], BF16)
        condT = sb("condT", [P, 2, KT])
        rows = ring[:, 24320:24576].rearrange("p (l n) -> p l n", l=2)
        allcols = sb("allcols", [P, DEPTH, ROWS])
        cols = sb("cols", [P, ROWS])
        mod = sb("mod", [P, 48, 2])
        A1 = sb("A1", [P, KT, 2])
        A2 = sb("A2", [P, KT, 2])
        g1b = sb("g1b", [P, 2, D])
        crow = g1b[0:16, 0, 0:P]
        modrow = g1b[0:2].rearrange("p s d -> p (s d)")
        w16 = sb("w16", [P, KT, 16])
        wr = sb("wr", [P, KT, EXPERTS])
        alog = sb("alog", [P, 2, 8])
        def ada_buffers(region):
            cut = region.rearrange("p (i k c) -> p i k c", i=5, k=KT)
            return [cut[:, 0], cut[:, 1]], cut[:, 2], cut[:, 3:5].rearrange("p i k c -> p (i k) c")

        ada_head = ada_buffers(yT[:, 4 * N:8 * N])
        ada_moe = ada_buffers(area[:, 13632:18752])
        gs = sb("gs", [P, 8, 8, T])
        hs = sb("hs", [P, 8, 2, T])
        hcw = sb("hcw", [P, 16])
        small = sb("small", [P, 64])
        tw = sb("tw", [P, 2, 17])
        ix = sb("ix", [P, 2, 17], U32)
        cur = sb("cur", [P, 2, 2])
        curi = sb("curi", [P, 2, 2], U32)
        xt = [area[:, 1024 * i:1024 * i + 1024] for i in range(2)]
        xn = [area[:, 1024 * i:1024 * i + 1024] for i in (2, 3)]
        h2T = [area[:, 1024 * i:1024 * i + 1024].rearrange("p (k n) -> p k n", k=KT) for i in (4, 5)]
        ada0 = [ring[:, at:at + 4096].rearrange("p (k c) -> p k c", k=KT) for at in range(0, 16384, 4096)]
        x0 = [area[:, 1024 * t:1024 * t + 1024] for t in range(LT)]
        wo = [area[:, at:at + 4096].rearrange("p (k c) -> p k c", k=KT) for at in (6144, 10240)]
        wo_end = ring[:, 9216:9728]
        LISTS, LHALF = 80, LAT // 2
        affs = area[:, 14336:14336 + 4 * LISTS].rearrange("p (j e) -> p j e", j=4)
        work = area[0:LISTS, 14848:14848 + LHALF]
        tv = area[0:LISTS, 15360:15360 + CAPL]
        ti = area[0:LISTS, 15488:15488 + CAPL].bitcast(U32)
        tf = area[0:LISTS, 15616:15616 + CAPL]
        tr = area[0:LISTS, 15744:15744 + CAPL]
        first_token = area[0:LISTS, 15872:15873]
        lists = area[:, 15904:15904 + 2 * LISTS].rearrange("p (i e) -> p i e", i=2)
        in_first = area[:, 16128:16128 + EXPERTS]
        merged = area[:, 16160:16160 + EXPERTS]
        square = area[:, 17664:18688]

        xeL = [area[:, 1024 * i:1024 * i + 1024] for i in range(2)]
        xeC = [area[0:CAPC, 1024 * i:1024 * i + 1024] for i in (2, 3)]
        xeT = [area[:, 4096 + 1280 * i:5376 + 1280 * i].rearrange("p (k n) -> p k n", k=KT) for i in range(2)]
        hid = area[:, 6656:7936].rearrange("p (k n) -> p k n", k=KT)
        yeT = area[:, 7936:9216].rearrange("p (k n) -> p k n", k=KT)
        yeL = [area[:, 9216 + 1024 * i:10240 + 1024 * i] for i in range(2)]
        yeC = [area[0:CAPC, 11264 + 1024 * i:12288 + 1024 * i] for i in range(2)]
        sg = area[:, 13312:13632].rearrange("p (b n) -> p b n", b=2)

        ps = ctx.enter_context(nc.psum_tensor("ps", [P, 8 * BANK], F32))
        PAB = [ps[:, 0:N], ps[:, 3 * BANK:3 * BANK + N]]
        PZ = ps[:, 4 * BANK:4 * BANK + N]
        diag = [area[:, at:at + 1024].rearrange("p (k n) -> p k n", k=KT) for at in (4096, 5120)]

        def chunks(ap):
            return ap.rearrange("p (c n) -> p c n", n=P)

        def spread(col, n):
            return col.unsqueeze(len(col.shape)).to_broadcast(list(col.shape) + [n])

        def over(mat, n):
            return mat.unsqueeze(1).to_broadcast([P, n, P])

        local = []

        def lsem(name):
            s = sem(name)
            local.append(s)
            return s

        loaded = [lsem(f"loaded{i}") for i in range(8)]
        stored = lsem("stored")
        act_step, dve_step, pool_step = lsem("act_step"), lsem("dve_step"), lsem("pool_step")
        mm_a, mm_b, mm_c, mm_d, mm_e = (lsem(f"mm_{x}") for x in "abcde")
        dv_a, dv_b, dv_c, dv_d, dv_e, dv_f = (lsem(f"dv_{x}") for x in "abcdef")
        ac_a, ac_b, ac_c, ac_d, ac_e = (lsem(f"ac_{x}") for x in "abcde")
        po_a, po_b = lsem("po_a"), lsem("po_b")
        ada_in = [lsem("ada_in0"), lsem("ada_in1")]
        ada_used, ada_sums, ada_ps = lsem("ada_used"), lsem("ada_sums"), lsem("ada_ps")
        hs_ready, hcw_ready, conv0, rn, dec, lsig, dv_g = (lsem(x) for x in (
            "hs_ready", "hcw_ready", "conv0", "rn", "dec", "lsig", "dv_g"))
        ks_ps, vprime, vnew_ps, vnew_sb, upd_ps, o_half, o_done = (lsem(x) for x in (
            "ks_ps", "vprime", "vnew_ps", "vnew_sb", "upd_ps", "o_half", "o_done"))
        st = [lsem(f"st{i}") for i in range(4)]
        rows_in = lsem("rows_in")
        x0_in = [lsem(f"x0_in{t}") for t in range(LT)]
        arrive = sem("arrive")
        go = {x: sem(f"go_{x}") for x in ("pe", "act", "dve", "sp")}
        hw_landed, hw_free = [sem("hw_landed"), sem("hz_landed")], [sem("hw_free"), sem("hz_free")]
        ada_landed, ada_free = sem("ada_landed"), sem("ada_free")
        ring_landed = [sem(f"ring_landed{i}") for i in range(6)]
        ring_free = [sem(f"ring_free{i}") for i in range(6)]
        epoch = []
        for b in range(2):
            e = {n: sem(f"{n}{b}") for n in ("gathered_lat", "gathered_ctx", "xe_ps", "xe_sb", "gu_ps", "gate_sb", "hid_sb", "dn_ps",
                                             "ye_ch", "ye_ps", "ye_sb", "moe_dve",
                                             "ada_sum", "ada_ps", "ada_out")}
            epoch.append(e)
        ep_arrive = [sem(f"ep_arrive{b}") for b in range(2)]
        ep_go = [{x: sem(f"ep_go_{x}{b}") for x in ("pe", "act", "dve")} for b in range(2)]
        scattered = [sem("scattered_lat"), sem("scattered_ctx")]

        SCAN, PREV, SEEN, last_of, visited, n = [], {}, {}, {}, {}, 0
        for stp in range(LT):
            live = []
            for x in range(4 if stp < CT else 2):
                cc = (stp, LT - 1 - stp, LT + stp, T - 1 - stp)[x]
                PREV[n], SEEN[n] = last_of.get(x), visited.get(cc)
                last_of[x] = visited[cc] = n
                live.append((n, x, cc))
                n += 1
            SCAN.append((stp, live))
        NSCAN = n

        def XA(x):
            return ps[:, 2 * x * BANK:2 * x * BANK + 2 * P]

        def XB(x):
            return ps[:, (2 * x + 1) * BANK:(2 * x + 1) * BANK + 3 * P]

        def aff_tile(t):
            j, at = (t, 0) if t < 4 else (t - 4, 32) if t < LT else (t - LT, 64)
            return affs[:, j, at:at + EXPERTS]

        def YF(t):
            return area[:, 14080 + 2560 * t:16640 + 2560 * t].rearrange("p (c n) -> p c n", n=256)

        def table(i):
            return (ring[:, 0:4096], area[:, 0:4096])[i].rearrange("p (k c) -> p k c", k=LT)

        def sine_part(t):
            return ring[:, 4096 + 512 * t:4608 + 512 * t]

        def table_ctx(i):
            return ring[:, 8192 + 512 * i:8704 + 512 * i].rearrange("p (k c) -> p k c", k=CT)

        def nums(sems):
            n = sorted(s.num for s in sems)
            assert n == list(range(n[0], n[-1] + 1))
            return range(n[0], n[-1] + 1)

        def meet(eng, who):
            eng.drain().then_inc(arrive, 1)
            eng.wait_ge(go[who], 1)
            eng.sem_clear(go[who])

        def meet_pool(pool):
            pool.drain()
            pool.wait_ge(arrive, 4)
            pool.sem_clear(arrive)
            pool.sem_clear(nums(local))
            for g in go.values():
                pool.sem_inc(g, 1)

        class Steps:

            def __init__(self, eng, s):
                self.eng, self.s, self.n = eng, s, 0

            def reset(self):
                self.n = 0

            def __call__(self, ins):
                self.n += 1
                ins.then_inc(self.s, 1)
                self.eng.wait_ge(self.s, self.n)

        xres_t = xres.rearrange("(t p) d -> t p d", p=P)
        xnorm_t = xnorm.rearrange("(t p) d -> t p d", p=P)
        xs_t = x_sample[0].rearrange("(t p) d -> t p d", p=P)
        sd = state_delta[0].rearrange("l s h k v -> (l s h) k v")
        ns = new_state[0].rearrange("l s h k v -> (l s h) k v")
        wg = w_gate.rearrange("l e d f -> (l e) d f")
        wu = w_up.rearrange("l e d f -> (l e) d f")
        wd = w_down.rearrange("l e d f -> (l e) d f")
        yp_t = y_prompt[0].rearrange("(t p) d -> t p d", p=P)
        ys_t = y_sample[0].rearrange("(t p) d -> t p d", p=P)

        block = ctx.enter_context(nc.Block())

        @block.sync
        def _(sp):
            def load_ring(slot, e):
                w = (wg, wu, wg, wu, wd, wd)[slot]
                half = (0, 0, 1, 1, 0, 1)[slot]
                src = w[ds(e, 1), :, 512 * half:512 * half + 512].rearrange("a (k p) f -> p (a k) f", p=P)
                sp.dma_start(ring[:, 4096 * slot:4096 * slot + 4096].rearrange("p (k f) -> p k f", k=KT),
                             src).then_inc(ring_landed[slot], 16)

            def take(s):
                sp.wait_ge(s, 1)
                sp.sem_clear(s)

            def load_heads(l, col, part):
                for j in (range(3), range(3, 4))[part]:
                    sp.dma_start(hw[:, j], w_in[ds(l, 1), :, ds(col(j), P)].rearrange(
                        "a (k p) c -> p (a k) c", p=P)).then_inc(hw_landed[part], 16)

            def load_ada(buf, layer, m, s):
                sp.dma_start(buf, w_ada[ds(layer, 1), :, ds(m * P, P)].rearrange("a (k p) c -> p (a k) c", p=P)
                             ).then_inc(s, 16)

            sp.dma_start(crow[0:8, :], c[0].rearrange("(r p) -> r p", p=P)).then_inc(loaded[0], 16)
            sp.dma_start(crow[8:16, :], c_ctx.rearrange("(r p) -> r p", p=P)).then_inc(loaded[0], 16)
            sp.dma_start(cst[:], consts).then_inc(loaded[0], 16)
            for half in range(2):
                sp.dma_start(area[64 * half:64 * half + 64, 12288:12800], pos_col).then_inc(loaded[1], 16)
            for t in range(LT):
                sp.dma_start(x0[t], xs_t[t]).then_inc(x0_in[t], 16)
                for half in range(2):
                    r = 2 * t + half
                    sp.dma_start(area[64 * half:64 * half + 64, 8192 + 512 * t:8704 + 512 * t],
                                 pos_row[r:r + 1, :].to_broadcast([64, 512])).then_inc(x0_in[t], 16)
                if t % 2:
                    j = t // 2
                    sp.dma_start(ada0[j], w_ada[0, :, 512 * j:512 * j + 512].rearrange("(k p) c -> p k c", p=P)
                                 ).then_inc(loaded[4 + j], 16)
            sp.dma_start(xres[LAT:N, :], x_prompt[0]).then_inc(stored, 16)
            for i in range(DEPTH):
                for r0, src in ((R_ADA, b_ada), (R_N1, norm1_w), (R_N2, norm2_w), (R_DNN, dn_norm_w)):
                    n = src.shape[1] // P
                    sp.dma_start(rows[r0:r0 + n, i, :], src[i].rearrange("(r p) -> r p", p=P)).then_inc(rows_in, 16)
                for r0, src in ((R_DNC, dn_conv_w), (R_SCC, sc_conv_w)):
                    n = src.shape[1] * src.shape[2] // P
                    sp.dma_start(rows[r0:r0 + n, i, :], src[i].rearrange("j (r p) -> (j r) p", p=P)
                                 ).then_inc(rows_in, 16)
            for t in range(LT):
                sp.wait_ge(dv_a, 2 * (t + 1))
                sp.dma_start(xres_t[t], x0[t]).then_inc(stored, 16)
            sp.wait_ge(stored, 16 * (LT + 1))
            meet(sp, "sp")

            with sp.Fori(0, DEPTH) as l:
                for t in range(T):
                    if t >= 2:
                        sp.wait_ge(dv_b, t - 1)
                        sp.wait_ge(ac_a, t - 1)
                    sp.dma_start(xt[t % 2], xres_t[t]).then_inc(loaded[5 + t % 2], 16)
                    if t == 1:
                        for i, src in enumerate((dn_a_log, dn_dt_bias)):
                            sp.dma_start(alog[:, i, :], src[ds(l, 1), :, :].rearrange("a s h -> a (s h)")
                                         .to_broadcast([P, 8])).then_inc(loaded[0], 16)
                        sp.dma_start(w16[:], w_in[ds(l, 1), :, 4 * DNW:4 * DNW + 16].rearrange(
                            "a (k p) c -> p (a k) c", p=P)).then_inc(loaded[0], 16)
                        sp.dma_start(wr[:], w_router[ds(l, 1), :, :].rearrange("a (k p) c -> p (a k) c", p=P)
                                     ).then_inc(loaded[0], 16)
                        load_heads(l, lambda j: j * DNW, 0)
                        load_heads(l, lambda j: j * DNW, 1)
                sp.wait_ge(loaded[0], 64)
                meet(sp, "sp")

                meet(sp, "sp")

                def head(h, following):
                    for s in range(2):
                        sp.dma_start(chain[:, s, 0], sd[ds(l * 8 + h + 4 * s, 1)].rearrange("a k v -> (a k) v")
                                     ).then_inc(loaded[0], 16)
                    for i in range(8):
                        if i >= 2:
                            sp.wait_ge(ada_used, i - 1)
                        load_ada(ada_head[0][i % 2], l, h * 8 + (16 + i), ada_in[i % 2])
                    take(hw_free[0])
                    load_heads(l, following, 0)
                    sp.wait_ge(dv_f, 4 * CT)
                    for s in range(2):
                        sp.dma_start(ns[ds(l * 8 + h + 4 * s, 1)].rearrange("a k v -> (a k) v"), chain[:, 2 + s, 0]
                                     ).then_inc(stored, 16)
                    sp.wait_ge(stored, 32)
                    take(hw_free[1])
                    load_heads(l, following, 1)
                    meet(sp, "sp")

                def branch(t):
                    return lambda j: SC0 + (1, 2, 0, 3)[j] * SCW + t * P

                with sp.Fori(0, HEADS - 1) as h:
                    head(h, lambda j: h * P + (j * DNW + P))
                head(HEADS - 1, branch(0))

                for part in range(2):
                    take(hw_free[part])
                    load_heads(l, branch(1), part)
                for i in (1, 0):
                    if i == 0:
                        sp.wait_ge(mm_a, 8)
                        for j in range(2):
                            sp.dma_start(table_ctx(j), dft_ctx[j].rearrange("(k p) c -> p k c", p=P)
                                         ).then_inc(loaded[0], 16)
                    sp.dma_start(table(i), dft_lat[i].rearrange("(k p) c -> p k c", p=P)).then_inc(loaded[0], 16)
                sp.wait_ge(dv_a, 4)
                sp.dma_start(wo[0], w_out[ds(l, 1), :, 0:512].rearrange("a (k p) c -> p (a k) c", p=P)
                             ).then_inc(loaded[1], 16)
                sp.dma_start(wo_end, w_out[ds(l, 1), D - P:D, 512:1024].rearrange("a p c -> p (a c)")
                             ).then_inc(loaded[1], 16)
                sp.wait_ge(mm_b, 6)
                sp.dma_start(wo[1][:, 0:KT - 1], w_out[ds(l, 1), 0:D - P, 512:1024].rearrange(
                    "a (k p) c -> p (a k) c", p=P)).then_inc(loaded[1], 16)
                for part in range(2):
                    take(hw_free[part])
                sp.wait_ge(loaded[0], 16 * 4)
                sp.wait_ge(loaded[1], 16 * 3)
                meet(sp, "sp")

                for t in range(T + 1):
                    if t < T:
                        if t >= 2:
                            sp.wait_ge(st[t % 2], 16 * (t // 2))
                            sp.wait_ge(dv_b, t - 1)
                        sp.dma_start(xt[t % 2], xres_t[t]).then_inc(loaded[1 + t % 2], 16)
                    if t == 0:
                        for s in (0, 1, 5):
                            load_ring(s, l * EXPERTS)
                    if t >= 1:
                        sp.wait_ge(po_a, t)
                        sp.dma_start(xres_t[t - 1], xt[(t - 1) % 2]).then_inc(st[(t - 1) % 2], 16)
                        sp.wait_ge(dv_b, t)
                        sp.dma_start(xnorm_t[t - 1], xn[(t - 1) % 2]).then_inc(st[2 + (t - 1) % 2], 16)
                sp.wait_ge(mm_a, T)
                for s in (2, 3, 4):
                    load_ring(s, l * EXPERTS)
                for i in range(4):
                    sp.wait_ge(st[i], 16 * T // 2)
                meet(sp, "sp")

                load_ada(ada_moe[0][0], 1 - l, 0, ada_landed)
                with sp.Fori(1, EXPERTS) as e:
                    for s in range(6):
                        take(ring_free[s])
                        load_ring(s, l * EXPERTS + e)
                        if s == 3:
                            take(ada_free)
                            load_ada(ada_moe[0][0], 1 - l, e, ada_landed)
                take(ada_free)
                for s in range(6):
                    take(ring_free[s])
                meet(sp, "sp")

            sp.dma_start(g1b[:, 0, :], final_norm_w.rearrange("(a d) -> a d", a=1).to_broadcast([P, D])
                         ).then_inc(loaded[0], 16)
            for t in range(T + 1):
                if t < T:
                    if t >= 2:
                        sp.wait_ge(dv_b, t - 1)
                        sp.wait_ge(ac_a, t - 1)
                    sp.dma_start(xt[t % 2], xres_t[t]).then_inc(loaded[1 + t % 2], 16)
                if t >= 1:
                    sp.wait_ge(dv_b, t)
                    dst = ys_t[t - 1] if t - 1 < LT else yp_t[t - 1 - LT]
                    sp.dma_start(dst, xn[(t - 1) % 2]).then_inc(st[(t - 1) % 2], 16)
            for b in range(2):
                sp.wait_ge(st[b], 16 * T // 2)

        @block.tensor
        def _(pe):
            mm = nc.tensor.matmul

            def transposes(dst, src, n=P):
                return nc.tensor.transpose(dst, src, ident[0:src.shape[0], 0:src.shape[0]])

            pe.wait_ge(loaded[0], 48)
            transposes(ps[:, 0:16], crow).then_inc(mm_a, 1)
            pe.wait_ge(ac_a, 1)
            for j in range(4):
                pe.wait_ge(loaded[4 + j], 16)
                for k in range(KT):
                    last = mm(ps[0:2, (1 + j) * BANK:(2 + j) * BANK], condT[:, :, k], ada0[j][:, k, :],
                              start=(k == 0), stop=(k == KT - 1))
                last.then_inc(mm_b, 1)
            pe.wait_ge(rows_in, 16 * 6 * DEPTH)
            for i in range(DEPTH):
                last = transposes(ps[:, 5 * BANK + P * i:5 * BANK + P * i + ROWS], rows[0:ROWS, i, :])
            last.then_inc(mm_c, 1)
            pe.wait_ge(ac_b, 4)
            for m in range(16):
                last = transposes(ps[:, 6 * BANK + 2 * m:6 * BANK + 2 * m + 2], modrow[:, P * m:P * m + P])
            last.then_inc(mm_d, 1)
            meet(pe, "pe")

            with pe.Fori(0, DEPTH) as l:
                for t in range(T):
                    pe.wait_ge(dv_b, t + 1)
                    if t >= 2:
                        pe.wait_ge(dv_d, 4 * (t - 1))
                        pe.wait_ge(ac_b, 4 * (t - 1))
                    for k in range(KT):
                        at = (2 + 2 * (t % 2)) * BANK + P * k
                        last = transposes(ps[:, at:at + P], xn[t % 2][:, P * k:P * k + P])
                    last.then_inc(mm_d, 1)
                meet(pe, "pe")

                for t in range(T):
                    for k in range(KT):
                        last = mm(ps[:, 16 * t:16 * t + 16], hT[:, k, P * t:P * t + P], w16[:, k, :],
                                  start=(k == 0), stop=(k == KT - 1))
                last.then_inc(mm_a, 1)
                pe.wait_ge(dv_a, 1)
                mm(ps[:, BANK:BANK + 4 * T], triF, gs[:, Q_G, 0:4, :], start=True, stop=True)
                mm(ps[:, BANK + 4 * T:BANK + 8 * T], triB, gs[:, Q_G, 4:8, :], start=True, stop=True)
                mm(ps[:, 2 * BANK:2 * BANK + 8 * T], ones, gs[:, Q_G, :, :], start=True, stop=True).then_inc(mm_b, 1)
                meet(pe, "pe")

                def head_weights(part):
                    pe.wait_ge(hw_landed[part], (48, 16)[part])
                    pe.sem_clear(hw_landed[part])

                def project(j, dst, part=range(KT)):
                    for k in part:
                        for a, b in SPANS:
                            last = mm(dst[:, a:b], hw[:, j, k, :], hT[:, k, a:b], start=(k == 0), stop=(k == KT - 1))
                    return last

                with pe.Fori(0, HEADS) as h:
                    head_weights(0)
                    for j in range(3):
                        if j >= 2:
                            pe.wait_ge(dv_a, j - 1)
                        last = project(j, PAB[j % 2])
                        last.then_inc(mm_a, 1)
                    pe.wait_ge(mm_a, 3)
                    pe.sem_inc(hw_free[0], 1)
                    for j in range(2):
                        pe.wait_ge(ac_b, j + 1)
                        pe.wait_ge(dv_a, 2 + j)
                        for a, b in SPANS:
                            last = mm(PAB[1 - j][:, a:b], ones, spare[4 + j][:, a:b], start=True, stop=True)
                        last.then_inc(mm_b, 1)
                    pe.wait_ge(dv_b, 2)
                    pe.wait_ge(ac_d, 2)
                    for cc in range(T):
                        last = transposes(chunks(PAB[0])[:, cc], kq[:, cc, 0])
                    last.then_inc(mm_c, 1)
                    pe.wait_ge(ac_a, 3)
                    for cc in range(T):
                        last = transposes(chunks(PAB[1])[:, cc], chunks(spare[3])[:, cc])
                    last.then_inc(mm_c, 1)
                    for d in range(2):
                        if d == 0:
                            pe.wait_ge(ac_e, 1)
                        else:
                            pe.wait_ge(dv_c, 1)
                        pe.wait_ge(hs_ready, 1)
                        for cc in range(T):
                            mm(chunks(PAB[d])[:, cc], hs[:, Q_G, d, cc:cc + 1].to_broadcast([P, P]), (triF, triB)[d],
                               start=True, stop=False)
                            last = mm(chunks(PAB[d])[:, cc], identb[:], bigb[:, d], start=False, stop=True)
                        last.then_inc(mm_d, 1)
                    for g, (a, b) in enumerate(GROUPS):
                        pe.wait_ge(dv_d, (1, 2, 6)[g])
                        dst = (ps[:, 0:1024], ps[:, 3 * BANK:5 * BANK], ps[:, 0:1024])[g]
                        for cc in range(a, b):
                            last = mm(dst[:, 256 * (cc - a):256 * (cc - a) + 256], kq[:, cc, 0], kq[:, cc],
                                      start=True, stop=True)
                        last.then_inc(mm_e, 1)
                    pe.wait_ge(dv_d, 14)
                    for d in range(2):
                        for cc in range(T):
                            last = transposes(chunks(PAB[d])[:, cc], DD[:, d, cc])
                        last.then_inc(mm_e, 1)
                    for d in range(2):
                        pe.wait_ge(dv_e, d + 1)
                        for cc in range(T):
                            last = transposes(chunks(PAB[d])[:, cc], DD[:, d, cc])
                        last.then_inc(mm_e, 1)
                    for i, s in enumerate(LEVELS[1:]):
                        for d in range(2):
                            pe.wait_ge(ac_e, 2 + 4 * i + d)
                            for cc in range(T):
                                last = mm(chunks(PAB[d])[:, cc], LL[:, d, cc], U[:, d, cc], start=True, stop=True)
                            last.then_inc(mm_e, 1)
                        for d in range(2):
                            pe.wait_ge(ac_e, 4 + 4 * i + d)
                            for cc in range(T):
                                last = mm(chunks(PAB[d])[:, cc], DD[:, d, cc], PP[:, d, cc], start=True, stop=True)
                            last.then_inc(mm_e, 1)
                        if i < 5:
                            for d in range(2):
                                pe.wait_ge(dv_e, 2 + 2 * i + d + 1)
                                for cc in range(T):
                                    last = transposes(chunks(PAB[d])[:, cc], U[:, d, cc])
                                last.then_inc(mm_e, 1)
                    pe.wait_ge(ada_sums, 16)
                    for i in range(16):
                        last = mm(ps[:, 7 * BANK + i:7 * BANK + i + 1], ada_head[2][:, i, :], ones[:, 0:1],
                                  start=True, stop=True)
                    last.then_inc(ada_ps, 1)
                    head_weights(1)
                    pe.wait_ge(loaded[0], 32)
                    pe.wait_ge(dv_e, 14 + 1)
                    for step, live in SCAN:
                        for n, x, cc in live:
                            if step:
                                pe.wait_ge(dv_f, PREV[n] + 1)
                            mm(XA(x)[:, 0:P], kq[:, cc, 0], chain[:, x, 0], start=True, stop=True)
                            mm(XA(x)[:, P:2 * P], kq[:, cc, 1], chain[:, x, 0], start=True, stop=True
                               ).then_inc(ks_ps, 1)
                        for n, x, cc in live:
                            pe.wait_ge(vprime, n + 1)
                            if step:
                                pe.wait_ge(o_done, PREV[n] + 1)
                            mm(XB(x)[:, 2 * P:3 * P], U[:, x % 2, cc], chain[:, x, 1], start=True, stop=True
                               ).then_inc(vnew_ps, 1)
                        for n, x, cc in live:
                            pe.wait_ge(vnew_sb, 2 * n + 2)
                            mm(XB(x)[:, P:2 * P], ktok[:, cc], chain[:, x, 3], start=True, stop=True)
                            mm(XB(x)[:, 0:P], QK[:, x % 2, cc], chain[:, x, 2], start=True, stop=True
                               ).then_inc(upd_ps, 1)
                            if step >= CT:
                                k = 2 * (step - CT) + x
                                if k == 0:
                                    pe.wait_ge(o_done, 4 * CT)
                                if k < KT:
                                    last = project(3, PZ, [k])
                                if k == KT - 1:
                                    last.then_inc(mm_a, 1)
                    pe.wait_ge(mm_a, 4)
                    pe.sem_inc(hw_free[1], 1)
                    pe.wait_ge(dv_c, 2)
                    for cc in range(T):
                        last = transposes(chunks(PAB[0])[:, cc], oo[:, cc])
                    last.then_inc(mm_c, 1)
                    meet(pe, "pe")

                for t in range(2):
                    head_weights(0)
                    head_weights(1)
                    for j in range(4):
                        n = 4 * t + j
                        if n == 2:
                            pe.wait_ge(ac_a, 1)
                        if n == 3:
                            pe.wait_ge(dv_a, 1)
                        if n == 4:
                            pe.wait_ge(dv_a, 2)
                        if n == 5:
                            pe.wait_ge(ac_a, 2)
                        if n == 6:
                            pe.wait_ge(ac_a, 3)
                        if n == 7:
                            pe.wait_ge(dv_a, 3)
                        last = project(j, PAB[j % 2])
                        last.then_inc(mm_a, 1)
                    pe.wait_ge(mm_a, 4 * t + 4)
                    for part in range(2):
                        pe.sem_inc(hw_free[part], 1)
                pe.wait_ge(ac_a, 4)
                pe.wait_ge(dv_a, 4)
                for t in range(2):
                    for g, (a, b) in enumerate(GROUPS):
                        n = 3 * t + g
                        if n >= 2:
                            pe.wait_ge(ac_b, n - 1)
                        dst = ps[:, 2 * BANK * (n % 2):2 * BANK * (n % 2) + 2 * BANK]
                        for cc in range(a, b):
                            last = mm(dst[:, 256 * (cc - a):256 * (cc - a) + 256],
                                      spare[4 + t][:, P * cc:P * cc + P], chdft, start=True, stop=True)
                        last.then_inc(mm_b, 1)
                for i in range(2):
                    pe.wait_ge(dv_c, i + 1)
                    if i == 1:
                        pe.wait_ge(ac_d, 1)
                    for k in range(KT):
                        last = mm(ps[:, 6 * BANK + P * k:6 * BANK + P * k + P], ones, diag[i][:, k], start=True, stop=True)
                    last.then_inc(mm_d, 1)
                pe.wait_ge(loaded[0], 16 * 4)
                pe.wait_ge(ac_b, 6)
                for t in range(2):
                    Y, (cosb, sinb, rest) = YF(t), ((4, 5, 3), (0, 1, 2))[t]
                    for i, bank in ((1, sinb), (0, cosb)):
                        for m in range(LT):
                            last = mm(ps[:, bank * BANK:(bank + 1) * BANK], Y[:, m, P * i:P * i + P], table(i)[:, m, :],
                                      start=(m == 0), stop=(m == LT - 1))
                        last.then_inc(mm_c, 1)
                    at = rest * BANK
                    for m in range(LT):
                        mm(ps[:, at + CTX:at + CTX + 1], Y[:, m, 0:P], middle_col, start=(m == 0), stop=(m == LT - 1))
                    for i in range(2):
                        for m in range(CT):
                            last = mm(ps[:, at:at + CTX], Y[:, LT + m, P * i:P * i + P], table_ctx(i)[:, m, :],
                                      start=(i == 0 and m == 0), stop=(i == 1 and m == CT - 1))
                    last.then_inc(mm_c, 1)
                meet(pe, "pe")

                yT3 = yT.rearrange("p (k n) -> p k n", k=KT)
                for i in range(T + 2):
                    if i < T:
                        if i >= 2:
                            pe.wait_ge(dv_a, i - 1)
                        for half in range(2):
                            for k in range(KT):
                                at = (2 * (i % 2) + half) * BANK
                                w = wo_end if (half, k) == (1, KT - 1) else wo[half][:, k, :]
                                last = mm(ps[:, at:at + 512], yT3[:, k, P * i:P * i + P], w,
                                          start=(k == 0), stop=(k == KT - 1))
                        last.then_inc(mm_a, 1)
                    if 1 <= i <= T:
                        u = i - 1
                        pe.wait_ge(dv_b, u + 1)
                        if u >= 1:
                            pe.wait_ge(dv_d, 4 * u)
                            pe.wait_ge(ac_b, 4 * u)
                        for k in range(KT):
                            last = transposes(ps[:, 4 * BANK + P * k:4 * BANK + P * k + P],
                                              xn[u % 2][:, P * k:P * k + P])
                        last.then_inc(mm_b, 1)
                    if i >= 2:
                        u = i - 2
                        pe.wait_ge(dv_d, 4 * u + 4)
                        pe.wait_ge(ac_b, 4 * u + 4)
                        if u >= 1:
                            pe.wait_ge(ac_e, u)
                        for k in range(KT):
                            last = mm(ps[:, 6 * BANK:6 * BANK + EXPERTS], h2T[u % 2][:, k, :], wr[:, k, :],
                                      start=(k == 0), stop=(k == KT - 1))
                        last.then_inc(mm_c, 1)
                pe.wait_ge(dv_c, T)
                for j in range(4):
                    last = transposes(ps[0:LISTS, 7 * BANK + P * j:7 * BANK + P * j + P], affs[:, j])
                last.then_inc(mm_d, 1)
                pe.wait_ge(dv_e, 1)
                for i, src in enumerate((tv, tf)):
                    last = transposes(ps[:, LISTS * i:LISTS * i + LISTS], src)
                last.then_inc(mm_e, 1)
                meet(pe, "pe")

                def gather_T(b):
                    E = epoch[b]
                    pe.wait_ge(E["gathered_lat"], 16)
                    pe.wait_ge(E["gathered_ctx"], 16)
                    for k in range(KT):
                        transposes(ps[:, P * k:P * k + P], xeL[b][:, P * k:P * k + P])
                    for k in range(KT):
                        last = transposes(ps[:, 2 * BANK + CAPC * k:2 * BANK + CAPC * k + CAPC],
                                          xeC[b][:, P * k:P * k + P])
                    last.then_inc(E["xe_ps"], 1)

                def slot(i):
                    return ring[:, 4096 * i:4096 * i + 4096].rearrange("p (k f) -> p k f", k=KT)

                def arrived(i):
                    pe.wait_ge(ring_landed[i], 16)
                    pe.sem_clear(ring_landed[i])

                gather_T(0)
                with pe.Fori(0, EXPERTS // 2) as i:
                    for b in range(2):
                        E = epoch[b]
                        pe.wait_ge(E["xe_sb"], 10)
                        for m in range(KT):
                            half = m // 4
                            if m % 4 == 0:
                                arrived(2 * half)
                                arrived(2 * half + 1)
                            if m >= 2:
                                pe.wait_ge(E["hid_sb"], m - 1)
                            for i in range(2):
                                at = (4 + m % 2) * BANK + CAP * i
                                for k in range(KT):
                                    last = mm(ps[:, at:at + CAP], slot(2 * half + i)[:, k, P * (m % 4):P * (m % 4) + P],
                                              xeT[b][:, k, :], start=(k == 0), stop=(k == KT - 1))
                            last.then_inc(E["gu_ps"], 1)
                            if m == 0:
                                pe.wait_ge(epoch[1 - b]["ye_sb"], 2)
                                pe.wait_ge(epoch[1 - b]["ada_out"], 1)
                                pe.sem_inc(ep_arrive[1 - b], 1)
                            if m % 4 == 3:
                                pe.wait_ge(E["gu_ps"], m + 1)
                                pe.sem_inc(ring_free[2 * half], 1)
                                pe.sem_inc(ring_free[2 * half + 1], 1)
                        pe.wait_ge(ep_go[1 - b]["pe"], 1)
                        pe.sem_clear(ep_go[1 - b]["pe"])
                        gather_T(1 - b)
                        pe.wait_ge(E["hid_sb"], KT)

                        def back(m):
                            pe.wait_ge(E["ye_ch"], 2 * m + 2)
                            if m == 0:
                                pe.wait_ge(epoch[1 - b]["xe_sb"], 10)
                            transposes(ps[:, P * m:P * m + P], yeT[:, m, 0:CAPL])
                            return transposes(ps[0:CAPC, 2 * BANK + P * m:2 * BANK + P * m + P], yeT[:, m, CAPL:CAP])

                        for m in range(KT):
                            half = m // 4
                            if m % 4 == 0:
                                arrived(4 + half)
                            if m >= 2:
                                pe.wait_ge(E["ye_ch"], 2 * (m - 1))
                            at = (6 + m % 2) * BANK
                            for k in range(KT):
                                last = mm(ps[:, at:at + CAP], slot(4 + half)[:, k, P * (m % 4):P * (m % 4) + P],
                                          hid[:, k, :], start=(k == 0), stop=(k == KT - 1))
                            last.then_inc(E["dn_ps"], 1)
                            if m % 4 == 3:
                                pe.wait_ge(E["dn_ps"], m + 1)
                                pe.sem_inc(ring_free[4 + half], 1)
                            if m >= 1:
                                back(m - 1)
                        pe.wait_ge(E["ada_sum"], 2)
                        pe.wait_ge(E["ye_ch"], 2 * KT - 2)
                        for i in range(2):
                            last = mm(ps[:, 6 * BANK + i:6 * BANK + i + 1], ada_moe[2][:, 2 * b + i, :], ones[:, 0:1],
                                      start=True, stop=True)
                        last.then_inc(E["ada_ps"], 1)
                        back(KT - 1).then_inc(E["ye_ps"], 1)
                meet(pe, "pe")

        @block.scalar
        def _(act):
            f = nc.scalar.activation
            step = Steps(act, act_step)

            act.wait_ge(mm_a, 1)
            f(condT[:], ps[:, 0:16].rearrange("p (s k) -> p s k", s=2), ACT.Silu).then_inc(ac_a, 1)
            for j in range(4):
                act.wait_ge(mm_b, j + 1)
                f(modrow[:, 512 * j:512 * j + 512], ps[0:2, (1 + j) * BANK:(2 + j) * BANK], ACT.Copy).then_inc(ac_b, 1)
            meet(act, "act")

            with act.Fori(0, DEPTH) as l:
                for t in range(T + 1):
                    if t < T:
                        act.wait_ge(loaded[5 + t % 2], 16 * (t // 2 + 1))
                        if t >= 1:
                            act.wait_ge(ac_a, t)
                        f(h2T[0].rearrange("p k n -> p (k n)"), xt[t % 2], ACT.Square,
                          accum_out=small[:, t:t + 1]).then_inc(ac_a, 1)
                        act.wait_ge(dv_a, t + 1)
                        f(small[:, 10 + t:11 + t], small[:, 10 + t:11 + t], ACT.Sqrt).then_inc(ac_d, 1)
                    if t >= 1:
                        u, s = t - 1, int(t - 1 >= LT)
                        act.wait_ge(mm_d, u + 1)
                        for k in range(4):
                            at = (2 + 2 * (u % 2)) * BANK + P * k
                            f(hT[:, k, P * u:P * u + P], ps[:, at:at + P], ACT.Identity, scale=A1[:, k, s:s + 1],
                              bias=mod[:, SH1 + k, s:s + 1]).then_inc(ac_b, 1)
                meet(act, "act")

                gate = ps[:, 0:16 * T].rearrange("p (t j) -> p j t", j=16)
                act.wait_ge(mm_a, 1)
                f(gs[:, Q_B], gate[:, 0:8], ACT.Exp, scale=-1.0).then_inc(ac_a, 1)
                f(alog[:, 0, :], alog[:, 0, :], ACT.Exp).then_inc(ac_a, 1)
                act.wait_ge(dv_b, 1)
                f(gs[:, Q_GC], gs[:, Q_GC], ACT.Exp, scale=-1.0).then_inc(ac_b, 1)
                act.wait_ge(dv_b, 2)
                f(gs[:, Q_GL], gs[:, Q_EG], ACT.Ln).then_inc(ac_b, 1)
                act.wait_ge(dv_c, 2)
                act.wait_ge(mm_b, 1)
                f(gs[:, Q_EG], gs[:, Q_GC], ACT.Exp).then_inc(ac_c, 1)
                f(gs[:, Q_END], gs[:, Q_END], ACT.Exp).then_inc(ac_c, 1)
                f(gs[:, Q_GL], ps[:, 2 * BANK:2 * BANK + 8 * T].rearrange("p (j t) -> p j t", t=T), ACT.Exp
                  ).then_inc(ac_c, 1)
                meet(act, "act")

                with act.Fori(0, HEADS) as h:
                    for j in range(4):
                        if j < 3:
                            act.wait_ge(mm_a, j + 1)
                            if j == 0:
                                act.wait_ge(hcw_ready, 1)
                            f(spare[j], PAB[j % 2], ACT.Copy, scale=hcw[:, 3 + j:4 + j]).then_inc(conv0, 1)
                        if j >= 1:
                            i = j - 1
                            act.wait_ge(dv_a, i + 1)
                            dst = (kq[:, :, 1], kq[:, :, 0], chunks(spare[3]))[i]
                            f(dst, chunks(spare[i]), ACT.Silu).then_inc(ac_a, 1)
                            if i < 2:
                                act.wait_ge(ac_a, i + 1)
                                f(chunks(spare[4 + i]), kq[:, :, 1 - i], ACT.Square).then_inc(ac_b, 1)
                    for i in range(2):
                        act.wait_ge(mm_b, i + 1)
                        f(spare[6 + i], PAB[1 - i], ACT.Ln, bias=eps_col).then_inc(ac_d, 1)
                    for i in range(2):
                        act.wait_ge(ac_d, i + 1)
                        f(spare[6 + i], spare[6 + i], ACT.Exp, scale=-0.5, bias=(qscale_col if i == 0 else 0.0)
                          ).then_inc(rn, 1)
                    act.wait_ge(mm_c, 1)
                    f(ktok, chunks(PAB[0]), ACT.Copy).then_inc(ac_e, 1)
                    for d in range(2):
                        act.wait_ge(dv_d, d + 1)
                        f(PP[:, d], PP[:, d], ACT.Exp).then_inc(dec, 1)
                    for d in range(2):
                        act.wait_ge(mm_e, 6 + d)
                        f(U[:, d], chunks(PAB[d]), ACT.Copy).then_inc(ac_e, 1)
                    for i in range(6):
                        for d in range(2):
                            act.wait_ge(mm_e, 7 + 6 * i + d + 1)
                            f(PP[:, d], chunks(PAB[d]), ACT.Copy).then_inc(ac_e, 1)
                        if i < 5:
                            for d in range(2):
                                act.wait_ge(mm_e, 7 + 6 * i + 4 + d + 1)
                                f(DD[:, d], chunks(PAB[d]), ACT.Copy).then_inc(ac_e, 1)
                    for stp, live in SCAN:
                        for n, x, cc in live:
                            act.wait_ge(vnew_ps, n + 1)
                            if stp:
                                act.wait_ge(upd_ps, PREV[n] + 1)
                            f(chain[:, x, 3], XB(x)[:, 2 * P:3 * P], ACT.Copy, scale=hs[:, Q_END, x % 2, cc:cc + 1]
                              ).then_inc(vnew_sb, 1)
                            f(chain[:, x, 2], XB(x)[:, 2 * P:3 * P], ACT.Copy).then_inc(vnew_sb, 1)
                    act.wait_ge(mm_a, 4)
                    f(zT, PZ, ACT.Silu).then_inc(ac_c, 1)
                    act.wait_ge(dv_b, 3)
                    f(small[:, 20:20 + T], small[:, 10:10 + T], ACT.Sqrt).then_inc(ac_b, 1)
                    meet(act, "act")

                for t in range(2):
                    act.wait_ge(mm_a, 4 * t + 1)
                    if t:
                        act.wait_ge(dv_a, 2)
                    f(spare[0], PAB[0], ACT.Copy).then_inc(ac_a, 1)
                    act.wait_ge(dv_a, 2 * t + 1)
                    f(spare[2], spare[1], ACT.Copy, scale=cols[:, R_SCC + 2 + t:R_SCC + 3 + t]).then_inc(ac_c, 1)
                    act.wait_ge(mm_a, 4 * t + 4)
                    f(spare[4 + t], PAB[1], ACT.Copy).then_inc(ac_a, 1)
                for n in range(6):
                    t, (a, b) = n // 3, GROUPS[n % 3]
                    act.wait_ge(mm_b, n + 1)
                    f(YF(t)[:, a:b], ps[:, 2 * BANK * (n % 2):2 * BANK * (n % 2) + 256 * (b - a)].rearrange(
                        "p (c n) -> p c n", n=256), ACT.Copy).then_inc(ac_b, 1)
                for i in range(2):
                    act.wait_ge(mm_d, i + 1)
                    f(g1b[:, i, :], ps[:, 6 * BANK:8 * BANK], ACT.Copy).then_inc(ac_d, 1)
                for t in range(2):
                    act.wait_ge(mm_c, 3 * t + 1)
                    f(sine_part(t), ps[:, (5, 1)[t] * BANK:(6, 2)[t] * BANK], ACT.Copy).then_inc(ac_e, 1)
                meet(act, "act")

                for i in range(T + 2):
                    if 1 <= i <= T:
                        u, s = i - 1, int(i - 1 >= LT)
                        act.wait_ge(mm_b, u + 1)
                        if u >= 2:
                            act.wait_ge(mm_c, u - 1)
                        for k in range(4):
                            f(h2T[u % 2][:, k, :], ps[:, 4 * BANK + P * k:4 * BANK + P * k + P], ACT.Identity,
                              scale=A2[:, k, s:s + 1], bias=mod[:, SH2 + k, s:s + 1]).then_inc(ac_b, 1)
                    if i < T:
                        act.wait_ge(po_a, i + 1)
                        if i >= 1:
                            act.wait_ge(ac_a, i)
                        f(square, xt[i % 2], ACT.Square, accum_out=small[:, i:i + 1]).then_inc(ac_a, 1)
                    if i >= 2:
                        u = i - 2
                        act.wait_ge(dv_g, u + 1)
                        f(aff_tile(u), ps[:, 6 * BANK:6 * BANK + EXPERTS], ACT.Exp, bias=small[:, 20 + u:21 + u],
                          accum_out=small[:, 30 + u:31 + u]).then_inc(ac_e, 1)
                    if i < T:
                        act.wait_ge(dv_f, i + 1)
                        f(small[:, 10 + i:11 + i], small[:, 10 + i:11 + i], ACT.Sqrt).then_inc(ac_c, 1)
                meet(act, "act")

                def modulate(b):
                    E = epoch[b]
                    act.wait_ge(E["xe_ps"], 1)
                    for k in range(4):
                        f(xeT[b][:, k, 0:CAPL], ps[:, P * k:P * k + P], ACT.Identity, scale=A2[:, k, 0:1],
                          bias=mod[:, SH2 + k, 0:1]).then_inc(E["xe_sb"], 1)

                modulate(0)
                with act.Fori(0, EXPERTS // 2):
                    for b in range(2):
                        E = epoch[b]
                        for m in range(KT):
                            act.wait_ge(E["gu_ps"], m + 1)
                            if m >= 2:
                                act.wait_ge(E["hid_sb"], m - 1)
                            f(sg[:, m % 2], ps[:, (4 + m % 2) * BANK:(4 + m % 2) * BANK + CAP], ACT.Silu
                              ).then_inc(E["gate_sb"], 1)
                        act.wait_ge(ep_go[1 - b]["act"], 1)
                        act.sem_clear(ep_go[1 - b]["act"])
                        modulate(1 - b)
                        for m in range(KT):
                            act.wait_ge(E["dn_ps"], m + 1)
                            at = (6 + m % 2) * BANK
                            f(yeT[:, m, 0:CAPL], ps[:, at:at + CAPL], ACT.Copy, scale=mod[:, G2 + m, 0:1]
                              ).then_inc(E["ye_ch"], 1)
                            f(yeT[:, m, CAPL:CAP], ps[:, at + CAPL:at + CAP], ACT.Copy, scale=mod[:, G2 + m, 1:2]
                              ).then_inc(E["ye_ch"], 1)
                        act.wait_ge(E["ye_ps"], 1)
                        f(yeC[b], ps[0:CAPC, 2 * BANK:4 * BANK], ACT.Copy, scale=cur[0:CAPC, b, 1:2]
                          ).then_inc(E["ye_sb"], 1)
                        act.drain().then_inc(ep_arrive[b], 1)
                meet(act, "act")

            for t in range(T):
                act.wait_ge(loaded[1 + t % 2], 16 * (t // 2 + 1))
                if t >= 1:
                    act.wait_ge(ac_a, t)
                f(h2T[0].rearrange("p k n -> p (k n)"), xt[t % 2], ACT.Square, accum_out=small[:, t:t + 1]
                  ).then_inc(ac_a, 1)
                act.wait_ge(dv_a, t + 1)
                f(small[:, 10 + t:11 + t], small[:, 10 + t:11 + t], ACT.Sqrt).then_inc(ac_d, 1)

        @block.vector
        def _(dve):
            v = nc.vector
            step = Steps(dve, dve_step)

            dve.wait_ge(loaded[0], 48)
            v.tensor_copy(identb[:], ident)
            v.tensor_copy(bigb[:].rearrange("p d n -> p (d n)"), big)
            v.memset(tw[:], 0.0)
            v.memset(ix[:], 0)
            dve.wait_ge(loaded[1], 32)
            for t in range(LT):
                dve.wait_ge(x0_in[t], 48)
                v.tensor_tensor(x0[t][:, 0:512], x0[t][:, 0:512], area[:, 8192 + 512 * t:8704 + 512 * t], ALU.add
                                ).then_inc(dv_a, 1)
                v.tensor_tensor(x0[t][:, 512:1024], x0[t][:, 512:1024], area[:, 12288:12800], ALU.add
                                ).then_inc(dv_a, 1)
            dve.wait_ge(mm_c, 1)
            v.tensor_copy(allcols[:], ps[:, 5 * BANK:5 * BANK + 2 * P].rearrange("p (l n) -> p l n", l=2)[:, :, 0:ROWS]
                          ).then_inc(dv_b, 1)
            dve.wait_ge(mm_d, 1)
            dve.wait_ge(dv_b, 1)
            v.tensor_tensor(mod[:, 0:16, :], ps[:, 6 * BANK:6 * BANK + 32].rearrange("p (m s) -> p m s", s=2),
                            spread(allcols[:, 0, 0:16], 2), ALU.add)
            meet(dve, "dve")

            with dve.Fori(0, DEPTH) as l:
                step.reset()
                step(v.tensor_copy(cols[:], allcols[:, ds(l, 1), :].rearrange("p a n -> p (a n)")))
                step(v.scalar_tensor_tensor(out=A1[:], in0=mod[:, SC1:SC1 + KT, :], scalar=1.0,
                                            in1=spread(cols[:, R_N1:R_N1 + KT], 2), op0=ALU.add, op1=ALU.mult))
                for t in range(T + 1):
                    if t < T:
                        dve.wait_ge(ac_a, t + 1)
                        step(v.tensor_scalar(small[:, 10 + t:11 + t], small[:, t:t + 1], 1.0 / D, EPS, ALU.mult, ALU.add))
                        v.reciprocal(small[:, 10 + t:11 + t], small[:, 10 + t:11 + t]).then_inc(dv_a, 1)
                        dve.wait_ge(ac_d, t + 1)
                        if t >= 2:
                            dve.wait_ge(mm_d, t - 1)
                        v.tensor_scalar(xn[t % 2], xt[t % 2], small[:, 10 + t:11 + t], None, ALU.mult).then_inc(dv_b, 1)
                    if t >= 1:
                        u, s = t - 1, int(t - 1 >= LT)
                        dve.wait_ge(mm_d, u + 1)
                        for k in range(4, KT):
                            at = (2 + 2 * (u % 2)) * BANK + P * k
                            v.tensor_scalar(hT[:, k, P * u:P * u + P], ps[:, at:at + P], A1[:, k, s:s + 1],
                                            mod[:, SH1 + k, s:s + 1], ALU.mult, ALU.add).then_inc(dv_d, 1)
                meet(dve, "dve")

                step.reset()
                gate = ps[:, 0:16 * T].rearrange("p (t j) -> p j t", j=16)
                dve.wait_ge(mm_a, 1)
                dve.wait_ge(ac_a, 1)
                X = gs[:, Q_G]
                step(v.tensor_tensor(X, gate[:, 8:16], spread(alog[:, 1, :], T), ALU.add))
                v.scalar_tensor_tensor(out=gs[:, Q_GC], in0=X, scalar=-1.0, in1=X, op0=ALU.mult, op1=ALU.max
                                       ).then_inc(dv_b, 1)
                dve.wait_ge(ac_b, 1)
                v.tensor_scalar(gs[:, Q_EG], gs[:, Q_GC], 1.0, None, ALU.add).then_inc(dv_b, 1)
                dve.wait_ge(dv_b, 2)
                step(v.tensor_scalar(gs[:, Q_NEG], gs[:, Q_EG], -1.0, None, ALU.add))
                step(v.tensor_tensor(gs[:, Q_NEG], gs[:, Q_GC], gs[:, Q_NEG], ALU.subtract))
                dve.wait_ge(ac_b, 2)
                step(v.tensor_tensor(gs[:, Q_GL], gs[:, Q_GL], gs[:, Q_NEG], ALU.add))
                step(v.scalar_tensor_tensor(out=X, in0=X, scalar=0.0, in1=gs[:, Q_GL], op0=ALU.max, op1=ALU.add))
                dve.wait_ge(ac_a, 2)
                v.scalar_tensor_tensor(out=X, in0=X, scalar=-1.0, in1=spread(alog[:, 0, :], T), op0=ALU.mult,
                                       op1=ALU.mult).then_inc(dv_a, 1)
                step(v.tensor_scalar(gs[:, Q_B], gs[:, Q_B], 1.0, None, ALU.add))
                step(v.reciprocal(gs[:, Q_B], gs[:, Q_B]))
                step(v.tensor_scalar(gs[:, Q_NB], gs[:, Q_B], -1.0, None, ALU.mult))
                dve.wait_ge(mm_b, 1)
                v.tensor_copy(gs[:, Q_GC], ps[:, BANK:BANK + 8 * T].rearrange("p (j t) -> p j t", t=T)
                              ).then_inc(dv_c, 1)
                dve.wait_ge(dv_c, 1)
                v.tensor_tensor(gs[:, Q_END], ps[:, 2 * BANK:2 * BANK + 8 * T].rearrange("p (j t) -> p j t", t=T),
                                gs[:, Q_GC], ALU.subtract).then_inc(dv_c, 1)
                dve.wait_ge(ac_c, 3)
                v.tensor_tensor(gs[:, Q_NEG], gs[:, Q_EG], gs[:, Q_NB], ALU.mult)
                meet(dve, "dve")

                with dve.Fori(0, HEADS) as h:
                    step.reset()
                    v.tensor_copy(hs[:].rearrange("p q d t -> p (q d) t"), gs[:].rearrange(
                        "p q (d h) t -> p (q d) (h t)", d=2)[:, :, ds(h * T, T)]).then_inc(hs_ready, 1)
                    v.tensor_copy(hcw[:, 0:9], cols[:, ds(h + R_DNC, 33)][:, 0:33:4]).then_inc(hcw_ready, 1)
                    dve.wait_ge(hcw_ready, 1)
                    for j in range(3):
                        dve.wait_ge(conv0, j + 1)
                        src, dst = PAB[j % 2], spare[j]
                        for lo, hi in SEGS:
                            ins = v.scalar_tensor_tensor(out=dst[:, lo + 1:hi], in0=src[:, lo:hi - 1],
                                                         scalar=hcw[:, j:j + 1], in1=dst[:, lo + 1:hi],
                                                         op0=ALU.mult, op1=ALU.add)
                        step(ins)
                        for lo, hi in SEGS:
                            ins = v.scalar_tensor_tensor(out=dst[:, lo:hi - 1], in0=src[:, lo + 1:hi],
                                                         scalar=hcw[:, 6 + j:7 + j], in1=dst[:, lo:hi - 1],
                                                         op0=ALU.mult, op1=ALU.add)
                        ins.then_inc(dv_a, 1)
                    for i in range(2):
                        dve.wait_ge(rn, i + 1)
                        v.tensor_tensor(kq[:, :, 1 - i], kq[:, :, 1 - i], chunks(spare[6 + i]), ALU.mult
                                        ).then_inc(dv_b, 1)
                    dve.wait_ge(mm_c, 2)
                    v.tensor_copy(vtok, chunks(PAB[1])).then_inc(dv_c, 1)
                    dve.wait_ge(dv_b, 2)
                    for d in range(2):
                        dve.wait_ge(mm_d, d + 1)
                        v.tensor_tensor(PP[:, d], chunks(PAB[d]), spread(hs[:, Q_GC, d], P), ALU.subtract
                                        ).then_inc(dv_d, 1)
                    for g, (a, b) in enumerate(GROUPS):
                        dve.wait_ge(mm_e, g + 1)
                        src = (ps[:, 0:1024], ps[:, 3 * BANK:5 * BANK], ps[:, 0:1024])[g]
                        src = src[:, 0:256 * (b - a)].rearrange("p (c j n) -> p c j n", j=2, n=P)
                        for d in range(2):
                            dve.wait_ge(dec, d + 1)
                            for i, dst in enumerate((DD, QK)):
                                v.tensor_tensor(dst[:, d, a:b], src[:, :, i], PP[:, d, a:b], ALU.mult
                                                ).then_inc(dv_d, 1)
                    for d in range(2):
                        dve.wait_ge(mm_e, 4 + d)
                        v.tensor_tensor(LL[:, d], chunks(PAB[d]), spread(hs[:, Q_NB, d], P), ALU.mult
                                        ).then_inc(lsig, 1)
                        step(v.tensor_copy(DD[:, d], over(ident, T)))
                        dve.wait_ge(lsig, d + 1)
                        v.copy_predicated(DD[:, d], over((lower, upper)[d][0], T), LL[:, d]).then_inc(dv_e, 1)
                    for i in range(6):
                        for d in range(2):
                            dve.wait_ge(mm_e, 7 + 6 * i + 2 + d + 1)
                            v.copy_predicated(U[:, d], over((upper, lower)[d][i + 1], T), chunks(PAB[d])
                                              ).then_inc(dv_e, 1)
                    dve.wait_ge(mm_e, 7 + 6 * 5 + 4)
                    dve.wait_ge(ada_ps, 1)
                    v.tensor_tensor(mod[:, ds(h * 8 + 16, 8), :], ps[:, 7 * BANK:7 * BANK + 16].rearrange(
                        "p (m s) -> p m s", s=2), spread(cols[:, ds(h * 8 + 16, 8)], 2), ALU.add)
                    v.memset(oo, 0.0)
                    v.memset(chain[:, 2:4, 0], 0.0).then_inc(dv_e, 1)
                    dve.wait_ge(dv_e, 15)
                    dve.wait_ge(po_b, 2)
                    for stp, live in SCAN:
                        for n, x, cc in live:
                            dve.wait_ge(ks_ps, n + 1)
                            v.scalar_tensor_tensor(out=chain[:, x, 1], in0=XA(x)[:, 0:P],
                                                   scalar=hs[:, Q_NEG, x % 2, cc:cc + 1], in1=LL[:, x % 2, cc],
                                                   op0=ALU.mult, op1=ALU.add).then_inc(vprime, 1)
                        for n, x, cc in live:
                            if SEEN[n] is not None:
                                dve.wait_ge(o_done, SEEN[n] + 1)
                            v.scalar_tensor_tensor(out=oo[:, cc], in0=XA(x)[:, P:2 * P],
                                                   scalar=hs[:, Q_EG, x % 2, cc:cc + 1], in1=oo[:, cc],
                                                   op0=ALU.mult, op1=ALU.add).then_inc(o_half, 1)
                        for n, x, cc in live:
                            dve.wait_ge(upd_ps, n + 1)
                            v.scalar_tensor_tensor(out=chain[:, x, 0], in0=chain[:, x, 0],
                                                   scalar=hs[:, Q_GL, x % 2, cc:cc + 1], in1=XB(x)[:, P:2 * P],
                                                   op0=ALU.mult, op1=ALU.add).then_inc(dv_f, 1)
                            dve.wait_ge(o_half, n + 1)
                            v.tensor_tensor(oo[:, cc], XB(x)[:, 0:P], oo[:, cc], ALU.add).then_inc(o_done, 1)
                    dve.wait_ge(o_done, NSCAN)
                    step(v.tensor_tensor(PP[:, 0], oo, oo, ALU.mult))
                    step(v.tensor_reduce(small[:, 0:T], PP[:, 0], AX.X, ALU.add))
                    step(v.tensor_scalar(small[:, 10:10 + T], small[:, 0:T], 1.0 / P, EPS, ALU.mult, ALU.add))
                    v.reciprocal(small[:, 10:10 + T], small[:, 10:10 + T]).then_inc(dv_b, 1)
                    dve.wait_ge(ac_b, 3)
                    v.tensor_tensor(oo, oo, spread(small[:, 20:20 + T], P), ALU.mult).then_inc(dv_c, 1)
                    dve.wait_ge(mm_c, 3)
                    dve.wait_ge(ac_c, 1)
                    v.scalar_tensor_tensor(out=yT[:, ds(h * N, N)], in0=PAB[0], scalar=cols[:, R_DNN:R_DNN + 1],
                                           in1=zT, op0=ALU.mult, op1=ALU.mult)
                    meet(dve, "dve")

                step.reset()
                v.scalar_tensor_tensor(out=A2[:], in0=mod[:, SC2:SC2 + KT, :], scalar=1.0,
                                       in1=spread(cols[:, R_N2:R_N2 + KT], 2), op0=ALU.add, op1=ALU.mult)
                for i in range(2):
                    v.tensor_tensor(diag[i], over(ident, KT), spread(mod[:, G1:G1 + KT, i], P), ALU.mult
                                    ).then_inc(dv_c, 1)
                for t in range(2):
                    dve.wait_ge(mm_a, 4 * t + 2)
                    dve.wait_ge(ac_a, 2 * t + 1)
                    v.tensor_tensor(spare[1], PAB[1], spare[0], ALU.mult).then_inc(dv_a, 1)
                    dve.wait_ge(dv_a, 2 * t + 1)
                    dve.wait_ge(ac_c, t + 1)
                    for tap, (di, si) in ((0, (1, 0)), (4, (0, 1))):
                        for lo, hi in SEGS:
                            ins = v.scalar_tensor_tensor(out=spare[2][:, lo + di:hi - si], in0=spare[1][:, lo + si:hi - di],
                                                         scalar=cols[:, R_SCC + tap + t:R_SCC + tap + t + 1],
                                                         in1=spare[2][:, lo + di:hi - si], op0=ALU.mult, op1=ALU.add)
                        step(ins)
                    dve.wait_ge(mm_a, 4 * t + 3)
                    v.tensor_tensor(yT[:, (4 + t) * N:(5 + t) * N], PAB[0], spare[2], ALU.mult).then_inc(dv_a, 1)
                    dve.wait_ge(dv_a, 2 * t + 2)
                for t in range(2):
                    cosine = ps[:, (4, 0)[t] * BANK:(5, 1)[t] * BANK]
                    out = yT[:, (6 + t) * N:(7 + t) * N]
                    dve.wait_ge(mm_c, 3 * t + 2)
                    dve.wait_ge(ac_e, t + 1)
                    v.tensor_tensor(out[:, 0:LAT // 2], cosine, sine_part(t), ALU.add)
                    v.tensor_tensor(out[:, LAT // 2 + 1:LAT][:, ::-1], cosine[:, 1:], sine_part(t)[:, 1:], ALU.subtract)
                    dve.wait_ge(mm_c, 3 * t + 3)
                    rest = ps[:, (3, 2)[t] * BANK:(4, 3)[t] * BANK]
                    v.tensor_copy(out[:, LAT // 2:LAT // 2 + 1], rest[:, CTX:CTX + 1])
                    v.tensor_copy(out[:, LAT:N], rest[:, 0:CTX])
                meet(dve, "dve")

                step.reset()
                step(v.memset(affs, -1.0))
                for at, first in ((0, 0), (32, LHALF), (64, LAT)):
                    v.memset(first_token[at:min(at + 32, LISTS)], float(first)).then_inc(lsig, 1)
                for i in range(T + 2):
                    b = i % 2
                    if i < T:
                        dve.wait_ge(mm_a, i + 1)
                        if i >= 2:
                            dve.wait_ge(st[2 + b], 16 * (i // 2))
                            dve.wait_ge(mm_b, i - 1)
                        v.tensor_tensor(xn[b], ps[:, 2 * b * BANK:2 * b * BANK + D], g1b[:, int(i >= LT), :], ALU.mult
                                        ).then_inc(dv_a, 1)
                    if 1 <= i <= T:
                        u, s = i - 1, int(i - 1 >= LT)
                        dve.wait_ge(mm_b, u + 1)
                        if u >= 2:
                            dve.wait_ge(mm_c, u - 1)
                        for k in range(4, KT):
                            v.tensor_scalar(h2T[u % 2][:, k, :], ps[:, 4 * BANK + P * k:4 * BANK + P * k + P],
                                            A2[:, k, s:s + 1], mod[:, SH2 + k, s:s + 1], ALU.mult, ALU.add
                                            ).then_inc(dv_d, 1)
                    if i >= 2:
                        u = i - 2
                        dve.wait_ge(mm_c, u + 1)
                        v.tensor_reduce(small[:, 20 + u:21 + u], ps[:, 6 * BANK:6 * BANK + EXPERTS], AX.X, ALU.max,
                                        negate=True).then_inc(dv_g, 1)
                    if i < T:
                        dve.wait_ge(ac_a, i + 1)
                        step(v.tensor_scalar(small[:, 10 + i:11 + i], small[:, i:i + 1], 1.0 / D, EPS, ALU.mult, ALU.add))
                        v.reciprocal(small[:, 10 + i:11 + i], small[:, 10 + i:11 + i]).then_inc(dv_f, 1)
                        dve.wait_ge(ac_c, i + 1)
                        v.tensor_scalar(xn[b], xt[b], small[:, 10 + i:11 + i], None, ALU.mult).then_inc(dv_b, 1)
                    if i >= 2:
                        u = i - 2
                        dve.wait_ge(ac_e, u + 1)
                        step(v.reciprocal(small[:, 40 + u:41 + u], small[:, 30 + u:31 + u]))
                        v.tensor_scalar(aff_tile(u), aff_tile(u), small[:, 40 + u:41 + u], None, ALU.mult
                                        ).then_inc(dv_c, 1)
                dve.wait_ge(mm_d, 1)
                step(v.tensor_copy(work, ps[0:LISTS, 7 * BANK:7 * BANK + LHALF]))
                for r in range(CAPL // 8):
                    q = slice(8 * r, 8 * r + 8)
                    step(v.max(out=tv[:, q], in_=work))
                    step(v.max_index(out=ti[:, q], in_max=tv[:, q], in_values=work))
                    if r < CAPL // 8 - 1:
                        step(v.match_replace(out=work, in_to_replace=tv[:, q], in_values=work, imm_value=-1.0))
                dve.wait_ge(lsig, 3)
                step(v.tensor_copy(tf, ti))
                step(v.tensor_scalar(tf, tf, first_token, None, ALU.add))
                for src in (tv, tf):
                    step(v.tensor_copy(tr[32:48], src[32:48, ::-1]))
                    step(v.tensor_copy(src[32:48], tr[32:48]))
                v.memset(merged, 0.0).then_inc(dv_e, 1)
                dve.wait_ge(mm_e, 1)
                step(v.tensor_copy(lists, ps[:, 0:2 * LISTS].rearrange("p (i e) -> p i e", i=2)))
                val, idx = lists[:, 0], lists[:, 1]
                step(v.tensor_tensor(in_first, val[:, 0:EXPERTS], val[:, 32:32 + EXPERTS], ALU.is_ge))
                step(v.tensor_copy(merged, idx[:, 32:32 + EXPERTS]))
                step(v.copy_predicated(merged, in_first.bitcast(I32), idx[:, 0:EXPERTS]))
                for j in (0, EXPERTS):
                    w = EXPERTS if j == 0 else 1
                    v.tensor_tensor(tw[:, 0, j:j + w], val[:, 0:w], val[:, 32:32 + w], ALU.max)
                    v.tensor_copy(ix[:, 0, j:j + w], merged[:, 0:w])
                    v.tensor_copy(tw[0:CAPC, 1, j:j + w], val[0:CAPC, 64:64 + w])
                    v.tensor_copy(ix[0:CAPC, 1, j:j + w], idx[0:CAPC, 64:64 + w])
                meet(dve, "dve")

                def modulate(b):
                    E = epoch[b]
                    dve.wait_ge(E["xe_ps"], 1)
                    for k in range(4, 8):
                        v.tensor_scalar(xeT[b][:, k, 0:CAPL], ps[:, P * k:P * k + P], A2[:, k, 0:1],
                                        mod[:, SH2 + k, 0:1], ALU.mult, ALU.add).then_inc(E["xe_sb"], 1)
                    v.tensor_tensor(xeT[b][:, :, CAPL:CAP], ps[:, 2 * BANK:2 * BANK + CAPC * KT].rearrange(
                        "p (k n) -> p k n", k=KT), spread(A2[:, :, 1], CAPC), ALU.mult).then_inc(E["moe_dve"], 1)
                    dve.wait_ge(E["moe_dve"], 1)
                    v.tensor_tensor(xeT[b][:, :, CAPL:CAP], xeT[b][:, :, CAPL:CAP],
                                    spread(mod[:, SH2:SH2 + KT, 1], CAPC), ALU.add).then_inc(E["xe_sb"], 2)

                modulate(0)
                with dve.Fori(0, EXPERTS // 2) as i:
                    for b in range(2):
                        E = epoch[b]
                        for m in range(KT):
                            dve.wait_ge(E["gate_sb"], m + 1)
                            at = (4 + m % 2) * BANK + CAP
                            v.tensor_tensor(hid[:, m, :], ps[:, at:at + CAP], sg[:, m % 2], ALU.mult
                                            ).then_inc(E["hid_sb"], 1)
                        dve.wait_ge(ep_go[1 - b]["dve"], 1)
                        dve.sem_clear(ep_go[1 - b]["dve"])
                        modulate(1 - b)
                        dve.wait_ge(E["ye_ps"], 1)
                        v.tensor_scalar(yeL[b], ps[:, 0:D], cur[:, b, 0:1], None, ALU.mult).then_inc(E["ye_sb"], 1)
                        dve.wait_ge(E["ada_ps"], 1)
                        v.tensor_tensor(mod[:, ds(i * 2 + b, 1), :].rearrange("p a s -> p (a s)"),
                                        ps[:, 6 * BANK:6 * BANK + 2],
                                        allcols[:, ds(1 - l, 1), ds(i * 2 + b, 1)].rearrange("p a m -> p (a m)")
                                        .to_broadcast([P, 2]), ALU.add).then_inc(E["ada_out"], 1)
                        dve.drain().then_inc(ep_arrive[b], 1)
                meet(dve, "dve")

            step.reset()
            dve.wait_ge(loaded[0], 16)
            for t in range(T):
                dve.wait_ge(ac_a, t + 1)
                step(v.tensor_scalar(small[:, 10 + t:11 + t], small[:, t:t + 1], 1.0 / D, EPS, ALU.mult, ALU.add))
                v.reciprocal(small[:, 10 + t:11 + t], small[:, 10 + t:11 + t]).then_inc(dv_a, 1)
                dve.wait_ge(ac_d, t + 1)
                if t >= 2:
                    dve.wait_ge(st[t % 2], 16 * (t // 2))
                v.scalar_tensor_tensor(out=xn[t % 2], in0=xt[t % 2], scalar=small[:, 10 + t:11 + t], in1=g1b[:, 0, :],
                                       op0=ALU.mult, op1=ALU.mult).then_inc(dv_b, 1)

        @block.gpsimd
        def _(pool):
            g = nc.gpsimd
            meet_pool(pool)

            def ada_tile(buf, prod, sums, at, done, done0, chain_sem, n0):
                n = n0

                def then(ins):
                    nonlocal n
                    n += 1
                    ins.then_inc(chain_sem, 1)
                    pool.wait_ge(chain_sem, n)

                for s in range(2):
                    then(g.tensor_tensor(prod, buf, spread(condT[:, s, :], P), ALU.mult))
                    then(g.tensor_tensor(prod[:, 0:4], prod[:, 0:4], prod[:, 4:8], ALU.add))
                    then(g.tensor_tensor(prod[:, 0:2], prod[:, 0:2], prod[:, 2:4], ALU.add))
                    g.tensor_tensor(sums[:, at + s, :], prod[:, 0], prod[:, 1], ALU.add).then_inc(done, 1)
                    pool.wait_ge(done, done0 + s + 1)
                return n
            with pool.Fori(0, DEPTH) as l:
                meet_pool(pool)
                meet_pool(pool)
                with pool.Fori(0, HEADS):
                    n = 0
                    for i in range(8):
                        pool.wait_ge(ada_in[i % 2], 16 * (i // 2 + 1))
                        n = ada_tile(ada_head[0][i % 2], ada_head[1], ada_head[2], 2 * i, ada_sums, 2 * i, pool_step, n)
                        pool.sem_inc(ada_used, 1)
                    pool.wait_ge(dv_c, 1)
                    pool.wait_ge(hs_ready, 1)
                    for d in range(2):
                        pool.wait_ge(mm_e, 38 + d)
                        g.tensor_tensor(LL[:, d], vtok, spread(hs[:, Q_B, d], P), ALU.mult).then_inc(po_b, 1)
                    meet_pool(pool)
                meet_pool(pool)
                for t in range(T):
                    pool.wait_ge(dv_a, t + 1)
                    pool.wait_ge(loaded[1 + t % 2], 16 * (t // 2 + 1))
                    g.tensor_tensor(xt[t % 2], xt[t % 2], xn[t % 2], ALU.add).then_inc(po_a, 1)
                meet_pool(pool)

                def gather(b, e):
                    E = epoch[b]
                    g.tensor_copy(curi[:, b, :], ix[:, :, ds(e, 1)].rearrange("p s a -> p (s a)")).then_inc(pool_step, 1)
                    g.tensor_copy(cur[:, b, :], tw[:, :, ds(e, 1)].rearrange("p s a -> p (s a)")).then_inc(pool_step, 1)
                    pool.wait_ge(pool_step, 2)
                    pool.sem_clear(pool_step)
                    for s, (dst, n) in enumerate(((xeL[b], CAPL), (xeC[b], CAPC))):
                        g.indirect_dma_start(out=dst, out_offset=None, in_=xnorm,
                                             in_offset=bass.IndirectOffsetOnAxis(ap=curi[0:n, b, s:s + 1], axis=0)
                                             ).then_inc(E[("gathered_lat", "gathered_ctx")[s]], 16)

                gather(0, 0)
                pool.sem_inc(epoch[1]["ye_sb"], 2)
                pool.sem_inc(epoch[1]["ada_out"], 1)
                pool.sem_inc(ep_arrive[1], 2)
                for s in ("gathered_lat", "gathered_ctx"):
                    pool.wait_ge(epoch[0][s], 16)
                with pool.Fori(0, EXPERTS // 2) as i:
                    for b in range(2):
                        E, O = epoch[b], epoch[1 - b]
                        pool.wait_ge(ep_arrive[1 - b], 3)
                        pool.sem_clear(ep_arrive[1 - b])
                        pool.dma_reset(nums([O["gathered_lat"], O["gathered_ctx"]]))
                        pool.sem_clear(nums(O.values()))
                        for x in ("pe", "act", "dve"):
                            pool.sem_inc(ep_go[1 - b][x], 1)
                        gather(1 - b, i * 2 + (b + 1))
                        pool.wait_ge(ada_landed, 16)
                        pool.sem_clear(ada_landed)
                        ada_tile(ada_moe[0][0], ada_moe[1], ada_moe[2], 2 * b, E["ada_sum"], 0, pool_step, 0)
                        pool.sem_clear(pool_step)
                        pool.sem_inc(ada_free, 1)
                        pool.wait_ge(E["ye_sb"], 2)
                        for s, (src, n) in enumerate(((yeL[b], CAPL), (yeC[b], CAPC))):
                            g.indirect_dma_start(out=xres, out_offset=bass.IndirectOffsetOnAxis(
                                ap=curi[0:n, b, s:s + 1], axis=0), in_=src, in_offset=None,
                                compute_op=ALU.add).then_inc(scattered[s], 16)
                        for s in scattered + [O["gathered_lat"], O["gathered_ctx"]]:
                            pool.wait_ge(s, 16)
                        pool.dma_reset(nums(scattered))
                        pool.sem_clear(nums(scattered))
                pool.wait_ge(ep_arrive[1], 2)
                pool.sem_clear(ep_arrive[1])
                pool.drain()
                pool.wait_ge(arrive, 4)
                pool.sem_clear(arrive)
                pool.sem_clear(nums(local))
                for E in epoch:
                    pool.dma_reset(nums([E["gathered_lat"], E["gathered_ctx"]]))
                    pool.sem_clear(nums(E.values()))
                for x in go.values():
                    pool.sem_inc(x, 1)


_INS = ["x_prompt", "x_sample", "state_delta", "c", "c_ctx", "w_ada", "b_ada", "norm1_w", "norm2_w", "w_in",
        "dn_conv_w", "dn_a_log", "dn_dt_bias", "dn_norm_w", "sc_conv_w", "w_out", "w_router", "w_gate", "w_up",
        "w_down", "final_norm_w"]
_OUTS = [(1, CTX, D), (1, LAT, D), (1, DEPTH, 2, HEADS, P, P)]


def _constants():
    import numpy as np

    i = np.arange(P)
    row, col = i[:, None], i[None, :]
    parts = [row == col, np.ones((P, P)), row <= col, row >= col]
    low = [(row // (2 * s) == col // (2 * s)) & (row // s % 2 == 1) & (col // s % 2 == 0) for s in LEVELS]
    parts += low + [m.T for m in low]
    parts += [-1e30 * (row > col), -1e30 * (row < col)]
    ang = 2 * np.pi * np.outer(i % 64, i % 64) / 64
    same = row // 64 == col // 64
    parts += [np.cos(ang) * same, np.sin(ang) * same]
    parts += [np.full((P, 1), EPS), np.full((P, 1), -0.5 * np.log(P)), (-1.0) ** row / np.sqrt(LAT * 64)]
    consts = np.concatenate([p.astype(np.float32) for p in parts], axis=1)

    def dft(n):
        ang = 2 * np.pi * (np.outer(np.arange(n), np.arange(n)) % n) / n
        return (np.stack([np.cos(ang), -np.sin(ang)]) / np.sqrt(n * 64)).astype(np.float32)

    quarter = D // 4
    omega = 10000.0 ** (-np.arange(quarter, dtype=np.float64) / quarter)

    def pos(n):
        a = np.arange(n)[:, None] * omega
        return np.concatenate([np.sin(a), np.cos(a)], axis=1).astype(np.float32)

    return {"consts": consts, "dft_lat": np.ascontiguousarray(dft(LAT)[:, :, 0:LAT // 2]), "dft_ctx": dft(CTX), "pos_row": pos(LAT // 64), "pos_col": pos(64)}


def kernel(**inputs):
    import numpy as _np
    import concourse.bacc as _bacc
    from concourse.bass_utils import run_bass_kernel_spmd as _run

    nc = _bacc.Bacc("TRN2", target_bir_lowering=False, num_devices=1)
    arrays, args = {}, []
    given = {name: _np.ascontiguousarray(inputs[name]) for name in _INS}
    given.update(_constants())
    for name, a in given.items():
        arrays[f"in_{name}_dram"] = a
        args.append(nc.dram_tensor(f"in_{name}_dram", a.shape, mybir.dt.from_np(a.dtype), kind="ExternalInput").ap())
    for i, shape in enumerate(_OUTS):
        args.append(nc.dram_tensor(f"out_{i}_dram", shape, F32, kind="ExternalOutput").ap())
    trunk(nc, *args)
    r = _run(nc, [arrays], core_ids=[0])
    return tuple(r.results[0][f"out_{i}_dram"] for i in range(len(_OUTS)))
```

```python
from contextlib import ExitStack

import concourse.bass as bass
from concourse import mybir

F32 = mybir.dt.float32
BF16 = mybir.dt.bfloat16
U32 = mybir.dt.uint32
I32 = mybir.dt.int32
ALU = mybir.AluOpType
ACT = mybir.ActivationFunctionType
AX = mybir.AxisListType
ds = bass.ds

P = 128
D = 1024
KT = D // P
DEPTH = 2
LAT, CTX = 1024, 256
LT, CT = LAT // P, CTX // P
T = LT + CT
N = T * P
HEADS = 4
DNW = HEADS * P
SCW = 256
SC0 = 3 * DNW + DNW + 4 * HEADS
EXPERTS = 16
CAPL, CAPC = 2 * LAT // EXPERTS, 2 * CTX // EXPERTS
CAP = CAPL + CAPC
LEVELS = [1, 2, 4, 8, 16, 32, 64]
EPS = 1e-6
BANK = 512
R_ADA, R_N1, R_N2, R_DNC, R_SCC, R_DNN = 0, 48, 56, 64, 100, 106
ROWS = 107
SH1, SC1, G1, SH2, SC2, G2 = 0, 8, 16, 24, 32, 40
Q_G, Q_NB, Q_B, Q_GC, Q_EG, Q_NEG, Q_END, Q_GL = range(8)
SPANS = [(0, 512), (512, 1024), (1024, 1280)]
GROUPS = [(0, 4), (4, 8), (8, 10)]
SEGS = [(0, LAT), (LAT, N)]
NCONST = 128 * (4 + 2 * len(LEVELS) + 2 + 2) + 3


def trunk(nc, x_prompt, x_sample, state_delta, c, c_ctx, w_ada, b_ada, norm1_w, norm2_w, w_in, dn_conv_w,
          dn_a_log, dn_dt_bias, dn_norm_w, sc_conv_w, w_out, w_router, w_gate, w_up, w_down, final_norm_w,
          consts, dft_lat, dft_ctx, pos_row, pos_col, row_select, y_prompt, y_sample, new_state):
    xres = nc.dram_tensor("xres", (N, D), F32, kind="Internal").ap()
    xnorm = nc.dram_tensor("xnorm", (N, D), F32, kind="Internal").ap()

    with ExitStack() as ctx:
        def sb(name, shape, dt=F32):
            return ctx.enter_context(nc.sbuf_tensor(name, shape, dt))

        def sem(name):
            return ctx.enter_context(nc.semaphore(name))

        ring = sb("ring", [P, 6 * 4096])
        hT = ring[:, 0:KT * N].rearrange("p (k n) -> p k n", k=KT)
        yT = ring[:, KT * N:2 * KT * N]
        hw = ring[:, 2 * KT * N:].rearrange("p (j k c) -> p j k c", j=4, k=KT)
        area = sb("area", [P, 19200])
        kq = area[:, 0:2560].rearrange("p (c j n) -> p c j n", j=2, n=P)
        ktok = area[:, 2560:3840].rearrange("p (c n) -> p c n", n=P)
        vtok = area[:, 3840:5120].rearrange("p (c n) -> p c n", n=P)
        zT = area[:, 5120:6400]

        def pair(at):
            return area[:, at:at + 2560].rearrange("p (d c n) -> p d c n", d=2, n=P)

        U, DD, LL, PP, QK = (pair(at) for at in range(6400, 19200, 2560))
        spare = [area[:, at:at + N] for at in range(6400, 19200, N)]
        oo = area[:, 8960:10240].rearrange("p (c n) -> p c n", n=P)
        chain = sb("chain", [P, 4, 4, P])
        cst = sb("cst", [P, NCONST])
        ident, ones, triF, triB = (cst[:, P * i:P * i + P] for i in range(4))
        lower = [cst[:, P * (4 + i):P * (5 + i)].bitcast(I32) for i in range(7)]
        upper = [cst[:, P * (11 + i):P * (12 + i)].bitcast(I32) for i in range(7)]
        big = cst[:, P * 18:P * 20]
        chdft = cst[:, P * 20:P * 22]
        eps_col = cst[:, P * 22:P * 22 + 1]
        qscale_col = cst[:, P * 22 + 1:P * 22 + 2]
        middle_col = cst[:, P * 22 + 2:P * 22 + 3]
        identb = sb("identb", [P, P], BF16)
        bigb = sb("bigb", [P, 2, P], BF16)
        condT = sb("condT", [P, 2, KT])
        rows = ring[:, 24320:24576].rearrange("p (l n) -> p l n", l=2)
        allcols = sb("allcols", [P, DEPTH, ROWS])
        cols = sb("cols", [P, ROWS])
        mod = sb("mod", [P, 48, 2])
        A1 = sb("A1", [P, KT, 2])
        A2 = sb("A2", [P, KT, 2])
        g1b = sb("g1b", [P, 2, D])
        crow = g1b[0:16, 0, 0:P]
        modrow = g1b[0:2].rearrange("p s d -> p (s d)")
        w16 = sb("w16", [P, KT, 16])
        wr = sb("wr", [P, KT, EXPERTS])
        alog = sb("alog", [P, 2, 8])
        def ada_buffers(region):
            cut = region.rearrange("p (i k c) -> p i k c", i=5, k=KT)
            return [cut[:, 0], cut[:, 1]], cut[:, 2], cut[:, 3:5].rearrange("p i k c -> p (i k) c")

        ada_head = ada_buffers(yT[:, 4 * N:8 * N])
        ada_moe = ada_buffers(area[:, 13632:18752])
        gs = sb("gs", [P, 8, 8, T])
        hs = sb("hs", [P, 8, 2, T])
        hcw = sb("hcw", [P, 16])
        small = sb("small", [P, 64])
        tw = sb("tw", [P, 2, 17])
        ix = sb("ix", [P, 2, 17], U32)
        cur = sb("cur", [P, 2, 2])
        curi = sb("curi", [P, 2, 2], U32)
        xt = [area[:, 1024 * i:1024 * i + 1024] for i in range(2)]
        xn = [area[:, 1024 * i:1024 * i + 1024] for i in (2, 3)]
        h2T = [area[:, 1024 * i:1024 * i + 1024].rearrange("p (k n) -> p k n", k=KT) for i in (4, 5)]
        row_pos, row_of_token = area[0:LAT // 64, 8704:9216], area[0:LAT // 64, 9216:9216 + LAT]
        ada0 = [ring[:, at:at + 4096].rearrange("p (k c) -> p k c", k=KT) for at in range(0, 16384, 4096)]
        xf = [area[:, 1024 * t:1024 * t + 1024] for t in range(T)]
        x0 = [area[:, 1024 * t:1024 * t + 1024] for t in range(LT)]
        wo = [area[:, at:at + 4096].rearrange("p (k c) -> p k c", k=KT) for at in (6144, 10240)]
        wo_end = ring[:, 9216:9728]
        LISTS, LHALF = 80, LAT // 2
        affs = area[:, 14336:14336 + 4 * LISTS].rearrange("p (j e) -> p j e", j=4)
        work = area[0:LISTS, 14848:14848 + LHALF]
        tv = area[0:LISTS, 15360:15360 + CAPL]
        ti = area[0:LISTS, 15488:15488 + CAPL].bitcast(U32)
        tf = area[0:LISTS, 15616:15616 + CAPL]
        tr = area[0:LISTS, 15744:15744 + CAPL]
        first_token = area[0:LISTS, 15872:15873]
        lists = area[:, 15904:15904 + 2 * LISTS].rearrange("p (i e) -> p i e", i=2)
        in_first = area[:, 16128:16128 + EXPERTS]
        merged = area[:, 16160:16160 + EXPERTS]
        square = area[:, 17664:18688]

        xeL = [area[:, 1024 * i:1024 * i + 1024] for i in range(2)]
        xeC = [area[0:CAPC, 1024 * i:1024 * i + 1024] for i in (2, 3)]
        xeT = [area[:, 4096 + 1280 * i:5376 + 1280 * i].rearrange("p (k n) -> p k n", k=KT) for i in range(2)]
        hid = area[:, 6656:7936].rearrange("p (k n) -> p k n", k=KT)
        yeT = area[:, 7936:9216].rearrange("p (k n) -> p k n", k=KT)
        yeL = [area[:, 9216 + 1024 * i:10240 + 1024 * i] for i in range(2)]
        yeC = [area[0:CAPC, 11264 + 1024 * i:12288 + 1024 * i] for i in range(2)]
        sg = area[:, 13312:13632].rearrange("p (b n) -> p b n", b=2)

        ps = ctx.enter_context(nc.psum_tensor("ps", [P, 8 * BANK], F32))
        PAB = [ps[:, 0:N], ps[:, 4 * BANK:4 * BANK + N]]
        FILL = [ps[:, 3 * BANK:4 * BANK], ps[:, 7 * BANK:8 * BANK]]
        diag = [area[:, at:at + 1024].rearrange("p (k n) -> p k n", k=KT) for at in (4096, 5120)]

        def chunks(ap):
            return ap.rearrange("p (c n) -> p c n", n=P)

        def spread(col, n):
            return col.unsqueeze(len(col.shape)).to_broadcast(list(col.shape) + [n])

        def over(mat, n):
            return mat.unsqueeze(1).to_broadcast([P, n, P])

        local = []

        def lsem(name):
            s = sem(name)
            local.append(s)
            return s

        stored = lsem("stored")
        dve_step, pool_step = lsem("dve_step"), lsem("pool_step")
        shared = [lsem(f"phase_count{i}") for i in range(28)]
        (consts_in, pos_in, cond_ps, cond_ready, ada0_ps, row_pos_ps, pos_added, vectors_ps,
         vectors_ready, mod_rows_ready, mod_cols_ps) = shared[0:11]
        ada0_in = shared[11:15]
        (gate_weights_in, xn_ready, x_squares, xnT_ps, hT_dve, hT_act, inv_ms, inv_rms) = shared[0:8]
        x_in = shared[8:10]
        (states_in, o_ms, o_rms, o_normed, oT_ps, conv_done, kv_ps, qk_squares, qk_norms_ps, qk_normed,
         vtok_ps, silu_done, qk_norms_log, qk_inv_norms, vtok_ready, decay_ps, decay_dve, decay_ready,
         inverse_ps, inverse_act, inverse_dve, l_ready, state_ready, vbeta_ready) = shared[0:24]
        (tables_in, w_out_in, branch_ps, channel_dft_ps, position_dft_ps, g1_ps, branch_act,
         channel_dft_sb, middle_tap, g1_ready, sine_ready, branch_dve, diag_ready) = shared[0:13]
        (mix_ps, x2T_ps, logits_ps, aff_rows_ps, lists_ps, mix_gated, x2_normed, aff_ready, h2_dve,
         h2_act, x2_squares, x2_inv_ms, x2_inv_rms, logits_exp, logits_max, mix_added, lists_ready,
         first_token_set) = shared[0:18]
        x2_in = shared[18:20]
        (norm_w_in, y_squares, y_inv_ms, y_inv_rms, y_ready) = shared[0:5]
        hs_ready, hcw_ready, conv0 = (lsem(x) for x in (
            "hs_ready", "hcw_ready", "conv0"))
        ada_in = [lsem("ada_in0"), lsem("ada_in1")]
        ada_used, ada_sums, ada_ps = lsem("ada_used"), lsem("ada_sums"), lsem("ada_ps")
        ks_ps, vprime, vnew_ps, vnew_sb, upd_ps, o_half, o_done = (lsem(x) for x in (
            "ks_ps", "vprime", "vnew_ps", "vnew_sb", "upd_ps", "o_half", "o_done"))
        gate_exp, gate_abs, gate_log, gate_dve, gate_sum_ps, gate_sums, gate_exps, o_sq, fill_ps = (lsem(x) for x in (
            "gate_exp", "gate_abs", "gate_log", "gate_dve", "gate_sum_ps", "gate_sums", "gate_exps", "o_sq", "fill_ps"))
        fill_out, z_out, ctx_zero = lsem("fill_out"), lsem("z_out"), lsem("ctx_zero")
        tile_in = [lsem(f"tile_in{t}") for t in range(T)]
        tile_out = [lsem(f"tile_out{i}") for i in range(4)]
        rows_in = lsem("rows_in")
        arrive = sem("arrive")
        go = {x: sem(f"go_{x}") for x in ("pe", "act", "dve", "sp")}
        hw_landed, hw_free = [sem("hw_landed"), sem("hz_landed")], [sem("hw_free"), sem("hz_free")]
        ada_landed, ada_free = sem("ada_landed"), sem("ada_free")
        ring_landed = [sem(f"ring_landed{i}") for i in range(6)]
        ring_free = [sem(f"ring_free{i}") for i in range(6)]
        epoch = []
        for b in range(2):
            e = {n: sem(f"{n}{b}") for n in (
                "gathered_lat", "gathered_ctx",
                "xe_ps", "xe_sb",
                "gu_ps", "gate_sb", "hid_sb",
                "dn_ps", "ye_ch", "ye_ps", "ye_sb",
                "moe_dve", "ada_sum", "ada_ps", "ada_out")}
            epoch.append(e)
        ep_arrive = [sem(f"ep_arrive{b}") for b in range(2)]
        ep_go = [{x: sem(f"ep_go_{x}{b}") for x in ("pe", "act", "dve")} for b in range(2)]
        scattered = [sem("scattered_lat"), sem("scattered_ctx")]

        SCAN, PREV, SEEN, last_of, visited, n = [], {}, {}, {}, {}, 0
        for stp in range(LT):
            live = []
            for x in range(4 if stp < CT else 2):
                cc = (stp, LT - 1 - stp, LT + stp, T - 1 - stp)[x]
                PREV[n], SEEN[n] = last_of.get(x), visited.get(cc)
                last_of[x] = visited[cc] = n
                live.append((n, x, cc))
                n += 1
            SCAN.append((stp, live))
        NSCAN = n

        def XA(x):
            return ps[:, 2 * x * BANK:2 * x * BANK + 2 * P]

        def XB(x):
            return ps[:, (2 * x + 1) * BANK:(2 * x + 1) * BANK + 3 * P]

        def aff_tile(t):
            j, at = (t, 0) if t < 4 else (t - 4, 32) if t < LT else (t - LT, 64)
            return affs[:, j, at:at + EXPERTS]

        def YF(t):
            return area[:, 14080 + 2560 * t:16640 + 2560 * t].rearrange("p (c n) -> p c n", n=256)

        def table(i):
            return (ring[:, 0:4096], area[:, 0:4096])[i].rearrange("p (k c) -> p k c", k=LT)

        def sine_part(t):
            return ring[:, 4096 + 512 * t:4608 + 512 * t]

        def table_ctx(i):
            return ring[:, 8192 + 512 * i:8704 + 512 * i].rearrange("p (k c) -> p k c", k=CT)

        def nums(sems):
            n = sorted(s.num for s in sems)
            assert n == list(range(n[0], n[-1] + 1))
            return range(n[0], n[-1] + 1)

        def meet(eng, who):
            eng.drain().then_inc(arrive, 1)
            eng.wait_ge(go[who], 1)
            eng.sem_clear(go[who])

        def meet_pool(pool):
            pool.drain()
            pool.wait_ge(arrive, 4)
            pool.sem_clear(arrive)
            pool.sem_clear(nums(local))
            for g in go.values():
                pool.sem_inc(g, 1)

        class Steps:

            def __init__(self, eng, s):
                self.eng, self.s, self.n = eng, s, 0

            def reset(self):
                self.n = 0

            def __call__(self, ins):
                self.n += 1
                ins.then_inc(self.s, 1)
                self.eng.wait_ge(self.s, self.n)

        xres_t = xres.rearrange("(t p) d -> t p d", p=P)
        xnorm_t = xnorm.rearrange("(t p) d -> t p d", p=P)
        xs_t = x_sample[0].rearrange("(t p) d -> t p d", p=P)
        sd = state_delta[0].rearrange("l s h k v -> (l s h) k v")
        ns = new_state[0].rearrange("l s h k v -> (l s h) k v")
        wg = w_gate.rearrange("l e d f -> (l e) d f")
        wu = w_up.rearrange("l e d f -> (l e) d f")
        wd = w_down.rearrange("l e d f -> (l e) d f")
        yp_t = y_prompt[0].rearrange("(t p) d -> t p d", p=P)
        ys_t = y_sample[0].rearrange("(t p) d -> t p d", p=P)

        gate = ps[:, 7 * BANK:7 * BANK + 16 * T].rearrange("p (t j) -> p j t", j=16)
        gate_cum = FILL[1][:, 256:256 + 2 * T].rearrange("p (d t) -> p d t", d=2)
        gate_total = FILL[1][:, 256 + 2 * T:256 + 4 * T].rearrange("p (d t) -> p d t", d=2)

        block = ctx.enter_context(nc.Block())

        @block.sync
        def _(sp):
            def load_ring(slot, e):
                w = (wg, wu, wg, wu, wd, wd)[slot]
                half = (0, 0, 1, 1, 0, 1)[slot]
                src = w[ds(e, 1), :, 512 * half:512 * half + 512].rearrange("a (k p) f -> p (a k) f", p=P)
                sp.dma_start(ring[:, 4096 * slot:4096 * slot + 4096].rearrange("p (k f) -> p k f", k=KT),
                             src).then_inc(ring_landed[slot], 16)

            def take(s):
                sp.wait_ge(s, 1)
                sp.sem_clear(s)

            def load_heads(l, col, part):
                for j in (range(3), range(3, 4))[part]:
                    sp.dma_start(hw[:, j], w_in[ds(l, 1), :, ds(col(j), P)].rearrange(
                        "a (k p) c -> p (a k) c", p=P)).then_inc(hw_landed[part], 16)

            def load_ada(buf, layer, m, s):
                sp.dma_start(buf, w_ada[ds(layer, 1), :, ds(m * P, P)].rearrange("a (k p) c -> p (a k) c", p=P)
                             ).then_inc(s, 16)

            sp.dma_start(crow[0:8, :], c[0].rearrange("(r p) -> r p", p=P)).then_inc(consts_in, 16)
            sp.dma_start(crow[8:16, :], c_ctx.rearrange("(r p) -> r p", p=P)).then_inc(consts_in, 16)
            sp.dma_start(cst[:], consts).then_inc(consts_in, 16)
            def load_ada0(j):
                sp.dma_start(ada0[j], w_ada[0, :, 512 * j:512 * j + 512].rearrange("(k p) c -> p k c", p=P)
                             ).then_inc(ada0_in[j], 16)

            load_ada0(0)
            for half in range(2):
                sp.dma_start(area[64 * half:64 * half + 64, 8192:8704], pos_col).then_inc(pos_in, 16)
            sp.dma_start(row_pos, pos_row).then_inc(pos_in, 16)
            sp.dma_start(row_of_token, row_select).then_inc(pos_in, 16)
            for t in range(LT):
                sp.dma_start(x0[t], xs_t[t]).then_inc(tile_in[t], 16)
                if t % 2 and t < 6:
                    load_ada0(t // 2 + 1)
            sp.dma_start(xres[LAT:N, :], x_prompt[0]).then_inc(stored, 16)
            for i in range(DEPTH):
                for r0, src in ((R_ADA, b_ada), (R_N1, norm1_w), (R_N2, norm2_w), (R_DNN, dn_norm_w)):
                    n = src.shape[1] // P
                    sp.dma_start(rows[r0:r0 + n, i, :], src[i].rearrange("(r p) -> r p", p=P)).then_inc(rows_in, 16)
                for r0, src in ((R_DNC, dn_conv_w), (R_SCC, sc_conv_w)):
                    n = src.shape[1] * src.shape[2] // P
                    sp.dma_start(rows[r0:r0 + n, i, :], src[i].rearrange("j (r p) -> (j r) p", p=P)
                                 ).then_inc(rows_in, 16)
            for t in range(LT):
                sp.wait_ge(pos_added, 2 * (t + 1))
                sp.dma_start(xres_t[t], x0[t]).then_inc(stored, 16)
            sp.wait_ge(stored, 16 * (LT + 1))
            meet(sp, "sp")

            with sp.Fori(0, DEPTH) as l:
                for t in range(T):
                    if t >= 2:
                        sp.wait_ge(xn_ready, t - 1)
                        sp.wait_ge(x_squares, t - 1)
                    sp.dma_start(xt[t % 2], xres_t[t]).then_inc(x_in[t % 2], 16)
                    if t == 1:
                        for i, src in enumerate((dn_a_log, dn_dt_bias)):
                            sp.dma_start(alog[:, i, :], src[ds(l, 1), :, :].rearrange("a s h -> a (s h)")
                                         .to_broadcast([P, 8])).then_inc(gate_weights_in, 16)
                        sp.dma_start(w16[:], w_in[ds(l, 1), :, 4 * DNW:4 * DNW + 16].rearrange(
                            "a (k p) c -> p (a k) c", p=P)).then_inc(gate_weights_in, 16)
                        sp.dma_start(wr[:], w_router[ds(l, 1), :, :].rearrange("a (k p) c -> p (a k) c", p=P)
                                     ).then_inc(gate_weights_in, 16)
                        load_heads(l, lambda j: j * DNW, 0)
                        load_heads(l, lambda j: j * DNW, 1)
                sp.wait_ge(gate_weights_in, 64)
                meet(sp, "sp")


                def head(h, following):
                    for s in range(2):
                        sp.dma_start(chain[:, s, 0], sd[ds(l * 8 + h + 4 * s, 1)].rearrange("a k v -> (a k) v")
                                     ).then_inc(states_in, 16)
                    for i in range(8):
                        if i >= 2:
                            sp.wait_ge(ada_used, i - 1)
                        load_ada(ada_head[0][i % 2], l, h * 8 + (16 + i), ada_in[i % 2])
                    take(hw_free[0])
                    load_heads(l, following, 0)
                    take(hw_free[1])
                    load_heads(l, following, 1)
                    sp.wait_ge(state_ready, 4 * CT)
                    for s in range(2):
                        sp.dma_start(ns[ds(l * 8 + h + 4 * s, 1)].rearrange("a k v -> (a k) v"), chain[:, 2 + s, 0]
                                     ).then_inc(stored, 16)
                    sp.wait_ge(stored, 32)
                    meet(sp, "sp")

                def branch(t):
                    return lambda j: SC0 + (1, 2, 0, 3)[j] * SCW + t * P

                with sp.Fori(0, HEADS - 1) as h:
                    head(h, lambda j: h * P + (j * DNW + P))
                head(HEADS - 1, branch(0))

                for part in range(2):
                    take(hw_free[part])
                    load_heads(l, branch(1), part)
                for i in (1, 0):
                    if i == 0:
                        sp.wait_ge(branch_ps, 7)
                        for j in range(2):
                            sp.dma_start(table_ctx(j), dft_ctx[j].rearrange("(k p) c -> p k c", p=P)
                                         ).then_inc(tables_in, 16)
                    sp.dma_start(table(i), dft_lat[i].rearrange("(k p) c -> p k c", p=P)).then_inc(tables_in, 16)
                sp.wait_ge(branch_dve, 4)
                sp.dma_start(wo[0], w_out[ds(l, 1), :, 0:512].rearrange("a (k p) c -> p (a k) c", p=P)
                             ).then_inc(w_out_in, 16)
                sp.dma_start(wo_end, w_out[ds(l, 1), D - P:D, 512:1024].rearrange("a p c -> p (a c)")
                             ).then_inc(w_out_in, 16)
                sp.wait_ge(channel_dft_ps, 6)
                sp.dma_start(wo[1][:, 0:KT - 1], w_out[ds(l, 1), 0:D - P, 512:1024].rearrange(
                    "a (k p) c -> p (a k) c", p=P)).then_inc(w_out_in, 16)
                for part in range(2):
                    take(hw_free[part])
                sp.wait_ge(tables_in, 16 * 4)
                sp.wait_ge(w_out_in, 16 * 3)
                meet(sp, "sp")

                for t in range(T + 1):
                    if t < T:
                        if t >= 2:
                            sp.wait_ge(tile_out[t % 2], 16 * (t // 2))
                            sp.wait_ge(x2_normed, t - 1)
                        sp.dma_start(xt[t % 2], xres_t[t]).then_inc(x2_in[t % 2], 16)
                    if t == 0:
                        for s in (0, 1, 5):
                            load_ring(s, l * EXPERTS)
                    if t >= 1:
                        sp.wait_ge(mix_added, t)
                        sp.dma_start(xres_t[t - 1], xt[(t - 1) % 2]).then_inc(tile_out[(t - 1) % 2], 16)
                        sp.wait_ge(x2_normed, t)
                        sp.dma_start(xnorm_t[t - 1], xn[(t - 1) % 2]).then_inc(tile_out[2 + (t - 1) % 2], 16)
                sp.wait_ge(mix_ps, T)
                for s in (2, 3, 4):
                    load_ring(s, l * EXPERTS)
                for i in range(4):
                    sp.wait_ge(tile_out[i], 16 * T // 2)
                meet(sp, "sp")

                load_ada(ada_moe[0][0], 1 - l, 0, ada_landed)
                with sp.Fori(1, EXPERTS) as e:
                    for s in range(6):
                        take(ring_free[s])
                        load_ring(s, l * EXPERTS + e)
                        if s == 3:
                            take(ada_free)
                            load_ada(ada_moe[0][0], 1 - l, e, ada_landed)
                take(ada_free)
                for s in range(6):
                    take(ring_free[s])
                meet(sp, "sp")

            sp.dma_start(g1b[:, 0, :], final_norm_w.rearrange("(a d) -> a d", a=1).to_broadcast([P, D])
                         ).then_inc(norm_w_in, 16)
            for t in range(T):
                sp.dma_start(xf[t], xres_t[t]).then_inc(tile_in[t], 16)
            for t in range(T):
                sp.wait_ge(y_ready, t + 1)
                sp.dma_start(ys_t[t] if t < LT else yp_t[t - LT], xf[t]).then_inc(stored, 16)
            sp.wait_ge(stored, 16 * T)

        @block.tensor
        def _(pe):
            mm = nc.tensor.matmul

            def transposes(dst, src, n=P):
                return nc.tensor.transpose(dst, src, ident[0:src.shape[0], 0:src.shape[0]])

            pe.wait_ge(consts_in, 48)
            transposes(ps[:, 0:16], crow).then_inc(cond_ps, 1)
            pe.wait_ge(cond_ready, 1)
            for j in range(4):
                pe.wait_ge(ada0_in[j], 16)
                for k in range(KT):
                    last = mm(ps[0:2, (1 + j) * BANK:(2 + j) * BANK], condT[:, :, k], ada0[j][:, k, :],
                              start=(k == 0), stop=(k == KT - 1))
                last.then_inc(ada0_ps, 1)
                pe.wait_ge(pos_in, 64)
                for t in (2 * j, 2 * j + 1):
                    if t >= 2:
                        pe.wait_ge(pos_added, 2 * t - 3)
                    mm(ps[:, (5, 7)[t % 2] * BANK:(6, 8)[t % 2] * BANK], row_of_token[:, P * t:P * t + P], row_pos,
                       start=True, stop=True).then_inc(row_pos_ps, 1)
            pe.wait_ge(rows_in, 16 * 6 * DEPTH)
            pe.wait_ge(pos_added, 2 * LT - 3)
            for i in range(DEPTH):
                last = transposes(ps[:, 5 * BANK + P * i:5 * BANK + P * i + ROWS], rows[0:ROWS, i, :])
            last.then_inc(vectors_ps, 1)
            pe.wait_ge(mod_rows_ready, 4)
            for m in range(16):
                last = transposes(ps[:, 6 * BANK + 2 * m:6 * BANK + 2 * m + 2], modrow[:, P * m:P * m + P])
            last.then_inc(mod_cols_ps, 1)
            meet(pe, "pe")

            def head_weights(part):
                pe.wait_ge(hw_landed[part], (48, 16)[part])
                pe.sem_clear(hw_landed[part])

            def project(j, dst, part=range(KT)):
                for k in part:
                    for a, b in SPANS:
                        last = mm(dst[:, a:b], hw[:, j, k, :], hT[:, k, a:b], start=(k == 0), stop=(k == KT - 1))
                return last

            with pe.Fori(0, DEPTH) as l:
                for t in range(T + 1):
                    if t < T:
                        pe.wait_ge(xn_ready, t + 1)
                        if t >= 2:
                            pe.wait_ge(hT_dve, 4 * (t - 1))
                            pe.wait_ge(hT_act, 4 * (t - 1))
                        for k in range(KT):
                            at = (2 + 2 * (t % 2)) * BANK + P * k
                            last = transposes(ps[:, at:at + P], xn[t % 2][:, P * k:P * k + P])
                        last.then_inc(xnT_ps, 1)
                    if t >= 1:
                        u = t - 1
                        if u == 0:
                            pe.wait_ge(gate_weights_in, 64)
                        pe.wait_ge(hT_dve, 4 * t)
                        pe.wait_ge(hT_act, 4 * t)
                        for k in range(KT):
                            mm(ps[:, 7 * BANK + 16 * u:7 * BANK + 16 * u + 16], hT[:, k, P * u:P * u + P], w16[:, k, :],
                               start=(k == 0), stop=(k == KT - 1))
                head_weights(0)
                project(0, PAB[1])
                meet(pe, "pe")

                with pe.Fori(0, HEADS) as h:
                    for j in (1, 2):
                        if j == 2:
                            pe.wait_ge(conv_done, 1)
                        last = project(j, PAB[1 - j % 2])
                        last.then_inc(kv_ps, 1)
                        if j == 1:
                            pe.wait_ge(hs_ready, 1)
                            mm(gate_cum[:, 0], triF, hs[:, Q_G, 0], start=True, stop=True)
                            mm(gate_cum[:, 1], triB, hs[:, Q_G, 1], start=True, stop=True)
                            mm(gate_total, ones, hs[:, Q_G], start=True, stop=True).then_inc(gate_sum_ps, 1)
                    pe.wait_ge(kv_ps, 2)
                    pe.sem_inc(hw_free[0], 1)
                    head_weights(1)
                    pe.wait_ge(gate_exps, 3)
                    z_steps = [(k, half) for k in range(KT) for half in range(2)]

                    def z_fill(n):
                        for _ in range(min(n, len(z_steps))):
                            k, half = z_steps.pop(0)
                            a, b = SPANS[half]
                            last = mm(FILL[half], hw[:, 3, k, :], hT[:, k, a:b], start=(k == 0), stop=(k == KT - 1))
                        if not z_steps:
                            last.then_inc(fill_ps, 1)

                    for j in range(2):
                        if j == 1:
                            z_fill(3)
                        pe.wait_ge(qk_squares, j + 1)
                        pe.wait_ge(conv_done, 2 + j)
                        for a, b in SPANS:
                            last = mm(PAB[j][:, a:b], ones, spare[4 + j][:, a:b], start=True, stop=True)
                        last.then_inc(qk_norms_ps, 1)
                    pe.wait_ge(silu_done, 3)
                    pe.wait_ge(qk_norms_log, 1)
                    for cc in range(T):
                        last = transposes(chunks(PAB[0])[:, cc], chunks(spare[3])[:, cc])
                    last.then_inc(vtok_ps, 1)
                    for d in range(2):
                        if d == 0:
                            pe.wait_ge(qk_norms_log, 2)
                        else:
                            z_fill(1)
                            pe.wait_ge(vtok_ready, 1)
                        for cc in range(T):
                            mm(chunks(PAB[1 - d])[:, cc], hs[:, Q_G, d, cc:cc + 1].to_broadcast([P, P]), (triF, triB)[d],
                               start=True, stop=False)
                            last = mm(chunks(PAB[1 - d])[:, cc], identb[:], bigb[:, d], start=False, stop=True)
                        last.then_inc(decay_ps, 1)
                    z_fill(5)
                    pe.wait_ge(qk_normed, 2)
                    for g, (a, b) in enumerate(GROUPS):
                        pe.wait_ge(decay_dve, (1, 2, 6)[g])
                        dst = PAB[(1, 0, 1)[g]][:, 0:1024]
                        for cc in range(a, b):
                            last = mm(dst[:, 256 * (cc - a):256 * (cc - a) + 256], kq[:, cc, 0], kq[:, cc],
                                      start=True, stop=True)
                        last.then_inc(inverse_ps, 1)
                    z_fill(4)
                    pe.wait_ge(decay_dve, 14)
                    for d in range(2):
                        for cc in range(T):
                            last = transposes(chunks(PAB[d])[:, cc], DD[:, d, cc])
                        last.then_inc(inverse_ps, 1)
                    z_fill(len(z_steps))
                    for d in range(2):
                        pe.wait_ge(inverse_dve, d + 1)
                        for cc in range(T):
                            last = transposes(chunks(PAB[d])[:, cc], DD[:, d, cc])
                        last.then_inc(inverse_ps, 1)
                    for i, s in enumerate(LEVELS[1:]):
                        for d in range(2):
                            pe.wait_ge(inverse_act, 1 + 4 * i + d)
                            for cc in range(T):
                                last = mm(chunks(PAB[d])[:, cc], LL[:, d, cc], U[:, d, cc], start=True, stop=True)
                            last.then_inc(inverse_ps, 1)
                        for d in range(2):
                            pe.wait_ge(inverse_act, 3 + 4 * i + d)
                            for cc in range(T):
                                last = mm(chunks(PAB[d])[:, cc], DD[:, d, cc], PP[:, d, cc], start=True, stop=True)
                            last.then_inc(inverse_ps, 1)
                        if i < 5:
                            if i < 3:
                                if i == 0:
                                    pe.wait_ge(z_out, 2)
                                if i == 2:
                                    pe.wait_ge(fill_out, 1)
                                for cc in range(4 * i, min(4 * i + 4, T)):
                                    last = transposes(chunks(FILL[i % 2])[:, cc - 4 * i], kq[:, cc, 0])
                                last.then_inc(fill_ps, 1)
                            else:
                                pe.wait_ge(fill_out, 2)
                                for k in range(4 * i - 12, 4 * i - 8):
                                    last = mm(FILL[1][:, 0:CTX], hw[:, 3, k, :], hT[:, k, LAT:N],
                                              start=(k == 0), stop=(k == KT - 1))
                                if i == 4:
                                    last.then_inc(fill_ps, 1)
                            for d in range(2):
                                pe.wait_ge(inverse_dve, 2 + 2 * i + d + 1)
                                for cc in range(T):
                                    last = transposes(chunks(PAB[d])[:, cc], U[:, d, cc])
                                last.then_inc(inverse_ps, 1)
                    pe.wait_ge(fill_ps, 5)
                    pe.sem_inc(hw_free[1], 1)
                    pe.wait_ge(ada_sums, 16)
                    pe.wait_ge(fill_out, 3)
                    for i in range(16):
                        last = mm(FILL[0][:, i:i + 1], ada_head[2][:, i, :], ones[:, 0:1],
                                  start=True, stop=True)
                    last.then_inc(ada_ps, 1)
                    pe.wait_ge(states_in, 32)
                    pe.wait_ge(z_out, 3)
                    pe.wait_ge(inverse_dve, 14)
                    pe.wait_ge(ctx_zero, 1)
                    for step, live in SCAN:
                        for n, x, cc in live:
                            if step:
                                pe.wait_ge(state_ready, PREV[n] + 1)
                            mm(XA(x)[:, 0:P], kq[:, cc, 0], chain[:, x, 0], start=True, stop=True)
                            mm(XA(x)[:, P:2 * P], kq[:, cc, 1], chain[:, x, 0], start=True, stop=True
                               ).then_inc(ks_ps, 1)
                        for n, x, cc in live:
                            pe.wait_ge(vprime, n + 1)
                            if step:
                                pe.wait_ge(o_done, PREV[n] + 1)
                            mm(XB(x)[:, 2 * P:3 * P], U[:, x % 2, cc], chain[:, x, 1], start=True, stop=True
                               ).then_inc(vnew_ps, 1)
                        for n, x, cc in live:
                            pe.wait_ge(vnew_sb, 2 * n + 2)
                            mm(XB(x)[:, P:2 * P], ktok[:, cc], chain[:, x, 3], start=True, stop=True)
                            mm(XB(x)[:, 0:P], QK[:, x % 2, cc], chain[:, x, 2], start=True, stop=True
                               ).then_inc(upd_ps, 1)
                    pe.wait_ge(o_done, 4 * CT)
                    head_weights(0)
                    project(0, PAB[1], range(4))
                    pe.wait_ge(o_normed, 1)
                    for cc in range(T):
                        last = transposes(chunks(PAB[0])[:, cc], oo[:, cc])
                    last.then_inc(oT_ps, 1)
                    project(0, PAB[1], range(4, KT))
                    meet(pe, "pe")

                for t in range(2):
                    if t:
                        head_weights(0)
                    head_weights(1)
                    for j in range(4):
                        n = 4 * t + j
                        if n == 0:
                            continue
                        if n == 2:
                            pe.wait_ge(branch_act, 1)
                        if n == 3:
                            pe.wait_ge(branch_dve, 1)
                        if n == 4:
                            pe.wait_ge(branch_dve, 2)
                        if n == 5:
                            pe.wait_ge(branch_act, 2)
                        if n == 6:
                            pe.wait_ge(branch_act, 3)
                        if n == 7:
                            pe.wait_ge(branch_dve, 3)
                        last = project(j, PAB[1 - j % 2])
                        last.then_inc(branch_ps, 1)
                    pe.wait_ge(branch_ps, 4 * t + 3)
                    for part in range(2):
                        pe.sem_inc(hw_free[part], 1)
                pe.wait_ge(branch_act, 4)
                pe.wait_ge(branch_dve, 4)
                for t in range(2):
                    for g, (a, b) in enumerate(GROUPS):
                        n = 3 * t + g
                        if n >= 2:
                            pe.wait_ge(channel_dft_sb, n - 1)
                        dst = ps[:, 2 * BANK * (n % 2):2 * BANK * (n % 2) + 2 * BANK]
                        for cc in range(a, b):
                            last = mm(dst[:, 256 * (cc - a):256 * (cc - a) + 256],
                                      spare[4 + t][:, P * cc:P * cc + P], chdft, start=True, stop=True)
                        last.then_inc(channel_dft_ps, 1)
                for i in range(2):
                    pe.wait_ge(diag_ready, i + 1)
                    if i == 1:
                        pe.wait_ge(g1_ready, 1)
                    for k in range(KT):
                        last = mm(ps[:, 6 * BANK + P * k:6 * BANK + P * k + P], ones, diag[i][:, k], start=True, stop=True)
                    last.then_inc(g1_ps, 1)
                pe.wait_ge(tables_in, 16 * 4)
                pe.wait_ge(channel_dft_sb, 6)
                for t in range(2):
                    Y, (cosb, sinb, rest) = YF(t), ((4, 5, 3), (0, 1, 2))[t]
                    for i, bank in ((1, sinb), (0, cosb)):
                        for m in range(LT):
                            last = mm(ps[:, bank * BANK:(bank + 1) * BANK], Y[:, m, P * i:P * i + P], table(i)[:, m, :],
                                      start=(m == 0), stop=(m == LT - 1))
                        last.then_inc(position_dft_ps, 1)
                    at = rest * BANK
                    for m in range(LT):
                        mm(ps[:, at + CTX:at + CTX + 1], Y[:, m, 0:P], middle_col, start=(m == 0), stop=(m == LT - 1))
                    for i in range(2):
                        for m in range(CT):
                            last = mm(ps[:, at:at + CTX], Y[:, LT + m, P * i:P * i + P], table_ctx(i)[:, m, :],
                                      start=(i == 0 and m == 0), stop=(i == 1 and m == CT - 1))
                    last.then_inc(position_dft_ps, 1)
                meet(pe, "pe")

                yT3 = yT.rearrange("p (k n) -> p k n", k=KT)
                for i in range(T + 2):
                    if i < T:
                        if i >= 2:
                            pe.wait_ge(mix_gated, i - 1)
                        for half in range(2):
                            for k in range(KT):
                                at = (2 * (i % 2) + half) * BANK
                                w = wo_end if (half, k) == (1, KT - 1) else wo[half][:, k, :]
                                last = mm(ps[:, at:at + 512], yT3[:, k, P * i:P * i + P], w,
                                          start=(k == 0), stop=(k == KT - 1))
                        last.then_inc(mix_ps, 1)
                    if 1 <= i <= T:
                        u = i - 1
                        pe.wait_ge(x2_normed, u + 1)
                        if u >= 1:
                            pe.wait_ge(h2_dve, 4 * u)
                            pe.wait_ge(h2_act, 4 * u)
                        for k in range(KT):
                            last = transposes(ps[:, 4 * BANK + P * k:4 * BANK + P * k + P],
                                              xn[u % 2][:, P * k:P * k + P])
                        last.then_inc(x2T_ps, 1)
                    if i >= 2:
                        u = i - 2
                        pe.wait_ge(h2_dve, 4 * u + 4)
                        pe.wait_ge(h2_act, 4 * u + 4)
                        if u >= 1:
                            pe.wait_ge(logits_exp, u)
                        for k in range(KT):
                            last = mm(ps[:, 6 * BANK:6 * BANK + EXPERTS], h2T[u % 2][:, k, :], wr[:, k, :],
                                      start=(k == 0), stop=(k == KT - 1))
                        last.then_inc(logits_ps, 1)
                pe.wait_ge(aff_ready, T)
                for j in range(4):
                    last = transposes(ps[0:LISTS, 7 * BANK + P * j:7 * BANK + P * j + P], affs[:, j])
                last.then_inc(aff_rows_ps, 1)
                pe.wait_ge(lists_ready, 1)
                for i, src in enumerate((tv, tf)):
                    last = transposes(ps[:, LISTS * i:LISTS * i + LISTS], src)
                last.then_inc(lists_ps, 1)
                meet(pe, "pe")

                def gather_T(b):
                    E = epoch[b]
                    pe.wait_ge(E["gathered_lat"], 16)
                    pe.wait_ge(E["gathered_ctx"], 16)
                    for k in range(KT):
                        transposes(ps[:, P * k:P * k + P], xeL[b][:, P * k:P * k + P])
                    for k in range(KT):
                        last = transposes(ps[:, 2 * BANK + CAPC * k:2 * BANK + CAPC * k + CAPC],
                                          xeC[b][:, P * k:P * k + P])
                    last.then_inc(E["xe_ps"], 1)

                def slot(i):
                    return ring[:, 4096 * i:4096 * i + 4096].rearrange("p (k f) -> p k f", k=KT)

                def arrived(i):
                    pe.wait_ge(ring_landed[i], 16)
                    pe.sem_clear(ring_landed[i])

                gather_T(0)
                with pe.Fori(0, EXPERTS // 2) as i:
                    for b in range(2):
                        E = epoch[b]
                        pe.wait_ge(E["xe_sb"], 10)
                        for m in range(KT):
                            half = m // 4
                            if m % 4 == 0:
                                arrived(2 * half)
                                arrived(2 * half + 1)
                            if m >= 2:
                                pe.wait_ge(E["hid_sb"], m - 1)
                            for i in range(2):
                                at = (4 + m % 2) * BANK + CAP * i
                                for k in range(KT):
                                    last = mm(ps[:, at:at + CAP], slot(2 * half + i)[:, k, P * (m % 4):P * (m % 4) + P],
                                              xeT[b][:, k, :], start=(k == 0), stop=(k == KT - 1))
                            last.then_inc(E["gu_ps"], 1)
                            if m == 0:
                                pe.wait_ge(epoch[1 - b]["ye_sb"], 2)
                                pe.wait_ge(epoch[1 - b]["ada_out"], 1)
                                pe.sem_inc(ep_arrive[1 - b], 1)
                            if m % 4 == 3:
                                pe.wait_ge(E["gu_ps"], m + 1)
                                pe.sem_inc(ring_free[2 * half], 1)
                                pe.sem_inc(ring_free[2 * half + 1], 1)
                        pe.wait_ge(ep_go[1 - b]["pe"], 1)
                        pe.sem_clear(ep_go[1 - b]["pe"])
                        gather_T(1 - b)
                        pe.wait_ge(E["hid_sb"], KT)

                        def back(m):
                            pe.wait_ge(E["ye_ch"], 2 * m + 2)
                            if m == 0:
                                pe.wait_ge(epoch[1 - b]["xe_sb"], 10)
                            transposes(ps[:, P * m:P * m + P], yeT[:, m, 0:CAPL])
                            return transposes(ps[0:CAPC, 2 * BANK + P * m:2 * BANK + P * m + P], yeT[:, m, CAPL:CAP])

                        for m in range(KT):
                            half = m // 4
                            if m % 4 == 0:
                                arrived(4 + half)
                            if m >= 2:
                                pe.wait_ge(E["ye_ch"], 2 * (m - 1))
                            at = (6 + m % 2) * BANK
                            for k in range(KT):
                                last = mm(ps[:, at:at + CAP], slot(4 + half)[:, k, P * (m % 4):P * (m % 4) + P],
                                          hid[:, k, :], start=(k == 0), stop=(k == KT - 1))
                            last.then_inc(E["dn_ps"], 1)
                            if m % 4 == 3:
                                pe.wait_ge(E["dn_ps"], m + 1)
                                pe.sem_inc(ring_free[4 + half], 1)
                            if m >= 1:
                                back(m - 1)
                        pe.wait_ge(E["ada_sum"], 2)
                        pe.wait_ge(E["ye_ch"], 2 * KT - 2)
                        for i in range(2):
                            last = mm(ps[:, 6 * BANK + i:6 * BANK + i + 1], ada_moe[2][:, 2 * b + i, :], ones[:, 0:1],
                                      start=True, stop=True)
                        last.then_inc(E["ada_ps"], 1)
                        back(KT - 1).then_inc(E["ye_ps"], 1)
                meet(pe, "pe")

        @block.scalar
        def _(act):
            f = nc.scalar.activation

            act.wait_ge(cond_ps, 1)
            f(condT[:], ps[:, 0:16].rearrange("p (s k) -> p s k", s=2), ACT.Silu).then_inc(cond_ready, 1)
            for j in range(4):
                act.wait_ge(ada0_ps, j + 1)
                f(modrow[:, 512 * j:512 * j + 512], ps[0:2, (1 + j) * BANK:(2 + j) * BANK], ACT.Copy).then_inc(mod_rows_ready, 1)
            meet(act, "act")

            with act.Fori(0, DEPTH) as l:
                for t in range(T + 1):
                    if t < T:
                        act.wait_ge(x_in[t % 2], 16 * (t // 2 + 1))
                        if t >= 1:
                            act.wait_ge(x_squares, t)
                        f(h2T[0].rearrange("p k n -> p (k n)"), xt[t % 2], ACT.Square,
                          accum_out=small[:, t:t + 1]).then_inc(x_squares, 1)
                        act.wait_ge(inv_ms, t + 1)
                        f(small[:, 10 + t:11 + t], small[:, 10 + t:11 + t], ACT.Sqrt).then_inc(inv_rms, 1)
                    if t >= 1:
                        u, s = t - 1, int(t - 1 >= LT)
                        act.wait_ge(xnT_ps, u + 1)
                        for k in range(4):
                            at = (2 + 2 * (u % 2)) * BANK + P * k
                            f(hT[:, k, P * u:P * u + P], ps[:, at:at + P], ACT.Identity, scale=A1[:, k, s:s + 1],
                              bias=mod[:, SH1 + k, s:s + 1]).then_inc(hT_act, 1)
                meet(act, "act")

                f(gs[:, Q_B], gate[:, 0:8], ACT.Exp, scale=-1.0).then_inc(gate_exp, 1)
                f(alog[:, 0, :], alog[:, 0, :], ACT.Exp).then_inc(gate_exp, 1)
                act.wait_ge(gate_abs, 1)
                f(gs[:, Q_GC], gs[:, Q_GC], ACT.Exp, scale=-1.0).then_inc(gate_log, 1)
                act.wait_ge(gate_abs, 2)
                f(gs[:, Q_GL], gs[:, Q_EG], ACT.Ln).then_inc(gate_log, 1)

                def squares(finished):
                    for n, cc in finished:
                        act.wait_ge(o_done, n + 1)
                        f(PP[:, 0, cc], oo[:, cc], ACT.Square, accum_out=small[:, cc:cc + 1]).then_inc(o_sq, 1)

                with act.Fori(0, HEADS) as h:
                    def silu(j):
                        act.wait_ge(conv_done, j + 1)
                        dst = (kq[:, :, 1], kq[:, :, 0], chunks(spare[3]))[j]
                        f(dst, chunks(spare[j]), ACT.Silu).then_inc(silu_done, 1)
                        if j < 2:
                            act.wait_ge(silu_done, j + 1)
                            f(chunks(spare[4 + j]), kq[:, :, 1 - j], ACT.Square).then_inc(qk_squares, 1)

                    for j in range(3):
                        if j == 0:
                            act.wait_ge(hcw_ready, 1)
                        else:
                            silu(j - 1)
                            if j == 2:
                                act.wait_ge(gate_sums, 2)
                                f(hs[:, Q_EG], hs[:, Q_GC], ACT.Exp).then_inc(gate_exps, 1)
                                f(hs[:, Q_END], hs[:, Q_END], ACT.Exp).then_inc(gate_exps, 1)
                                f(hs[:, Q_GL], gate_total, ACT.Exp).then_inc(gate_exps, 1)
                            act.wait_ge(kv_ps, j)
                        f(spare[j], PAB[1 - j % 2], ACT.Copy, scale=hcw[:, 3 + j:4 + j]).then_inc(conv0, 1)
                    silu(2)
                    for i in range(2):
                        act.wait_ge(qk_norms_ps, i + 1)
                        f(spare[6 + i], PAB[i], ACT.Ln, bias=eps_col).then_inc(qk_norms_log, 1)
                    for i in range(2):
                        act.wait_ge(qk_norms_log, i + 1)
                        f(spare[6 + i], spare[6 + i], ACT.Exp, scale=-0.5, bias=(qscale_col if i == 0 else 0.0)
                          ).then_inc(qk_inv_norms, 1)
                    for d in range(2):
                        act.wait_ge(decay_dve, d + 1)
                        f(PP[:, d], PP[:, d], ACT.Exp).then_inc(decay_ready, 1)
                    for d in range(2):
                        act.wait_ge(inverse_ps, 6 + d)
                        f(U[:, d], chunks(PAB[d]), ACT.Copy).then_inc(inverse_act, 1)
                    act.wait_ge(fill_ps, 1)
                    for half in range(2):
                        f(zT[:, 512 * half:512 * half + 512], FILL[half], ACT.Silu).then_inc(z_out, 1)
                    for i in range(6):
                        for d in range(2):
                            act.wait_ge(inverse_ps, 7 + 6 * i + d + 1)
                            f(PP[:, d], chunks(PAB[d]), ACT.Copy).then_inc(inverse_act, 1)
                        if i < 5:
                            for d in range(2):
                                act.wait_ge(inverse_ps, 7 + 6 * i + 4 + d + 1)
                                f(DD[:, d], chunks(PAB[d]), ACT.Copy).then_inc(inverse_act, 1)
                            if i < 3:
                                act.wait_ge(fill_ps, i + 2)
                                n = min(4, T - 4 * i)
                                f(ktok[:, 4 * i:4 * i + n], chunks(FILL[i % 2])[:, 0:n], ACT.Copy).then_inc(fill_out, 1)
                    act.wait_ge(fill_ps, 5)
                    f(zT[:, LAT:N], FILL[1][:, 0:CTX], ACT.Silu).then_inc(z_out, 1)
                    act.wait_ge(gate_exps, 3)
                    complete = []
                    for stp, live in SCAN:
                        for n, x, cc in live:
                            act.wait_ge(vnew_ps, n + 1)
                            if stp:
                                act.wait_ge(upd_ps, PREV[n] + 1)
                            f(chain[:, x, 3], XB(x)[:, 2 * P:3 * P], ACT.Copy, scale=hs[:, Q_END, x % 2, cc:cc + 1]
                              ).then_inc(vnew_sb, 1)
                            f(chain[:, x, 2], XB(x)[:, 2 * P:3 * P], ACT.Copy).then_inc(vnew_sb, 1)
                        squares(complete)
                        complete = [(n, cc) for n, x, cc in live if SEEN[n] is not None]
                    squares(complete)
                    act.wait_ge(o_ms, 1)
                    f(small[:, 20:20 + T], small[:, 10:10 + T], ACT.Sqrt).then_inc(o_rms, 1)
                    meet(act, "act")

                for t in range(2):
                    if t:
                        act.wait_ge(branch_ps, 4 * t)
                        act.wait_ge(branch_dve, 2)
                    f(spare[0], PAB[1], ACT.Copy).then_inc(branch_act, 1)
                    act.wait_ge(branch_dve, 2 * t + 1)
                    f(spare[2], spare[1], ACT.Copy, scale=cols[:, R_SCC + 2 + t:R_SCC + 3 + t]).then_inc(middle_tap, 1)
                    act.wait_ge(branch_ps, 4 * t + 3)
                    f(spare[4 + t], PAB[0], ACT.Copy).then_inc(branch_act, 1)
                for n in range(6):
                    t, (a, b) = n // 3, GROUPS[n % 3]
                    act.wait_ge(channel_dft_ps, n + 1)
                    f(YF(t)[:, a:b], ps[:, 2 * BANK * (n % 2):2 * BANK * (n % 2) + 256 * (b - a)].rearrange(
                        "p (c n) -> p c n", n=256), ACT.Copy).then_inc(channel_dft_sb, 1)
                for i in range(2):
                    act.wait_ge(g1_ps, i + 1)
                    f(g1b[:, i, :], ps[:, 6 * BANK:8 * BANK], ACT.Copy).then_inc(g1_ready, 1)
                for t in range(2):
                    act.wait_ge(position_dft_ps, 3 * t + 1)
                    f(sine_part(t), ps[:, (5, 1)[t] * BANK:(6, 2)[t] * BANK], ACT.Copy).then_inc(sine_ready, 1)
                meet(act, "act")

                for i in range(T + 2):
                    if 1 <= i <= T:
                        u, s = i - 1, int(i - 1 >= LT)
                        act.wait_ge(x2T_ps, u + 1)
                        if u >= 2:
                            act.wait_ge(logits_ps, u - 1)
                        for k in range(4):
                            f(h2T[u % 2][:, k, :], ps[:, 4 * BANK + P * k:4 * BANK + P * k + P], ACT.Identity,
                              scale=A2[:, k, s:s + 1], bias=mod[:, SH2 + k, s:s + 1]).then_inc(h2_act, 1)
                    if i < T:
                        act.wait_ge(mix_added, i + 1)
                        if i >= 1:
                            act.wait_ge(x2_squares, i)
                        f(square, xt[i % 2], ACT.Square, accum_out=small[:, i:i + 1]).then_inc(x2_squares, 1)
                    if i >= 2:
                        u = i - 2
                        act.wait_ge(logits_max, u + 1)
                        f(aff_tile(u), ps[:, 6 * BANK:6 * BANK + EXPERTS], ACT.Exp, bias=small[:, 20 + u:21 + u],
                          accum_out=small[:, 30 + u:31 + u]).then_inc(logits_exp, 1)
                    if i < T:
                        act.wait_ge(x2_inv_ms, i + 1)
                        f(small[:, 10 + i:11 + i], small[:, 10 + i:11 + i], ACT.Sqrt).then_inc(x2_inv_rms, 1)
                meet(act, "act")

                def modulate(b):
                    E = epoch[b]
                    act.wait_ge(E["xe_ps"], 1)
                    for k in range(4):
                        f(xeT[b][:, k, 0:CAPL], ps[:, P * k:P * k + P], ACT.Identity, scale=A2[:, k, 0:1],
                          bias=mod[:, SH2 + k, 0:1]).then_inc(E["xe_sb"], 1)

                modulate(0)
                with act.Fori(0, EXPERTS // 2):
                    for b in range(2):
                        E = epoch[b]
                        for m in range(KT):
                            act.wait_ge(E["gu_ps"], m + 1)
                            if m >= 2:
                                act.wait_ge(E["hid_sb"], m - 1)
                            f(sg[:, m % 2], ps[:, (4 + m % 2) * BANK:(4 + m % 2) * BANK + CAP], ACT.Silu
                              ).then_inc(E["gate_sb"], 1)
                        act.wait_ge(ep_go[1 - b]["act"], 1)
                        act.sem_clear(ep_go[1 - b]["act"])
                        modulate(1 - b)
                        for m in range(KT):
                            act.wait_ge(E["dn_ps"], m + 1)
                            at = (6 + m % 2) * BANK
                            f(yeT[:, m, 0:CAPL], ps[:, at:at + CAPL], ACT.Copy, scale=mod[:, G2 + m, 0:1]
                              ).then_inc(E["ye_ch"], 1)
                            f(yeT[:, m, CAPL:CAP], ps[:, at + CAPL:at + CAP], ACT.Copy, scale=mod[:, G2 + m, 1:2]
                              ).then_inc(E["ye_ch"], 1)
                        act.wait_ge(E["ye_ps"], 1)
                        f(yeC[b], ps[0:CAPC, 2 * BANK:4 * BANK], ACT.Copy, scale=cur[0:CAPC, b, 1:2]
                          ).then_inc(E["ye_sb"], 1)
                        act.drain().then_inc(ep_arrive[b], 1)
                meet(act, "act")

            for t in range(T):
                act.wait_ge(tile_in[t], 16)
                if t >= 1:
                    act.wait_ge(y_squares, t)
                f(area[:, 1024 * T:1024 * T + 1024], xf[t], ACT.Square, accum_out=small[:, t:t + 1]).then_inc(y_squares, 1)
                act.wait_ge(y_inv_ms, t + 1)
                f(small[:, 10 + t:11 + t], small[:, 10 + t:11 + t], ACT.Sqrt).then_inc(y_inv_rms, 1)

        @block.vector
        def _(dve):
            v = nc.vector
            step, gate_step = Steps(dve, dve_step), Steps(dve, gate_dve)

            dve.wait_ge(consts_in, 48)
            v.tensor_copy(identb[:], ident)
            v.tensor_copy(bigb[:].rearrange("p d n -> p (d n)"), big)
            v.memset(tw[:], 0.0)
            v.memset(ix[:], 0)
            dve.wait_ge(pos_in, 64)
            for t in range(LT):
                dve.wait_ge(tile_in[t], 16)
                dve.wait_ge(row_pos_ps, t + 1)
                v.tensor_tensor(x0[t][:, 0:512], x0[t][:, 0:512], ps[:, (5, 7)[t % 2] * BANK:(6, 8)[t % 2] * BANK],
                                ALU.add).then_inc(pos_added, 1)
                v.tensor_tensor(x0[t][:, 512:1024], x0[t][:, 512:1024], area[:, 8192:8704], ALU.add
                                ).then_inc(pos_added, 1)
            dve.wait_ge(vectors_ps, 1)
            v.tensor_copy(allcols[:], ps[:, 5 * BANK:5 * BANK + 2 * P].rearrange("p (l n) -> p l n", l=2)[:, :, 0:ROWS]
                          ).then_inc(vectors_ready, 1)
            dve.wait_ge(mod_cols_ps, 1)
            dve.wait_ge(vectors_ready, 1)
            v.tensor_tensor(mod[:, 0:16, :], ps[:, 6 * BANK:6 * BANK + 32].rearrange("p (m s) -> p m s", s=2),
                            spread(allcols[:, 0, 0:16], 2), ALU.add)
            meet(dve, "dve")

            with dve.Fori(0, DEPTH) as l:
                step.reset()
                step(v.tensor_copy(cols[:], allcols[:, ds(l, 1), :].rearrange("p a n -> p (a n)")))
                step(v.scalar_tensor_tensor(out=A1[:], in0=mod[:, SC1:SC1 + KT, :], scalar=1.0,
                                            in1=spread(cols[:, R_N1:R_N1 + KT], 2), op0=ALU.add, op1=ALU.mult))
                for t in range(T + 1):
                    if t < T:
                        dve.wait_ge(x_squares, t + 1)
                        step(v.tensor_scalar(small[:, 10 + t:11 + t], small[:, t:t + 1], 1.0 / D, EPS, ALU.mult, ALU.add))
                        v.reciprocal(small[:, 10 + t:11 + t], small[:, 10 + t:11 + t]).then_inc(inv_ms, 1)
                        dve.wait_ge(inv_rms, t + 1)
                        if t >= 2:
                            dve.wait_ge(xnT_ps, t - 1)
                        v.tensor_scalar(xn[t % 2], xt[t % 2], small[:, 10 + t:11 + t], None, ALU.mult).then_inc(xn_ready, 1)
                    if t >= 1:
                        u, s = t - 1, int(t - 1 >= LT)
                        dve.wait_ge(xnT_ps, u + 1)
                        for k in range(4, KT):
                            at = (2 + 2 * (u % 2)) * BANK + P * k
                            v.tensor_scalar(hT[:, k, P * u:P * u + P], ps[:, at:at + P], A1[:, k, s:s + 1],
                                            mod[:, SH1 + k, s:s + 1], ALU.mult, ALU.add).then_inc(hT_dve, 1)
                meet(dve, "dve")

                gate_step.reset()
                X = gs[:, Q_G]
                dve.wait_ge(gate_exp, 1)
                gate_step(v.tensor_tensor(X, gate[:, 8:16], spread(alog[:, 1, :], T), ALU.add))
                v.scalar_tensor_tensor(out=gs[:, Q_GC], in0=X, scalar=-1.0, in1=X, op0=ALU.mult, op1=ALU.max
                                       ).then_inc(gate_abs, 1)
                dve.wait_ge(gate_log, 1)
                v.tensor_scalar(gs[:, Q_EG], gs[:, Q_GC], 1.0, None, ALU.add).then_inc(gate_abs, 1)
                dve.wait_ge(gate_abs, 2)
                gate_step(v.tensor_scalar(gs[:, Q_NEG], gs[:, Q_EG], -1.0, None, ALU.add))
                gate_step(v.tensor_tensor(gs[:, Q_NEG], gs[:, Q_GC], gs[:, Q_NEG], ALU.subtract))
                dve.wait_ge(gate_log, 2)
                gate_step(v.tensor_tensor(gs[:, Q_GL], gs[:, Q_GL], gs[:, Q_NEG], ALU.add))
                gate_step(v.scalar_tensor_tensor(out=X, in0=X, scalar=0.0, in1=gs[:, Q_GL], op0=ALU.max, op1=ALU.add))
                dve.wait_ge(gate_exp, 2)
                gate_step(v.scalar_tensor_tensor(out=X, in0=X, scalar=-1.0, in1=spread(alog[:, 0, :], T),
                                                 op0=ALU.mult, op1=ALU.mult))
                gate_step(v.tensor_scalar(gs[:, Q_B], gs[:, Q_B], 1.0, None, ALU.add))
                gate_step(v.reciprocal(gs[:, Q_B], gs[:, Q_B]))
                gate_step(v.tensor_scalar(gs[:, Q_NB], gs[:, Q_B], -1.0, None, ALU.mult))

                with dve.Fori(0, HEADS) as h:
                    step.reset()
                    v.memset(chain[:, 2:4, 0], 0.0).then_inc(ctx_zero, 1)
                    v.tensor_copy(hs[:, 0:3].rearrange("p q d t -> p (q d) t"), gs[:, 0:3].rearrange(
                        "p q (d h) t -> p (q d) (h t)", d=2)[:, :, ds(h * T, T)]).then_inc(hs_ready, 1)
                    v.tensor_copy(hcw[:, 0:9], cols[:, ds(h + R_DNC, 33)][:, 0:33:4]).then_inc(hcw_ready, 1)
                    dve.wait_ge(hcw_ready, 1)
                    for j in range(3):
                        dve.wait_ge(conv0, j + 1)
                        src, dst = PAB[1 - j % 2], spare[j]
                        for lo, hi in SEGS:
                            ins = v.scalar_tensor_tensor(out=dst[:, lo + 1:hi], in0=src[:, lo:hi - 1],
                                                         scalar=hcw[:, j:j + 1], in1=dst[:, lo + 1:hi],
                                                         op0=ALU.mult, op1=ALU.add)
                        step(ins)
                        for lo, hi in SEGS:
                            ins = v.scalar_tensor_tensor(out=dst[:, lo:hi - 1], in0=src[:, lo + 1:hi],
                                                         scalar=hcw[:, 6 + j:7 + j], in1=dst[:, lo:hi - 1],
                                                         op0=ALU.mult, op1=ALU.add)
                        ins.then_inc(conv_done, 1)
                        if j == 1:
                            dve.wait_ge(gate_sum_ps, 1)
                            v.tensor_copy(hs[:, Q_GC], gate_cum).then_inc(gate_sums, 1)
                            dve.wait_ge(gate_sums, 1)
                            v.tensor_tensor(hs[:, Q_END], gate_total, hs[:, Q_GC], ALU.subtract).then_inc(gate_sums, 1)
                    dve.wait_ge(gate_exps, 3)
                    step(v.tensor_tensor(hs[:, Q_NEG], hs[:, Q_EG], hs[:, Q_NB], ALU.mult))
                    dve.wait_ge(vtok_ps, 1)
                    v.tensor_copy(vtok, chunks(PAB[0])).then_inc(vtok_ready, 1)
                    for i in range(2):
                        dve.wait_ge(qk_inv_norms, i + 1)
                        v.tensor_tensor(kq[:, :, 1 - i], kq[:, :, 1 - i], chunks(spare[6 + i]), ALU.mult
                                        ).then_inc(qk_normed, 1)
                    dve.wait_ge(qk_normed, 2)
                    for d in range(2):
                        dve.wait_ge(decay_ps, d + 1)
                        v.tensor_tensor(PP[:, d], chunks(PAB[1 - d]), spread(hs[:, Q_GC, d], P), ALU.subtract
                                        ).then_inc(decay_dve, 1)
                    for g, (a, b) in enumerate(GROUPS):
                        dve.wait_ge(inverse_ps, g + 1)
                        src = PAB[(1, 0, 1)[g]][:, 0:256 * (b - a)].rearrange("p (c j n) -> p c j n", j=2, n=P)
                        for d in range(2):
                            dve.wait_ge(decay_ready, d + 1)
                            for i, dst in enumerate((DD, QK)):
                                v.tensor_tensor(dst[:, d, a:b], src[:, :, i], PP[:, d, a:b], ALU.mult
                                                ).then_inc(decay_dve, 1)
                    for d in range(2):
                        dve.wait_ge(inverse_ps, 4 + d)
                        v.tensor_tensor(LL[:, d], chunks(PAB[d]), spread(hs[:, Q_NB, d], P), ALU.mult
                                        ).then_inc(l_ready, 1)
                        step(v.tensor_copy(DD[:, d], over(ident, T)))
                        dve.wait_ge(l_ready, d + 1)
                        v.copy_predicated(DD[:, d], over((lower, upper)[d][0], T), LL[:, d]).then_inc(inverse_dve, 1)
                    for i in range(6):
                        for d in range(2):
                            dve.wait_ge(inverse_ps, 7 + 6 * i + 2 + d + 1)
                            v.copy_predicated(U[:, d], over((upper, lower)[d][i + 1], T), chunks(PAB[d])
                                              ).then_inc(inverse_dve, 1)
                    dve.wait_ge(inverse_ps, 7 + 6 * 5 + 4)
                    dve.wait_ge(ada_ps, 1)
                    v.tensor_tensor(mod[:, ds(h * 8 + 16, 8), :], FILL[0][:, 0:16].rearrange(
                        "p (m s) -> p m s", s=2), spread(cols[:, ds(h * 8 + 16, 8)], 2), ALU.add)
                    dve.wait_ge(vbeta_ready, 2)
                    dve.wait_ge(ctx_zero, 1)
                    for stp, live in SCAN:
                        for n, x, cc in live:
                            dve.wait_ge(ks_ps, n + 1)
                            v.scalar_tensor_tensor(out=chain[:, x, 1], in0=XA(x)[:, 0:P],
                                                   scalar=hs[:, Q_NEG, x % 2, cc:cc + 1], in1=LL[:, x % 2, cc],
                                                   op0=ALU.mult, op1=ALU.add).then_inc(vprime, 1)
                        for n, x, cc in live:
                            if SEEN[n] is None:
                                v.tensor_scalar(oo[:, cc], XA(x)[:, P:2 * P], hs[:, Q_EG, x % 2, cc:cc + 1], None, ALU.mult
                                                ).then_inc(o_half, 1)
                                continue
                            dve.wait_ge(o_done, SEEN[n] + 1)
                            v.scalar_tensor_tensor(out=oo[:, cc], in0=XA(x)[:, P:2 * P],
                                                   scalar=hs[:, Q_EG, x % 2, cc:cc + 1], in1=oo[:, cc],
                                                   op0=ALU.mult, op1=ALU.add).then_inc(o_half, 1)
                        for n, x, cc in live:
                            dve.wait_ge(upd_ps, n + 1)
                            v.scalar_tensor_tensor(out=chain[:, x, 0], in0=chain[:, x, 0],
                                                   scalar=hs[:, Q_GL, x % 2, cc:cc + 1], in1=XB(x)[:, P:2 * P],
                                                   op0=ALU.mult, op1=ALU.add).then_inc(state_ready, 1)
                            dve.wait_ge(o_half, n + 1)
                            v.tensor_tensor(oo[:, cc], XB(x)[:, 0:P], oo[:, cc], ALU.add).then_inc(o_done, 1)
                    dve.wait_ge(o_done, NSCAN)
                    dve.wait_ge(o_sq, T)
                    step(v.tensor_scalar(small[:, 10:10 + T], small[:, 0:T], 1.0 / P, EPS, ALU.mult, ALU.add))
                    v.reciprocal(small[:, 10:10 + T], small[:, 10:10 + T]).then_inc(o_ms, 1)
                    dve.wait_ge(o_rms, 1)
                    v.tensor_tensor(oo, oo, spread(small[:, 20:20 + T], P), ALU.mult).then_inc(o_normed, 1)
                    dve.wait_ge(oT_ps, 1)
                    dve.wait_ge(z_out, 3)
                    v.scalar_tensor_tensor(out=yT[:, ds(h * N, N)], in0=PAB[0], scalar=cols[:, R_DNN:R_DNN + 1],
                                           in1=zT, op0=ALU.mult, op1=ALU.mult)
                    meet(dve, "dve")

                step.reset()
                v.scalar_tensor_tensor(out=A2[:], in0=mod[:, SC2:SC2 + KT, :], scalar=1.0,
                                       in1=spread(cols[:, R_N2:R_N2 + KT], 2), op0=ALU.add, op1=ALU.mult)
                for i in range(2):
                    v.tensor_tensor(diag[i], over(ident, KT), spread(mod[:, G1:G1 + KT, i], P), ALU.mult
                                    ).then_inc(diag_ready, 1)
                for t in range(2):
                    dve.wait_ge(branch_ps, 4 * t + 1)
                    dve.wait_ge(branch_act, 2 * t + 1)
                    v.tensor_tensor(spare[1], PAB[0], spare[0], ALU.mult).then_inc(branch_dve, 1)
                    dve.wait_ge(branch_dve, 2 * t + 1)
                    dve.wait_ge(middle_tap, t + 1)
                    for tap, (di, si) in ((0, (1, 0)), (4, (0, 1))):
                        for lo, hi in SEGS:
                            ins = v.scalar_tensor_tensor(out=spare[2][:, lo + di:hi - si], in0=spare[1][:, lo + si:hi - di],
                                                         scalar=cols[:, R_SCC + tap + t:R_SCC + tap + t + 1],
                                                         in1=spare[2][:, lo + di:hi - si], op0=ALU.mult, op1=ALU.add)
                        step(ins)
                    dve.wait_ge(branch_ps, 4 * t + 2)
                    v.tensor_tensor(yT[:, (4 + t) * N:(5 + t) * N], PAB[1], spare[2], ALU.mult).then_inc(branch_dve, 1)
                    dve.wait_ge(branch_dve, 2 * t + 2)
                for t in range(2):
                    cosine = ps[:, (4, 0)[t] * BANK:(5, 1)[t] * BANK]
                    out = yT[:, (6 + t) * N:(7 + t) * N]
                    dve.wait_ge(position_dft_ps, 3 * t + 2)
                    dve.wait_ge(sine_ready, t + 1)
                    v.tensor_tensor(out[:, 0:LAT // 2], cosine, sine_part(t), ALU.add)
                    v.tensor_tensor(out[:, LAT // 2 + 1:LAT][:, ::-1], cosine[:, 1:], sine_part(t)[:, 1:], ALU.subtract)
                    dve.wait_ge(position_dft_ps, 3 * t + 3)
                    rest = ps[:, (3, 2)[t] * BANK:(4, 3)[t] * BANK]
                    v.tensor_copy(out[:, LAT // 2:LAT // 2 + 1], rest[:, CTX:CTX + 1])
                    v.tensor_copy(out[:, LAT:N], rest[:, 0:CTX])
                meet(dve, "dve")

                step.reset()
                step(v.memset(affs, -1.0))
                for at, first in ((0, 0), (32, LHALF), (64, LAT)):
                    v.memset(first_token[at:min(at + 32, LISTS)], float(first)).then_inc(first_token_set, 1)
                for i in range(T + 2):
                    b = i % 2
                    if i < T:
                        dve.wait_ge(mix_ps, i + 1)
                        if i >= 2:
                            dve.wait_ge(tile_out[2 + b], 16 * (i // 2))
                            dve.wait_ge(x2T_ps, i - 1)
                        v.tensor_tensor(xn[b], ps[:, 2 * b * BANK:2 * b * BANK + D], g1b[:, int(i >= LT), :], ALU.mult
                                        ).then_inc(mix_gated, 1)
                    if 1 <= i <= T:
                        u, s = i - 1, int(i - 1 >= LT)
                        dve.wait_ge(x2T_ps, u + 1)
                        if u >= 2:
                            dve.wait_ge(logits_ps, u - 1)
                        for k in range(4, KT):
                            v.tensor_scalar(h2T[u % 2][:, k, :], ps[:, 4 * BANK + P * k:4 * BANK + P * k + P],
                                            A2[:, k, s:s + 1], mod[:, SH2 + k, s:s + 1], ALU.mult, ALU.add
                                            ).then_inc(h2_dve, 1)
                    if i >= 2:
                        u = i - 2
                        dve.wait_ge(logits_ps, u + 1)
                        v.tensor_reduce(small[:, 20 + u:21 + u], ps[:, 6 * BANK:6 * BANK + EXPERTS], AX.X, ALU.max,
                                        negate=True).then_inc(logits_max, 1)
                    if i < T:
                        dve.wait_ge(x2_squares, i + 1)
                        step(v.tensor_scalar(small[:, 10 + i:11 + i], small[:, i:i + 1], 1.0 / D, EPS, ALU.mult, ALU.add))
                        v.reciprocal(small[:, 10 + i:11 + i], small[:, 10 + i:11 + i]).then_inc(x2_inv_ms, 1)
                        dve.wait_ge(x2_inv_rms, i + 1)
                        v.tensor_scalar(xn[b], xt[b], small[:, 10 + i:11 + i], None, ALU.mult).then_inc(x2_normed, 1)
                    if i >= 2:
                        u = i - 2
                        dve.wait_ge(logits_exp, u + 1)
                        step(v.reciprocal(small[:, 40 + u:41 + u], small[:, 30 + u:31 + u]))
                        v.tensor_scalar(aff_tile(u), aff_tile(u), small[:, 40 + u:41 + u], None, ALU.mult
                                        ).then_inc(aff_ready, 1)
                dve.wait_ge(aff_rows_ps, 1)
                step(v.tensor_copy(work, ps[0:LISTS, 7 * BANK:7 * BANK + LHALF]))
                for r in range(CAPL // 8):
                    q = slice(8 * r, 8 * r + 8)
                    step(v.max(out=tv[:, q], in_=work))
                    step(v.max_index(out=ti[:, q], in_max=tv[:, q], in_values=work))
                    if r < CAPL // 8 - 1:
                        step(v.match_replace(out=work, in_to_replace=tv[:, q], in_values=work, imm_value=-1.0))
                dve.wait_ge(first_token_set, 3)
                step(v.tensor_copy(tf, ti))
                step(v.tensor_scalar(tf, tf, first_token, None, ALU.add))
                for src in (tv, tf):
                    step(v.tensor_copy(tr[32:48], src[32:48, ::-1]))
                    step(v.tensor_copy(src[32:48], tr[32:48]))
                v.memset(merged, 0.0).then_inc(lists_ready, 1)
                dve.wait_ge(lists_ps, 1)
                step(v.tensor_copy(lists, ps[:, 0:2 * LISTS].rearrange("p (i e) -> p i e", i=2)))
                val, idx = lists[:, 0], lists[:, 1]
                step(v.tensor_tensor(in_first, val[:, 0:EXPERTS], val[:, 32:32 + EXPERTS], ALU.is_ge))
                step(v.tensor_copy(merged, idx[:, 32:32 + EXPERTS]))
                step(v.copy_predicated(merged, in_first.bitcast(I32), idx[:, 0:EXPERTS]))
                for j in (0, EXPERTS):
                    w = EXPERTS if j == 0 else 1
                    v.tensor_tensor(tw[:, 0, j:j + w], val[:, 0:w], val[:, 32:32 + w], ALU.max)
                    v.tensor_copy(ix[:, 0, j:j + w], merged[:, 0:w])
                    v.tensor_copy(tw[0:CAPC, 1, j:j + w], val[0:CAPC, 64:64 + w])
                    v.tensor_copy(ix[0:CAPC, 1, j:j + w], idx[0:CAPC, 64:64 + w])
                meet(dve, "dve")

                def modulate(b):
                    E = epoch[b]
                    dve.wait_ge(E["xe_ps"], 1)
                    for k in range(4, 8):
                        v.tensor_scalar(xeT[b][:, k, 0:CAPL], ps[:, P * k:P * k + P], A2[:, k, 0:1],
                                        mod[:, SH2 + k, 0:1], ALU.mult, ALU.add).then_inc(E["xe_sb"], 1)
                    v.tensor_tensor(xeT[b][:, :, CAPL:CAP], ps[:, 2 * BANK:2 * BANK + CAPC * KT].rearrange(
                        "p (k n) -> p k n", k=KT), spread(A2[:, :, 1], CAPC), ALU.mult).then_inc(E["moe_dve"], 1)
                    dve.wait_ge(E["moe_dve"], 1)
                    v.tensor_tensor(xeT[b][:, :, CAPL:CAP], xeT[b][:, :, CAPL:CAP],
                                    spread(mod[:, SH2:SH2 + KT, 1], CAPC), ALU.add).then_inc(E["xe_sb"], 2)

                modulate(0)
                with dve.Fori(0, EXPERTS // 2) as i:
                    for b in range(2):
                        E = epoch[b]
                        for m in range(KT):
                            dve.wait_ge(E["gate_sb"], m + 1)
                            at = (4 + m % 2) * BANK + CAP
                            v.tensor_tensor(hid[:, m, :], ps[:, at:at + CAP], sg[:, m % 2], ALU.mult
                                            ).then_inc(E["hid_sb"], 1)
                        dve.wait_ge(ep_go[1 - b]["dve"], 1)
                        dve.sem_clear(ep_go[1 - b]["dve"])
                        modulate(1 - b)
                        dve.wait_ge(E["ye_ps"], 1)
                        v.tensor_scalar(yeL[b], ps[:, 0:D], cur[:, b, 0:1], None, ALU.mult).then_inc(E["ye_sb"], 1)
                        dve.wait_ge(E["ada_ps"], 1)
                        v.tensor_tensor(mod[:, ds(i * 2 + b, 1), :].rearrange("p a s -> p (a s)"),
                                        ps[:, 6 * BANK:6 * BANK + 2],
                                        allcols[:, ds(1 - l, 1), ds(i * 2 + b, 1)].rearrange("p a m -> p (a m)")
                                        .to_broadcast([P, 2]), ALU.add).then_inc(E["ada_out"], 1)
                        dve.drain().then_inc(ep_arrive[b], 1)
                meet(dve, "dve")

            step.reset()
            dve.wait_ge(norm_w_in, 16)
            for t in range(T):
                dve.wait_ge(y_squares, t + 1)
                step(v.tensor_scalar(small[:, 10 + t:11 + t], small[:, t:t + 1], 1.0 / D, EPS, ALU.mult, ALU.add))
                v.reciprocal(small[:, 10 + t:11 + t], small[:, 10 + t:11 + t]).then_inc(y_inv_ms, 1)
                dve.wait_ge(y_inv_rms, t + 1)
                v.scalar_tensor_tensor(out=xf[t], in0=xf[t], scalar=small[:, 10 + t:11 + t], in1=g1b[:, 0, :],
                                       op0=ALU.mult, op1=ALU.mult).then_inc(y_ready, 1)

        @block.gpsimd
        def _(pool):
            g = nc.gpsimd
            meet_pool(pool)

            def ada_tile(buf, prod, sums, at, done, done0, chain_sem, n0):
                n = n0

                def then(ins):
                    nonlocal n
                    n += 1
                    ins.then_inc(chain_sem, 1)
                    pool.wait_ge(chain_sem, n)

                for s in range(2):
                    then(g.tensor_tensor(prod, buf, spread(condT[:, s, :], P), ALU.mult))
                    then(g.tensor_tensor(prod[:, 0:4], prod[:, 0:4], prod[:, 4:8], ALU.add))
                    then(g.tensor_tensor(prod[:, 0:2], prod[:, 0:2], prod[:, 2:4], ALU.add))
                    g.tensor_tensor(sums[:, at + s, :], prod[:, 0], prod[:, 1], ALU.add).then_inc(done, 1)
                    pool.wait_ge(done, done0 + s + 1)
                return n
            with pool.Fori(0, DEPTH) as l:
                meet_pool(pool)
                with pool.Fori(0, HEADS):
                    n = 0
                    for i in range(8):
                        pool.wait_ge(ada_in[i % 2], 16 * (i // 2 + 1))
                        n = ada_tile(ada_head[0][i % 2], ada_head[1], ada_head[2], 2 * i, ada_sums, 2 * i, pool_step, n)
                        pool.sem_inc(ada_used, 1)
                    pool.wait_ge(vtok_ready, 1)
                    pool.wait_ge(hs_ready, 1)
                    for d in range(2):
                        pool.wait_ge(inverse_ps, 38 + d)
                        g.tensor_tensor(LL[:, d], vtok, spread(hs[:, Q_B, d], P), ALU.mult).then_inc(vbeta_ready, 1)
                    meet_pool(pool)
                meet_pool(pool)
                for t in range(T):
                    pool.wait_ge(mix_gated, t + 1)
                    pool.wait_ge(x2_in[t % 2], 16 * (t // 2 + 1))
                    g.tensor_tensor(xt[t % 2], xt[t % 2], xn[t % 2], ALU.add).then_inc(mix_added, 1)
                meet_pool(pool)

                def gather(b, e):
                    E = epoch[b]
                    g.tensor_copy(curi[:, b, :], ix[:, :, ds(e, 1)].rearrange("p s a -> p (s a)")).then_inc(pool_step, 1)
                    g.tensor_copy(cur[:, b, :], tw[:, :, ds(e, 1)].rearrange("p s a -> p (s a)")).then_inc(pool_step, 1)
                    pool.wait_ge(pool_step, 2)
                    pool.sem_clear(pool_step)
                    for s, (dst, n) in enumerate(((xeL[b], CAPL), (xeC[b], CAPC))):
                        g.indirect_dma_start(out=dst, out_offset=None, in_=xnorm,
                                             in_offset=bass.IndirectOffsetOnAxis(ap=curi[0:n, b, s:s + 1], axis=0)
                                             ).then_inc(E[("gathered_lat", "gathered_ctx")[s]], 16)

                gather(0, 0)
                pool.sem_inc(epoch[1]["ye_sb"], 2)
                pool.sem_inc(epoch[1]["ada_out"], 1)
                pool.sem_inc(ep_arrive[1], 2)
                for s in ("gathered_lat", "gathered_ctx"):
                    pool.wait_ge(epoch[0][s], 16)
                with pool.Fori(0, EXPERTS // 2) as i:
                    for b in range(2):
                        E, O = epoch[b], epoch[1 - b]
                        pool.wait_ge(ep_arrive[1 - b], 3)
                        pool.sem_clear(ep_arrive[1 - b])
                        pool.dma_reset(nums([O["gathered_lat"], O["gathered_ctx"]]))
                        pool.sem_clear(nums(O.values()))
                        for x in ("pe", "act", "dve"):
                            pool.sem_inc(ep_go[1 - b][x], 1)
                        gather(1 - b, i * 2 + (b + 1))
                        pool.wait_ge(ada_landed, 16)
                        pool.sem_clear(ada_landed)
                        ada_tile(ada_moe[0][0], ada_moe[1], ada_moe[2], 2 * b, E["ada_sum"], 0, pool_step, 0)
                        pool.sem_clear(pool_step)
                        pool.sem_inc(ada_free, 1)
                        pool.wait_ge(E["ye_sb"], 2)
                        for s, (src, n) in enumerate(((yeL[b], CAPL), (yeC[b], CAPC))):
                            g.indirect_dma_start(out=xres, out_offset=bass.IndirectOffsetOnAxis(
                                ap=curi[0:n, b, s:s + 1], axis=0), in_=src, in_offset=None,
                                compute_op=ALU.add).then_inc(scattered[s], 16)
                        for s in scattered + [O["gathered_lat"], O["gathered_ctx"]]:
                            pool.wait_ge(s, 16)
                        pool.dma_reset(nums(scattered))
                        pool.sem_clear(nums(scattered))
                pool.wait_ge(ep_arrive[1], 2)
                pool.sem_clear(ep_arrive[1])
                pool.drain()
                pool.wait_ge(arrive, 4)
                pool.sem_clear(arrive)
                pool.sem_clear(nums(local))
                for E in epoch:
                    pool.dma_reset(nums([E["gathered_lat"], E["gathered_ctx"]]))
                    pool.sem_clear(nums(E.values()))
                for x in go.values():
                    pool.sem_inc(x, 1)


_INS = ["x_prompt", "x_sample", "state_delta", "c", "c_ctx", "w_ada", "b_ada", "norm1_w", "norm2_w", "w_in",
        "dn_conv_w", "dn_a_log", "dn_dt_bias", "dn_norm_w", "sc_conv_w", "w_out", "w_router", "w_gate", "w_up",
        "w_down", "final_norm_w"]
_OUTS = [(1, CTX, D), (1, LAT, D), (1, DEPTH, 2, HEADS, P, P)]


def _constants():
    import numpy as np

    i = np.arange(P)
    row, col = i[:, None], i[None, :]
    parts = [row == col, np.ones((P, P)), row <= col, row >= col]
    low = [(row // (2 * s) == col // (2 * s)) & (row // s % 2 == 1) & (col // s % 2 == 0) for s in LEVELS]
    parts += low + [m.T for m in low]
    parts += [-1e30 * (row > col), -1e30 * (row < col)]
    ang = 2 * np.pi * np.outer(i % 64, i % 64) / 64
    same = row // 64 == col // 64
    parts += [np.cos(ang) * same, np.sin(ang) * same]
    parts += [np.full((P, 1), EPS), np.full((P, 1), -0.5 * np.log(P)), (-1.0) ** row / np.sqrt(LAT * 64)]
    consts = np.concatenate([p.astype(np.float32) for p in parts], axis=1)

    def dft(n):
        ang = 2 * np.pi * (np.outer(np.arange(n), np.arange(n)) % n) / n
        return (np.stack([np.cos(ang), -np.sin(ang)]) / np.sqrt(n * 64)).astype(np.float32)

    quarter = D // 4
    omega = 10000.0 ** (-np.arange(quarter, dtype=np.float64) / quarter)

    def pos(n):
        a = np.arange(n)[:, None] * omega
        return np.concatenate([np.sin(a), np.cos(a)], axis=1).astype(np.float32)

    tok = np.arange(LAT)
    select = (np.arange(LAT // 64)[:, None] == tok[None, :] // 64).astype(np.float32)
    return {"consts": consts, "dft_lat": np.ascontiguousarray(dft(LAT)[:, :, 0:LAT // 2]), "dft_ctx": dft(CTX),
            "pos_row": pos(LAT // 64), "pos_col": pos(64),
            "row_select": select}


def kernel(**inputs):
    import numpy as _np
    import concourse.bacc as _bacc
    from concourse.bass_utils import run_bass_kernel_spmd as _run

    nc = _bacc.Bacc("TRN2", target_bir_lowering=False, num_devices=1)
    arrays, args = {}, []
    given = {name: _np.ascontiguousarray(inputs[name]) for name in _INS}
    given.update(_constants())
    for name, a in given.items():
        arrays[f"in_{name}_dram"] = a
        args.append(nc.dram_tensor(f"in_{name}_dram", a.shape, mybir.dt.from_np(a.dtype), kind="ExternalInput").ap())
    for i, shape in enumerate(_OUTS):
        args.append(nc.dram_tensor(f"out_{i}_dram", shape, F32, kind="ExternalOutput").ap())
    trunk(nc, *args)
    r = _run(nc, [arrays], core_ids=[0])
    return tuple(r.results[0][f"out_{i}_dram"] for i in range(len(_OUTS)))
```
